# Optimizing a Trainium2 kernel written in Bass

```python
import math
import jax, jax.numpy as jnp
from jax import lax
import numpy as np

D_MODEL = 1024
BATCH = 1
SEQ = 512
DEPTH = 1

MEM_LEN = 256
EPS = 1e-6
M_HEADS = 4
M_INNER = 2 * D_MODEL
M_HD = M_INNER // M_HEADS
M_CONV = 4
M_CHUNK = 128
A_HEADS = 8
A_QK = D_MODEL // 16
A_V = 2 * A_QK
A_WIDTH = A_HEADS * A_V
Q_BLOCK = 128
X_HEADS = 4
X_HD = D_MODEL // X_HEADS
X_WIDTH = X_HEADS * X_HD
REL_BUCKETS = 32
REL_MAX_DIST = 128
D_FF = 2816
N_BRANCH = 3
IN_SIZES = [M_INNER, M_INNER, M_HEADS, M_HEADS,
            A_HEADS * 2 * A_QK, A_HEADS * 2 * A_QK, A_WIDTH,
            X_WIDTH, N_BRANCH * D_MODEL]
IN_WIDTH = sum(IN_SIZES)
IN_SPLITS = [int(s) for s in np.cumsum(IN_SIZES)[:-1]]

kernel_name = 'hybrid_mlstm_diffattn_xattn_block'

def rmsnorm(x, g):
    xf = x.astype(jnp.float32)
    y = xf * lax.rsqrt(jnp.mean(xf * xf, axis=-1, keepdims=True) + EPS)
    return (y * g.astype(jnp.float32)).astype(x.dtype)

def head_rmsnorm(h, g):
    B, H, S, d = h.shape
    hf = h.astype(jnp.float32)
    hn = hf * lax.rsqrt(jnp.mean(hf * hf, axis=-1, keepdims=True) + EPS)
    hn = jnp.transpose(hn, (0, 2, 1, 3)).reshape(B, S, H * d)
    return hn * g.astype(jnp.float32)

def swiglu(h, w_gu, w_down):
    gate, up = jnp.split(h @ w_gu, 2, axis=-1)
    return (jax.nn.silu(gate) * up) @ w_down

def causal_conv(x, w, b):
    C = x.shape[-1]
    y = lax.conv_general_dilated(x, w[:, None, :].astype(x.dtype), window_strides=(1,),
                                 padding=[(M_CONV - 1, 0)],
                                 dimension_numbers=('NWC', 'WIO', 'NWC'),
                                 feature_group_count=C)
    return y + b

def headwise(x, w):
    B, S, _ = x.shape
    H, d, _ = w.shape
    return jnp.einsum('bshd,hde->bhse', x.reshape(B, S, H, d), w)

def mlstm_chunkwise(q, k, v, ig, lf):
    B, H, S, d = q.shape
    L = M_CHUNK
    NC = S // L

    def chunks(a):
        return jnp.moveaxis(a.reshape((B, H, NC, L) + a.shape[3:]), 2, 0)

    causal = jnp.tril(jnp.ones((L, L), dtype=bool))

    def step(carry, inp):
        C, n, m = carry
        qb, kb, vb, ib, fb = inp
        b = jnp.cumsum(fb, axis=-1)
        dlog = b[..., :, None] - b[..., None, :] + ib[..., None, :]
        dlog = jnp.where(causal, dlog, -jnp.inf)
        inter = b + m[..., None]
        m_t = jnp.maximum(inter, jnp.max(dlog, axis=-1))
        w_intra = jnp.exp(dlog - m_t[..., None])
        w_inter = jnp.exp(inter - m_t)
        s = jnp.einsum('bhtd,bhsd->bhts', qb, kb) * w_intra
        num = jnp.einsum('bhts,bhse->bhte', s, vb) + w_inter[..., None] * jnp.einsum('bhtd,bhde->bhte', qb, C)
        den = jnp.sum(s, axis=-1) + w_inter * jnp.einsum('bhtd,bhd->bht', qb, n)
        h = num / jnp.maximum(jnp.abs(den), jnp.exp(-m_t))[..., None]
        bL = b[..., -1]
        tail = bL[..., None] - b + ib
        m_new = jnp.maximum(bL + m, jnp.max(tail, axis=-1))
        w_s = jnp.exp(tail - m_new[..., None])
        decay = jnp.exp(bL + m - m_new)
        C_new = decay[..., None, None] * C + jnp.einsum('bhs,bhsd,bhse->bhde', w_s, kb, vb)
        n_new = decay[..., None] * n + jnp.einsum('bhs,bhsd->bhd', w_s, kb)
        return (C_new, n_new, m_new), h

    init = (jnp.zeros((B, H, d, d), jnp.float32), jnp.zeros((B, H, d), jnp.float32),
            jnp.zeros((B, H), jnp.float32))
    _, hc = lax.scan(step, init, (chunks(q), chunks(k), chunks(v), chunks(ig), chunks(lf)))
    return jnp.moveaxis(hc, 0, 2).reshape(B, H, S, v.shape[-1])

def t5_bucket(rel):
    n = jnp.maximum(-rel, 0)
    max_exact = REL_BUCKETS // 2
    nf = jnp.maximum(n, 1).astype(jnp.float32)
    large = max_exact + (jnp.log(nf / max_exact) / math.log(REL_MAX_DIST / max_exact)
                         * (REL_BUCKETS - max_exact)).astype(jnp.int32)
    large = jnp.minimum(large, REL_BUCKETS - 1)
    return jnp.where(n < max_exact, n, large)

def diff_attention(q1, q2, k1, k2, v, positions, rel_bias, lam):
    B, H, S, dq = q1.shape
    NB = S // Q_BLOCK
    scale = dq ** -0.5

    def to_blocks(a):
        return jnp.moveaxis(a.reshape(B, H, NB, Q_BLOCK, a.shape[-1]), 2, 0)

    def block(inp):
        q1b, q2b, pq = inp
        rel = positions[None, :] - pq[:, None]
        bias = jnp.transpose(rel_bias[t5_bucket(rel)], (2, 0, 1))[None].astype(jnp.float32)
        visible = rel <= 0

        def probs(qb, kk):
            s = jnp.einsum('bhqd,bhkd->bhqk', qb, kk).astype(jnp.float32) * scale + bias
            return jax.nn.softmax(jnp.where(visible, s, -jnp.inf), axis=-1)

        a = probs(q1b, k1) - lam * probs(q2b, k2)
        return jnp.einsum('bhqk,bhkd->bhqd', a.astype(v.dtype), v)

    out = lax.map(block, (to_blocks(q1), to_blocks(q2), positions.reshape(NB, Q_BLOCK)))
    return jnp.moveaxis(out, 0, 2).reshape(B, H, S, v.shape[-1])

def cross_attention(qx, mem_n, w_mem_kv):
    B, S, _ = qx.shape
    kx, vx = jnp.split(mem_n @ w_mem_kv, 2, axis=-1)
    q = qx.reshape(B, S, X_HEADS, X_HD)
    k = kx.reshape(B, MEM_LEN, X_HEADS, X_HD)
    v = vx.reshape(B, MEM_LEN, X_HEADS, X_HD)
    s = jnp.einsum('bshd,bmhd->bhsm', q, k).astype(jnp.float32) * X_HD ** -0.5
    p = jax.nn.softmax(s, axis=-1).astype(v.dtype)
    return jnp.einsum('bhsm,bmhd->bshd', p, v).reshape(B, S, X_WIDTH)

def setup_inputs(seed: int = 0) -> dict:
    key = jax.random.key(seed)
    ks = iter(jax.random.split(key, 40))

    def nrm(shape, scale):
        return jax.random.normal(next(ks), shape, jnp.float32) * scale

    def gain(shape):
        return 1.0 + nrm(shape, 0.02)

    L, D = DEPTH, D_MODEL
    f_bias = jnp.broadcast_to(jnp.linspace(3.0, 6.0, M_HEADS, dtype=jnp.float32), (L, M_HEADS))
    b_if = jnp.concatenate([nrm((L, M_HEADS), 0.1), f_bias + nrm((L, M_HEADS), 0.1)], axis=-1)
    offset = jax.random.randint(next(ks), (), 0, 1024, dtype=jnp.int32)
    return {
        'x': nrm((BATCH, SEQ, D), 1.0),
        'mem': nrm((BATCH, MEM_LEN, D), 1.0),
        'positions': offset + jnp.arange(SEQ, dtype=jnp.int32),
        'rel_bias': nrm((REL_BUCKETS, A_HEADS), 0.5),
        'ffn1_norm': gain((L, D)),
        'ffn1_w_gu': nrm((L, D, 2 * D_FF), D ** -0.5),
        'ffn1_w_down': nrm((L, D_FF, D), D_FF ** -0.5),
        'mix_norm': gain((L, D)),
        'mem_norm': gain((L, D)),
        'w_in': nrm((L, D, IN_WIDTH), D ** -0.5),
        'b_if': b_if,
        'b_gate': nrm((L, N_BRANCH * D), 0.01),
        'm_conv_w': nrm((L, M_CONV, M_INNER), 0.5),
        'm_conv_b': nrm((L, M_INNER), 0.01),
        'm_wq': nrm((L, M_HEADS, M_HD, M_HD), M_HD ** -0.5),
        'm_wk': nrm((L, M_HEADS, M_HD, M_HD), M_HD ** -0.5),
        'm_wv': nrm((L, M_HEADS, M_HD, M_HD), M_HD ** -0.5),
        'm_head_norm': gain((L, M_INNER)),
        'a_lam_q1': nrm((L, A_QK), 0.1),
        'a_lam_k1': nrm((L, A_QK), 0.1),
        'a_lam_q2': nrm((L, A_QK), 0.1),
        'a_lam_k2': nrm((L, A_QK), 0.1),
        'a_head_norm': gain((L, A_WIDTH)),
        'w_mem_kv': nrm((L, D, 2 * X_WIDTH), D ** -0.5),
        'w_branch_m': nrm((L, M_INNER, D), M_INNER ** -0.5),
        'w_branch_a': nrm((L, A_WIDTH, D), A_WIDTH ** -0.5),
        'w_branch_x': nrm((L, X_WIDTH, D), X_WIDTH ** -0.5),
        'w_out': nrm((L, D, D), D ** -0.5),
        'ffn2_norm': gain((L, D)),
        'ffn2_w_gu': nrm((L, D, 2 * D_FF), D ** -0.5),
        'ffn2_w_down': nrm((L, D_FF, D), D_FF ** -0.5),
        'final_norm': gain((D,)),
    }

def reference(x, mem, positions, rel_bias, ffn1_norm, ffn1_w_gu, ffn1_w_down, mix_norm, mem_norm,
              w_in, b_if, b_gate, m_conv_w, m_conv_b, m_wq, m_wk, m_wv, m_head_norm,
              a_lam_q1, a_lam_k1, a_lam_q2, a_lam_k2, a_head_norm, w_mem_kv,
              w_branch_m, w_branch_a, w_branch_x, w_out, ffn2_norm, ffn2_w_gu, ffn2_w_down,
              final_norm):
    B, S, D = x.shape
    for l in range(DEPTH):
        x = x + 0.5 * swiglu(rmsnorm(x, ffn1_norm[l]), ffn1_w_gu[l], ffn1_w_down[l])

        h = rmsnorm(x, mix_norm[l])
        (xm, o_pre, i_pre, f_pre, qa, ka, va, qx, g_pre) = jnp.split(h @ w_in[l], IN_SPLITS, axis=-1)

        xc = jax.nn.silu(causal_conv(xm, m_conv_w[l], m_conv_b[l]))
        q_m = headwise(xc, m_wq[l]).astype(jnp.float32)
        k_m = headwise(xc, m_wk[l]).astype(jnp.float32) * M_HD ** -0.5
        v_m = headwise(xm, m_wv[l]).astype(jnp.float32)
        gates_if = (jnp.concatenate([i_pre, f_pre], axis=-1) + b_if[l]).astype(jnp.float32)
        ig = jnp.transpose(gates_if[..., :M_HEADS], (0, 2, 1))
        lf = jnp.transpose(jax.nn.log_sigmoid(gates_if[..., M_HEADS:]), (0, 2, 1))
        h_m = mlstm_chunkwise(q_m, k_m, v_m, ig, lf)
        y_m = (jax.nn.sigmoid(o_pre.astype(jnp.float32)) * head_rmsnorm(h_m, m_head_norm[l])).astype(x.dtype)

        qa = jnp.transpose(qa.reshape(B, S, A_HEADS, 2, A_QK), (3, 0, 2, 1, 4))
        ka = jnp.transpose(ka.reshape(B, S, A_HEADS, 2, A_QK), (3, 0, 2, 1, 4))
        va = jnp.transpose(va.reshape(B, S, A_HEADS, A_V), (0, 2, 1, 3))
        lam_init = 0.8 - 0.6 * math.exp(-0.3 * l)
        lam = (jnp.exp(jnp.sum(a_lam_q1[l] * a_lam_k1[l]).astype(jnp.float32))
               - jnp.exp(jnp.sum(a_lam_q2[l] * a_lam_k2[l]).astype(jnp.float32)) + lam_init)
        h_a = diff_attention(qa[0], qa[1], ka[0], ka[1], va, positions, rel_bias, lam)
        y_a = (head_rmsnorm(h_a, a_head_norm[l]) * (1.0 - lam_init)).astype(x.dtype)

        y_x = cross_attention(qx, rmsnorm(mem, mem_norm[l]), w_mem_kv[l])

        g = jax.nn.sigmoid(g_pre + b_gate[l]).reshape(B, S, N_BRANCH, D)
        merged = (g[:, :, 0] * (y_m @ w_branch_m[l]) + g[:, :, 1] * (y_a @ w_branch_a[l])
                  + g[:, :, 2] * (y_x @ w_branch_x[l]))
        x = x + merged @ w_out[l]

        x = x + 0.5 * swiglu(rmsnorm(x, ffn2_norm[l]), ffn2_w_gu[l], ffn2_w_down[l])
    return rmsnorm(x, final_norm)


_drawn_inputs = setup_inputs


def setup_inputs(seed=0):
    import zlib

    import numpy as np

    out = dict(_drawn_inputs(seed))
    spreads = {}
    factors = {'ffn1_norm': 5.223,
     'mix_norm': 2.912,
     'mem_norm': 36.82,
     'b_gate': 31.372,
     'm_conv_b': 6.485,
     'm_head_norm': 200.0,
     'a_lam_q1': 6.063,
     'a_lam_k1': 8.0,
     'a_lam_q2': 4.801,
     'a_lam_k2': 8.0,
     'a_head_norm': 190.901,
     'ffn2_norm': 31.582,
     'final_norm': 20.623}
    for name, (base, spread) in spreads.items():
        noise = np.random.default_rng([zlib.crc32(name.encode()), seed]).standard_normal(out[name].shape)
        drawn = base * np.exp(spread * noise) if base else spread * noise
        out[name] = __import__('jax').numpy.asarray(drawn.astype(out[name].dtype))
    for name, factor in factors.items():
        out[name] = (out[name] * factor).astype(out[name].dtype)
    return out
```

```python
from contextlib import ExitStack

import numpy as np

import concourse.bass as bass
from concourse import mybir

F32 = mybir.dt.float32
F32R = mybir.dt.float32r
BF16 = mybir.dt.bfloat16
I32 = mybir.dt.int32
ALU = mybir.AluOpType
ACT = mybir.ActivationFunctionType
AX = mybir.AxisListType

P = 128
S = 512
D = 1024
KD = D // P
NT = S // P
F = 2816
KF = F // P
COLS = 256
EPS = 1e-6
KB = 1024
MEM = 256
MT = MEM // P
M_HEADS = 4
M_HD = 2 * D // M_HEADS
MK = M_HD // P
CHUNKS = S // P
A_HEADS = 8
A_QK = 64
X_HEADS = 4
X_HD = D // X_HEADS
BUCKETS = 32
LAM_INIT = 0.2
A_SCALE = A_QK ** -0.5
X_SCALE = X_HD ** -0.5
HIDE = -1e30
KEYS4 = S // 4
QSTEP = 16
C_XM, C_O, C_IF = 0, 2 * D, 4 * D
C_QA = C_IF + 2 * M_HEADS
C_KA, C_VA, C_QX, C_G = C_QA + D, C_QA + 2 * D, C_QA + 3 * D, C_QA + 4 * D
WIDE = 512
HEAD_BLOCKS = 9


class Progress:

    def __init__(self):
        self.block = 0
        self.reader = [None] * 8


def build(nc, t, stages):
    ctx = ExitStack()
    with ctx:
        def sem(name):
            return ctx.enter_context(nc.semaphore(name))

        base = -(-nc.sbuf_base // 64) * 64

        def at(name, kb, shape, dtype=F32):
            return nc.alloc_sbuf_tensor_at(name, shape, dtype, offset=base + int(kb * KB))

        xT = at("xT", 0, [P, KD, S])
        w_raw = [at(f"w_raw{i}", 16 + 8 * i, [P, 2048]) for i in range(2)]
        w_hi = [at(f"w_hi{i}", 32 + 8 * i, [P, 2048], F32R) for i in range(2)]
        w_lo = [at(f"w_lo{i}", 48 + 8 * i, [P, 2048], F32R) for i in range(2)]
        h_hi = at("h_hi", 64, [P, KD, S], F32R)
        h_lo = at("h_lo", 80, [P, KD, S], F32R)
        merged = at("merged", 96, [P, KD, S])
        ident = at("ident", 112, [P, P])
        ones = at("ones", 112.5, [P, P])
        par = at("par", 113, [P, 176])
        eps_c = at("eps_c", 114, [P, 1])
        smalls = at("smalls", 114.0625, [P, 40])
        mask = at("mask", 114.25, [P, P])
        Z = 115
        sq = at("sq", Z, [P, KD, S])
        act_hi = at("act_hi", Z, [P, KF, S], F32R)
        act_lo = at("act_lo", Z + 44, [P, KF, S], F32R)
        gate_s = at("gate_s", 96, [P, 2, S])
        act_f = at("act_f", 100, [P, 2, S])
        rinv = at("rinv", 104, [P, S])
        lnv = at("lnv", 106, [P, S])
        x_tok = at("x_tok", Z + 32, [P, NT, D])
        prm1 = at("prm1", Z + 48, [104, P])
        prm2 = at("prm2", Z + 49, [64, P])
        rb_cur = at("rb_cur", Z, [P, A_HEADS])
        rb_prev = at("rb_prev", Z + 0.0625, [P, A_HEADS])
        rb_base = at("rb_base", Z + 0.125, [P, 1])
        thr = at("thr", Z + 0.1875, [P, 1])
        step_f = at("step_f", Z + 0.25, [P, 32])
        step_b = [at(f"step_b{i}", Z + 0.5 + 0.125 * i, [P, 32], BF16) for i in range(3)]
        sign_row = at("sign_row", Z + 1, [1, P])
        pos_i = at("pos_i", Z + 2, [1, S], I32)
        pos_h = at("pos_h", Z + 4, [1, S], I32)
        pos_l = at("pos_l", Z + 6, [1, S], I32)
        pos_hf = at("pos_hf", Z + 8, [1, S])
        pos_lf = at("pos_lf", Z + 10, [1, S])
        pos_r = at("pos_r", Z + 12, [1, S])
        pk_s = at("pk_s", Z + 14, [P, KEYS4])
        pq_s = at("pq_s", Z + 16, [P, S])
        past = [at(f"past{i}", Z + 18 + 4 * i, [P, QSTEP, KEYS4], BF16) for i in range(2)]
        bias_out = [at(f"bias_out{i}", Z + 26 + 2 * i, [P, S]) for i in range(2)]
        g_i = at("g_i", Z, [M_HEADS, S])
        g_f = at("g_f", Z + 2, [M_HEADS, S])
        g_abs = at("g_abs", Z + 4, [M_HEADS, S])
        g_ln = at("g_ln", Z + 6, [M_HEADS, S])
        g_lf = at("g_lf", Z + 8, [M_HEADS, S])
        g_b = at("g_b", Z + 10, [M_HEADS, S])
        g_m = at("g_m", Z + 12, [M_HEADS, S])
        g_rows = at("g_rows", Z + 14, [M_HEADS, 4, S])
        one_row = at("one_row", Z + 22, [M_HEADS, S])
        g_neg = at("g_neg", Z + 87.5, [M_HEADS, S])
        tokp = at("tokp", Z + 89.5, [P, 4, CHUNKS, M_HEADS])
        m_small = at("m_small", Z + 89.75, [P, 64])
        sel = at("sel", Z + 90.25, [M_HEADS, M_HEADS, P])
        decay = m_small[:, 0:8]
        dec_row = at("dec_row", Z + 92.25, [M_HEADS, 2])
        dec_diag = at("dec_diag", Z + 92.3125, [M_HEADS, 2, M_HEADS])
        xm_f = at("xm_f", Z, [P, MK, S + 4])
        xm_hi = at("xm_hi", Z + 8.5, [P, MK, S], F32R)
        xm_lo = at("xm_lo", Z + 16.5, [P, MK, S], F32R)
        xc_hi = at("xc_hi", Z + 24.5, [P, MK, S], F32R)
        xc_lo = at("xc_lo", Z + 32.5, [P, MK, S], F32R)
        q_f = at("q_f", Z + 40.5, [P, MK, S])
        k_f = at("k_f", Z + 48.5, [P, MK, S])
        v_f = at("v_f", Z + 56.5, [P, CHUNKS, M_HD])
        conv = at("conv", Z + 64.5, [P, MK, S])
        k_ws = at("k_ws", Z + 64.5, [P, M_HD])
        c_st = at("c_st", Z + 72.5, [P, MK, M_HD])
        w_in_tr = at("w_in_tr", Z + 80.5, [P, CHUNKS, P])
        s_w = at("s_w", Z + 82.5, [P, P])
        y_f = [at(f"y_f{i}", Z + 83.5 + 2 * i, [P, S]) for i in range(2)]
        h_m = at("h_m", Z, [P, CHUNKS, M_HD])
        o_sig = at("o_sig", Z + 24.5, [P, MK, S])
        ym_hi = at("ym_hi", Z + 8.5, [P, MK, S], F32R)
        ym_lo = at("ym_lo", Z + 16.5, [P, MK, S], F32R)
        n_st = m_small[:, 8:12]
        sumsq = m_small[:, 12:16]
        den = m_small[:, 16:24]
        va = at("va", Z, [P, NT, D])
        q_a = at("q_a", Z + 16, [P, 2, S])
        k_a = at("k_a", Z + 20, [P, 2, S])
        o_a = at("o_a", Z + 24, [P, S])
        o_sq = at("o_sq", Z + 26, [P, S])
        o_ln = at("o_ln", Z + 28, [P, S])
        y_af = at("y_af", Z + 30, [P, S])
        ya_hi = at("ya_hi", Z + 32, [P, KD, S], F32R)
        ya_lo = at("ya_lo", Z + 48, [P, KD, S], F32R)
        bias_sb = [at(f"bias_sb{i}", Z + 64 + 2 * i, [P, S]) for i in range(4)]
        probs = [at(f"probs{i}", Z + 72 + 4 * i, [P, 2, S]) for i in range(2)]
        a_mix = [at(f"a_mix{i}", Z + 80 + 2 * i, [P, S]) for i in range(2)]
        a_tr = at("a_tr", Z + 84, [P, NT, S])
        g_sig = at("g_sig", Z + 84, [P, 2, S])
        g_tmp = at("g_tmp", Z + 88, [P, 2, S])
        memn_hi = at("memn_hi", Z, [P, KD, MEM], F32R)
        memn_lo = at("memn_lo", Z + 8, [P, KD, MEM], F32R)
        k_x = at("k_x", Z + 16, [P, KD, MEM])
        v_x = at("v_x", Z + 24, [P, MT, D])
        q_x = at("q_x", Z + 32, [P, KD, S])
        mem_tok = at("mem_tok", Z + 32, [P, MT, D])
        memn_f = at("memn_f", Z + 40, [P, KD, MEM])
        mem_sq = at("mem_sq", Z + 48, [P, MT, D])
        yx_hi = at("yx_hi", Z + 48, [P, KD, S], F32R)
        yx_lo = at("yx_lo", Z + 64, [P, KD, S], F32R)
        p_tr = at("p_tr", Z + 80, [P, MT, S])
        p_x = [at(f"p_x{i}", Z + 88 + i, [P, MEM]) for i in range(2)]
        mg_hi = at("mg_hi", Z, [P, KD, S], F32R)
        mg_lo = at("mg_lo", Z + 16, [P, KD, S], F32R)
        bias_dram = nc.dram_tensor("bias_dram", [A_HEADS * 4, S, KEYS4], F32, kind="Internal").ap()
        o_tok = at("o_tok", Z + 32, [P, NT, D])

        pair = [ctx.enter_context(nc.psum_tensor(f"pair{i}", [P, 2, S], F32)) for i in range(4)]

        PC = {}
        col = 0
        for name, n in (("ffn1_norm", 8), ("mix_norm", 8), ("mem_norm", 8), ("ffn2_norm", 8),
                        ("final_norm", 8), ("m_head_norm", 16), ("a_head_norm", 8), ("m_conv_b", 16),
                        ("b_gate", 24), ("m_conv_w", 64)):
            PC[name] = (col, n)
            col += n

        def pcol(name, k):
            return par[:, PC[name][0] + k:PC[name][0] + k + 1]

        raw_loaded = [sem(f"raw_loaded{i}") for i in range(2)]
        hi_made = sem("hi_made")
        lo_made = sem("lo_made")
        block_done = sem("block_done")
        consts_made = sem("consts_made")
        prm_loaded = sem("prm_loaded")
        x_loaded = sem("x_loaded")
        par_turned = sem("par_turned")
        par_made = sem("par_made")
        xt_turned = sem("xt_turned")
        xt_made = sem("xt_made")
        out_turned = sem("out_turned")
        out_lo_made = sem("out_lo_made")
        out_hi_made = sem("out_hi_made")
        out_stored = sem("out_stored")

        chain_d = sem("chain_d")
        chain_a = sem("chain_a")
        thr_loaded = sem("thr_loaded")
        pos_loaded = sem("pos_loaded")
        pos_made = sem("pos_made")
        pos_spread = sem("pos_spread")
        past_made = sem("past_made")
        bias_summed = sem("bias_summed")
        bias_made = sem("bias_made")
        bias_stored = [sem(f"bias_stored{i}") for i in range(2)]
        bif_loaded = sem("bif_loaded")
        g_pre = sem("g_pre")
        g_exp = sem("g_exp")
        g_arg = sem("g_arg")
        g_w = sem("g_w")
        g_diag = sem("g_diag")
        g_turned = sem("g_turned")
        g_ready = sem("g_ready")
        xm_made = sem("xm_made")
        xmh_made = sem("xmh_made")
        xml_made = sem("xml_made")
        conv_made = sem("conv_made")
        xc_made = sem("xc_made")
        xcl_made = sem("xcl_made")
        q_made = sem("q_made")
        k_made = sem("k_made")
        v_made = sem("v_made")
        o_made = sem("o_made")
        negm_spread = sem("negm_spread")
        w_arg = sem("w_arg")
        w_made = sem("w_made")
        sc_ready = sem("sc_ready")
        kt_ready = sem("kt_ready")
        sw_made = sem("sw_made")
        kws_made = sem("kws_made")
        num_ready = sem("num_ready")
        upd_ready = sem("upd_ready")
        c_made = sem("c_made")
        r_made = sem("r_made")
        h_part = sem("h_part")
        h_made = sem("h_made")
        hn_made = sem("hn_made")
        h_turned = sem("h_turned")
        yf_made = sem("yf_made")
        ymh_made = sem("ymh_made")
        yml_made = sem("yml_made")
        bm_added = sem("bm_added")
        g_sig_made = sem("g_sig_made")
        mg_made = sem("mg_made")
        lam_loaded = sem("lam_loaded")
        lam_summed = sem("lam_summed")
        va_made = sem("va_made")
        qa_made = sem("qa_made")
        ka_made = sem("ka_made")
        bias_loaded = [sem(f"bias_loaded{i}") for i in range(4)]
        a_scored = sem("a_scored")
        a_shifted = sem("a_shifted")
        a_exp = sem("a_exp")
        a_mixed = sem("a_mixed")
        a_turned = sem("a_turned")
        a_tr_made = sem("a_tr_made")
        a_out = sem("a_out")
        a_sq = sem("a_sq")
        a_sum = sem("a_sum")
        a_r = sem("a_r")
        a_y = sem("a_y")
        a_yh = sem("a_yh")
        a_yl = sem("a_yl")
        mem_loaded = sem("mem_loaded")
        mem_sq_made = sem("mem_sq_made")
        mem_r = sem("mem_r")
        mem_turned = sem("mem_turned")
        memn_made = sem("memn_made")
        memh_made = sem("memh_made")
        meml_made = sem("meml_made")
        kx_made = sem("kx_made")
        vx_made = sem("vx_made")
        qx_made = sem("qx_made")
        x_scored = sem("x_scored")
        x_max = sem("x_max")
        x_exp = sem("x_exp")
        x_norm = sem("x_norm")
        x_turned = sem("x_turned")
        x_tr_made = sem("x_tr_made")
        x_out = sem("x_out")
        x_yh = sem("x_yh")
        x_yl = sem("x_yl")
        mgh_made = sem("mgh_made")
        mgl_made = sem("mgl_made")
        x_mixed = sem("x_mixed")

        class NormSems:
            def __init__(self, name):
                self.sq_made = sem(f"{name}_sq_made")
                self.sum_ready = sem(f"{name}_sum_ready")
                self.ln_made = sem(f"{name}_ln_made")
                self.r_made = sem(f"{name}_r_made")
                self.raw_made = sem(f"{name}_raw_made")
                self.hi_made = sem(f"{name}_hi_made")
                self.ready = sem(f"{name}_ready")

        class FfnSems:
            def __init__(self, name):
                self.gate_made = sem(f"{name}_gate_made")
                self.act_made = sem(f"{name}_act_made")
                self.act_hi = sem(f"{name}_act_hi")
                self.act_ready = sem(f"{name}_act_ready")
                self.x_added = sem(f"{name}_x_added")

        n_ffn = [NormSems(f"n_ffn{i}") for i in range(2)]
        n_mix = NormSems("n_mix")
        n_fin = NormSems("n_fin")
        ffn = [FfnSems(f"ffn{i}") for i in range(2)]

        block = ctx.enter_context(nc.Block())

        TOTAL = 34 * (1 + ("ffn2" in stages)) + (1 + HEAD_BLOCKS * M_HEADS + 4 + 4) * ("M" in stages) \
            + 20 * ("A" in stages) + 20 * ("X" in stages)
        MERGES = 4 * (("M" in stages) + ("A" in stages) + ("X" in stages))

        def narrow(w, k0, kts, c0):
            return w[k0 * P:(k0 + kts) * P, bass.ds(c0, COLS)].rearrange("(k p) c -> p k c", p=P)

        @block.sync
        def _(sp):
            q = Progress()

            def load(n, slot, src, kts=8, width=COLS, peeled=False):
                if not peeled:
                    sp.wait_ge(lo_made, n - 1)
                dst = w_raw[slot][:, 0:kts * width].rearrange("p (k c) -> p k c", c=width)
                sp.dma_start(dst, src).then_inc(raw_loaded[slot], 16)

            def ffn_loads(w_gu, w_down):
                b = q.block
                first = 0
                if b == 0:
                    load(0, 0, narrow(w_gu, 0, KD, 0), peeled=True)
                    load(1, 1, narrow(w_gu, 0, KD, F), peeled=True)
                    first = 1
                with sp.Fori(first, F // COLS) as i:
                    load(b + 2 * i, b % 2, narrow(w_gu, 0, KD, i * COLS))
                    load(b + 2 * i + 1, (b + 1) % 2, narrow(w_gu, 0, KD, F + i * COLS))
                b = q.block = b + 2 * (F // COLS)
                with sp.Fori(0, 2) as i:
                    for m in range(2):
                        for c, k0 in enumerate((0, 8, 16)):
                            o = 3 * m + c
                            load(b + 6 * i + o, (b + o) % 2,
                                 narrow(w_down, k0, min(8, KF - k0), i * 2 * COLS + m * COLS),
                                 kts=min(8, KF - k0))
                q.block = b + 12

            ffn_loads(t["ffn1_w_gu"], t["ffn1_w_down"])
            def load_next(src, kts=8, width=COLS):
                load(q.block, q.block % 2, src, kts, width)
                q.block += 1

            def wide(w, k0, c0):
                return w[k0 * P:(k0 + 4) * P, c0:c0 + WIDE].rearrange("(k p) c -> p k c", p=P)

            def branch_loads(w, gate):
                for m in range(4):
                    load_next(narrow(t["w_in"], 0, KD, C_G + gate * D + m * COLS))
                    if w is not None:
                        load_next(narrow(w, 0, KD, m * COLS))

            if "M" in stages:
                load_next(narrow(t["w_in"], 0, KD, C_IF))
                for h in range(M_HEADS):
                    for m in range(2):
                        load_next(narrow(t["w_in"], 0, KD, C_XM + h * M_HD + m * COLS))
                    for w in ("m_wq", "m_wk", "m_wv"):
                        load_next(t[w][h].rearrange("(k p) c -> p k c", p=P), 4, WIDE)
                    for m in range(2):
                        load_next(narrow(t["w_in"], 0, KD, C_O + h * M_HD + m * COLS))
                    for m in range(2):
                        load_next(wide(t["w_branch_m"], h * MK, m * WIDE), 4, WIDE)
                branch_loads(None, 0)
            if "A" in stages:
                for nh in range(2):
                    for kh in range(2):
                        load_next(wide(t["w_in"], 4 * kh, C_VA + nh * WIDE), 4, WIDE)
                for hp in range(4):
                    load_next(narrow(t["w_in"], 0, KD, C_QA + hp * COLS))
                    load_next(narrow(t["w_in"], 0, KD, C_KA + hp * COLS))
                branch_loads(t["w_branch_a"], 1)
            if "X" in stages:
                for m in range(4):
                    load_next(narrow(t["w_mem_kv"], 0, KD, m * COLS))
                for nh in range(2):
                    for kh in range(2):
                        load_next(wide(t["w_mem_kv"], 4 * kh, D + nh * WIDE), 4, WIDE)
                for m in range(4):
                    load_next(narrow(t["w_in"], 0, KD, C_QX + m * COLS))
                branch_loads(t["w_branch_x"], 2)
            if "M" in stages:
                for m in range(4):
                    load_next(narrow(t["w_out"], 0, KD, m * COLS))
            if "ffn2" in stages:
                ffn_loads(t["ffn2_w_gu"], t["ffn2_w_down"])
            for tt in range(NT):
                sp.wait_ge(out_lo_made, tt + 1)
                sp.wait_ge(out_hi_made, tt + 1)
                sp.dma_start(t["out"][tt * P:(tt + 1) * P, :], o_tok[:, tt, :]).then_inc(out_stored, 16)
            sp.wait_ge(out_stored, 16 * NT)

        @block.gpsimd
        def _(pool):
            pool.memset(ident[:, :], 0.0).then_inc(consts_made, 1)
            pool.memset(ones[:, :], 1.0).then_inc(consts_made, 1)
            pool.memset(eps_c[:, :], EPS).then_inc(consts_made, 1)
            pool.wait_ge(consts_made, 3)
            pool.affine_select(out=ident[:, :], in_=ident[:, :], compare_op=ALU.not_equal, fill=1.0,
                               base=0, pattern=[[-1, P]], channel_multiplier=1).then_inc(consts_made, 1)
            pool.memset(mask[:, :], 0.0).then_inc(consts_made, 1)
            pool.wait_ge(consts_made, 5)
            pool.affine_select(out=mask[:, :], in_=mask[:, :], compare_op=ALU.is_ge, fill=HIDE,
                               base=0, pattern=[[1, P]], channel_multiplier=-1).then_inc(consts_made, 1)
            if "A" in stages:
                pool.wait_ge(ffn[0].x_added, 4)
                pool.dma_start(pos_i[:, :], t["positions"].rearrange("(a s) -> a s", a=1)).then_inc(pos_loaded, 16)
                for j, name in enumerate(("a_lam_q1", "a_lam_k1", "a_lam_q2", "a_lam_k2")):
                    pool.dma_start(smalls[0:A_QK, 32 + j:33 + j], t[name].rearrange("(p a) -> p a", a=1))\
                        .then_inc(lam_loaded, 16)
                pool.dma_start(thr[:, :], t["thresholds"]).then_inc(thr_loaded, 16)
                for k in range(4):
                    pool.dma_start(rb_cur[k * BUCKETS:(k + 1) * BUCKETS, :], t["rel_bias"]).then_inc(thr_loaded, 16)
                    pool.dma_start(rb_prev[k * BUCKETS:k * BUCKETS + 1, :], t["rel_bias"][0:1, :])\
                        .then_inc(thr_loaded, 16)
                    pool.dma_start(rb_prev[k * BUCKETS + 1:(k + 1) * BUCKETS, :], t["rel_bias"][0:BUCKETS - 1, :])\
                        .then_inc(thr_loaded, 16)
                for j in range(4):
                    for k in range(4):
                        pool.dma_start(rb_base[j * 32 + k:j * 32 + 32:4, :],
                                       t["rel_bias"][0:1, :].rearrange("a h -> h a")).then_inc(thr_loaded, 16)
            if "M" in stages:
                pool.wait_ge(ffn[0].x_added, 4)
                pool.memset(sel[:, :, :], 0.0).then_inc(consts_made, 1)
                pool.wait_ge(consts_made, 7)
                pool.affine_select(out=sel[:, :, :], in_=sel[:, :, :], compare_op=ALU.not_equal, fill=1.0,
                                   base=0, pattern=[[-1, M_HEADS], [0, P]], channel_multiplier=1)\
                    .then_inc(consts_made, 1)
            if "A" in stages:
                for i in range(2):
                    pool.wait_ge(bias_stored[i], 64 * (S // QSTEP // 2))
                pool.wait_ge(mg_made, 4)
                for u in range(4 * A_HEADS):
                    if u >= 4:
                        pool.wait_ge(a_shifted, 2 * (u - 4) + 2)
                    head = bias_dram[u // 4 * 4:u // 4 * 4 + 4, (u % 4) * P:(u % 4 + 1) * P, :]
                    pool.dma_start(bias_sb[u % 4][:, :].rearrange("p (k c) -> p k c", k=4),
                                   head.rearrange("k q c -> q k c")).then_inc(bias_loaded[u % 4], 16)

        @block.scalar
        def _(act):
            q = Progress()
            act.dma_start(x_tok[:, :, :], t["x"].rearrange("(a p) d -> p a d", p=P)).then_inc(x_loaded, 16)
            for name in ("ffn1_norm", "mix_norm", "mem_norm", "ffn2_norm", "final_norm", "m_head_norm",
                         "a_head_norm", "m_conv_b", "b_gate"):
                r, n = PC[name]
                act.dma_start(prm1[r:r + n, :], t[name].rearrange("(k p) -> k p", p=P)).then_inc(prm_loaded, 16)
            act.dma_start(prm2[:, :], t["m_conv_w"].rearrange("j (k p) -> (j k) p", p=P)).then_inc(prm_loaded, 16)

            def split_hi(n, slot):
                act.wait_ge(raw_loaded[slot], 16 * (n // 2 + 1) if isinstance(n, int) else n)
                nc.scalar.activation(w_hi[slot][:, :], w_raw[slot][:, :], ACT.Copy).then_inc(hi_made, 1)

            def hi_at(b, o, step=0, i=0):
                n, slot = b + o, (b + o) % 2
                act.wait_ge(raw_loaded[slot], 16 * (n // 2 + 1) + (8 * step) * i if step else 16 * (n // 2 + 1))
                if n >= 2:
                    act.wait_ge(block_done, (n - 1) + step * i if step else n - 1)
                nc.scalar.activation(w_hi[slot][:, :], w_raw[slot][:, :], ACT.Copy).then_inc(hi_made, 1)

            def norm(s, x_sem, x_count):
                act.wait_ge(x_sem, x_count)
                act.wait_ge(consts_made, 4)
                for g in range(4):
                    nc.scalar.activation(sq[:, 2 * g:2 * g + 2, :], xT[:, 2 * g:2 * g + 2, :],
                                         ACT.Square).then_inc(s.sq_made, 1)
                act.wait_ge(s.sum_ready, 1)
                nc.scalar.activation(lnv[:, :], pair[3][:, 0, :], ACT.Ln, bias=eps_c[:, 0:1],
                                     scale=1.0 / D).then_inc(s.ln_made, 1)
                act.wait_ge(s.ln_made, 1)
                nc.scalar.activation(rinv[:, :], lnv[:, :], ACT.Exp, scale=-0.5).then_inc(s.r_made, 1)

            def norm_hi(s):
                for k in range(KD):
                    act.wait_ge(s.raw_made, k + 1)
                    nc.scalar.activation(h_hi[:, k, :], sq[:, k, :], ACT.Copy).then_inc(s.hi_made, 1)

            def ffn_act(s):
                b = q.block
                with act.Fori(0, F // COLS) as i:
                    act.wait_ge(block_done, b + 1 + 2 * i)
                    nc.scalar.activation(gate_s[:, :, :], pair[0][:, :, :], ACT.Silu).then_inc(s.gate_made, 1)
                    hi_at(b, 2, 2, i)
                    act.wait_ge(s.act_made, i + 1)
                    nc.scalar.activation(act_hi[:, bass.ds(2 * i, 2), :], act_f[:, :, :], ACT.Copy)\
                        .then_inc(s.act_hi, 1)
                    hi_at(b, 3, 2, i)
                b = q.block = b + 2 * (F // COLS)
                last = b + 12 == TOTAL
                with act.Fori(0, 1 if last else 2) as i:
                    for o in range(6):
                        hi_at(b, o + 2, 6, i)
                if last:
                    for o in range(4):
                        hi_at(b, 6 + o + 2)
                q.block = b + 12

            def next_hi():
                if q.block + 2 < TOTAL:
                    hi_at(q.block + 2, 0)
                q.block += 1

            def done(k=0):
                act.wait_ge(block_done, q.block + 1 + k)

            chain = [0]

            def link(ins):
                chain[0] += 1
                ins.then_inc(chain_a, 1)
                act.wait_ge(chain_a, chain[0])

            def bias_act():
                act.wait_ge(thr_loaded, 16 * 29)
                act.wait_ge(pos_made, 2)
                for i in range(S // QSTEP):
                    act.wait_ge(bias_summed, i + 1)
                    if i >= 2:
                        act.wait_ge(bias_stored[i % 2], 64 * (i // 2))
                    nc.scalar.activation(bias_out[i % 2][:, :], pair[i % 2][:, 0, :], ACT.Identity,
                                         bias=rb_base[:, 0:1]).then_inc(bias_made, 1)
                    act.wait_ge(bias_made, i + 1)
                    for j in range(4):
                        q0 = i * QSTEP + 4 * j
                        act.dma_start(bias_dram[:, q0:q0 + 4, :],
                                      bias_out[i % 2][j * 32:(j + 1) * 32, :]
                                      .rearrange("p (q c) -> p q c", q=4)).then_inc(bias_stored[i % 2], 16)
                for i in range(2):
                    act.wait_ge(bias_stored[i], 64 * (S // QSTEP // 2))

            def gates_act():
                for j in range(2):
                    act.dma_start(smalls[0:M_HEADS, j:j + 1],
                                  t["b_if"][j * M_HEADS:(j + 1) * M_HEADS].rearrange("(h a) -> h a", a=1))\
                        .then_inc(bif_loaded, 16)
                act.wait_ge(bif_loaded, 32)
                done()
                nc.scalar.activation(g_i[:, :], pair[0][0:M_HEADS, 0, :], ACT.Identity, bias=smalls[0:M_HEADS, 0:1])
                nc.scalar.activation(g_f[:, :], pair[0][0:M_HEADS, 1, :], ACT.Identity, bias=smalls[0:M_HEADS, 1:2])
                link(nc.scalar.activation(g_abs[:, :], pair[0][0:M_HEADS, 1, :], ACT.Abs, bias=smalls[0:M_HEADS, 1:2]))
                link(nc.scalar.activation(g_abs[:, :], g_abs[:, :], ACT.Exp, scale=-1.0))
                nc.scalar.activation(g_ln[:, :], g_abs[:, :], ACT.Ln, bias=ones[0:M_HEADS, 0:1]).then_inc(g_pre, 1)
                next_hi()
                act.wait_ge(g_arg, 1)
                nc.scalar.activation(dec_row[:, :], dec_row[:, :], ACT.Exp).then_inc(g_exp, 1)
                nc.scalar.activation(g_rows[:, 1:4, :], g_rows[:, 1:4, :], ACT.Exp).then_inc(g_exp, 1)

            def head_act(h):
                for m in range(2):
                    done()
                    if m == 0 and h > 0:
                        act.wait_ge(ymh_made, MK * h)
                    nc.scalar.activation(xm_f[:, 2 * m:2 * m + 2, 3:3 + S], pair[m][:, :, :], ACT.Copy)\
                        .then_inc(xm_made, 1)
                    nc.scalar.activation(xm_hi[:, 2 * m:2 * m + 2, :], pair[m][:, :, :], ACT.Copy).then_inc(xmh_made, 1)
                    next_hi()
                act.wait_ge(conv_made, h + 1)
                link(nc.scalar.activation(conv[:, :, :], conv[:, :, :], ACT.Silu))
                nc.scalar.activation(xc_hi[:, :, :], conv[:, :, :], ACT.Copy).then_inc(xc_made, 1)
                done()
                for j in range(2):
                    nc.scalar.activation(q_f[:, 2 * j:2 * j + 2, :], pair[2 + j][:, :, :], ACT.Copy).then_inc(q_made, 1)
                next_hi()
                next_hi()
                done()
                for j in range(2):
                    nc.scalar.activation(v_f[:, 2 * j:2 * j + 2, :], pair[2 + j][:, :, :], ACT.Copy).then_inc(v_made, 1)
                next_hi()
                for m in range(2):
                    done()
                    nc.scalar.activation(o_sig[:, 2 * m:2 * m + 2, :], pair[m][:, :, :], ACT.Sigmoid).then_inc(o_made, 1)
                    next_hi()
                act.wait_ge(w_arg, h + 1)
                nc.scalar.activation(w_in_tr[:, :, :], w_in_tr[:, :, :], ACT.Exp).then_inc(w_made, 1)
                for c in range(CHUNKS):
                    g = CHUNKS * h + c
                    if c < CHUNKS - 1:
                        act.wait_ge(kt_ready, 3 * h + c + 1)
                        if c > 0:
                            act.wait_ge(upd_ready, 2 * (3 * h + c))
                        nc.scalar.activation(k_ws[:, :], pair[2][:, 1, :], ACT.Copy,
                                             scale=tokp[:, 3, c, h:h + 1]).then_inc(kws_made, 1)
                    act.wait_ge(r_made, g + 1)
                    nc.scalar.activation(h_m[:, c, :], pair[0][:, 0, :], ACT.Copy,
                                         scale=den[:, 4:5]).then_inc(h_part, 1)
                    if c > 0:
                        act.wait_ge(h_made, 3 * h + c)
                    else:
                        act.wait_ge(h_part, g + 1)
                    nc.scalar.activation(y_f[0][:, :], h_m[:, c, :], ACT.Square, accum_out=sumsq[:, c:c + 1])\
                        .then_inc(chain_a, 1)
                    chain[0] += 1
                    act.wait_ge(chain_a, chain[0])
                link(nc.scalar.activation(sumsq, sumsq, ACT.Ln, bias=eps_c[:, 0:1], scale=1.0 / M_HD))
                link(nc.scalar.activation(sumsq, sumsq, ACT.Exp, scale=-0.5))
                for c in range(CHUNKS):
                    nc.scalar.activation(h_m[:, c, :], h_m[:, c, :], ACT.Copy, scale=sumsq[:, c:c + 1])\
                        .then_inc(hn_made, 1)
                for e in range(MK):
                    act.wait_ge(yf_made, MK * h + e + 1)
                    nc.scalar.activation(ym_hi[:, e, :], y_f[e % 2][:, :], ACT.Copy).then_inc(ymh_made, 1)
                next_hi()
                next_hi()

            def merge_act(gate, base):
                for m in range(4):
                    done()
                    if base + m >= 1:
                        act.wait_ge(mg_made, base + m)
                    for j in range(2):
                        ins = nc.scalar.activation(g_sig[:, j, :], pair[2 * (m % 2)][:, j, :], ACT.Sigmoid,
                                                   bias=pcol("b_gate", 8 * gate + 2 * m + j))
                    ins.then_inc(g_sig_made, 1)
                    next_hi()
                    if gate:
                        next_hi()

            def attention_act():
                for nh in range(2):
                    next_hi()
                    done()
                    for j in range(2):
                        nc.scalar.activation(va[:, 2 * j:2 * j + 2, nh * WIDE:(nh + 1) * WIDE],
                                             pair[2 * nh + j][:, :, :], ACT.Copy).then_inc(va_made, 1)
                    next_hi()
                act.wait_ge(lam_summed, 1)
                nc.scalar.activation(smalls[:, 2:4], pair[3][:, 1, 0:2], ACT.Exp).then_inc(g_exp, 1)
                for hp in range(4):
                    done()
                    if hp:
                        act.wait_ge(a_scored, 8 * hp)
                    nc.scalar.activation(q_a[:, :, :], pair[0][:, :, :], ACT.Copy).then_inc(qa_made, 1)
                    next_hi()
                    next_hi()
                    for u in range(8 * hp, 8 * hp + 8):
                        for j in range(2):
                            act.wait_ge(a_shifted, 2 * u + j + 1)
                            nc.scalar.activation(probs[u % 2][:, j, :], probs[u % 2][:, j, :], ACT.Exp,
                                                 bias=smalls[:, 8 + 2 * (u % 2) + j:9 + 2 * (u % 2) + j],
                                                 scale=A_SCALE,
                                                 accum_out=smalls[:, 12 + 2 * (u % 2) + j:13 + 2 * (u % 2) + j])\
                                .then_inc(a_exp, 1)
                        act.wait_ge(a_turned, u + 1)
                        if u % 4 == 0 and u:
                            act.wait_ge(a_out, u // 4)
                        nc.scalar.activation(a_tr[:, :, (u % 4) * P:(u % 4 + 1) * P],
                                             pair[0][:, u % 2, :].rearrange("p (k c) -> p k c", k=NT),
                                             ACT.Copy).then_inc(a_tr_made, 1)
                        if u % 4 == 3:
                            e = u // 4
                            act.wait_ge(a_out, e + 1)
                            nc.scalar.activation(o_a[:, :], pair[1][:, 0, :], ACT.Copy)
                            nc.scalar.activation(o_sq[:, :], pair[1][:, 0, :], ACT.Square).then_inc(a_sq, 1)
                            act.wait_ge(a_sum, e + 1)
                            link(nc.scalar.activation(o_ln[:, :], pair[1][:, 1, :], ACT.Ln, bias=eps_c[:, 0:1],
                                                      scale=1.0 / P))
                            nc.scalar.activation(o_ln[:, :], o_ln[:, :], ACT.Exp, scale=-0.5).then_inc(a_r, 1)
                            act.wait_ge(a_y, e + 1)
                            nc.scalar.activation(ya_hi[:, e, :], y_af[:, :], ACT.Copy).then_inc(a_yh, 1)

            def cross_act():
                act.dma_start(mem_tok[:, :, :], t["mem"].rearrange("(a p) d -> p a d", p=P)).then_inc(mem_loaded, 16)
                act.wait_ge(mem_loaded, 16)
                for a in range(MT):
                    ins = nc.scalar.activation(mem_sq[:, a, :], mem_tok[:, a, :], ACT.Square,
                                               accum_out=smalls[:, 20 + a:21 + a])
                link(ins)
                link(nc.scalar.activation(smalls[:, 20:22], smalls[:, 20:22], ACT.Ln, bias=eps_c[:, 0:1],
                                          scale=1.0 / D))
                link(nc.scalar.activation(smalls[:, 20:22], smalls[:, 20:22], ACT.Exp, scale=-0.5))
                for a in range(MT):
                    nc.scalar.activation(mem_tok[:, a, :], mem_tok[:, a, :], ACT.Copy,
                                         scale=smalls[:, 20 + a:21 + a]).then_inc(mem_r, 1)
                for k in range(KD):
                    act.wait_ge(memn_made, k + 1)
                    nc.scalar.activation(memn_hi[:, k, :], memn_f[:, k, :], ACT.Copy).then_inc(memh_made, 1)
                for m in range(4):
                    done()
                    nc.scalar.activation(k_x[:, 2 * m:2 * m + 2, :], pair[m % 2][:, :, 0:MEM], ACT.Copy)\
                        .then_inc(kx_made, 1)
                    next_hi()
                for nh in range(2):
                    next_hi()
                    done()
                    nc.scalar.activation(v_x[:, :, nh * WIDE:(nh + 1) * WIDE], pair[2 + nh][:, :, :], ACT.Copy)\
                        .then_inc(vx_made, 1)
                    next_hi()
                for m in range(4):
                    done()
                    nc.scalar.activation(q_x[:, 2 * m:2 * m + 2, :], pair[m % 2][:, :, :], ACT.Copy)\
                        .then_inc(qx_made, 1)
                    next_hi()
                for u in range(4 * X_HEADS):
                    act.wait_ge(x_max, u + 1)
                    nc.scalar.activation(p_x[u % 2][:, :], pair[2][:, u % 2, 0:MEM], ACT.Exp,
                                         bias=smalls[:, 24 + u % 2:25 + u % 2], scale=X_SCALE,
                                         accum_out=smalls[:, 26 + u % 2:27 + u % 2]).then_inc(x_exp, 1)
                    act.wait_ge(x_turned, u + 1)
                    if u % 4 == 0 and u:
                        act.wait_ge(x_out, u // 4)
                    nc.scalar.activation(p_tr[:, :, (u % 4) * P:(u % 4 + 1) * P],
                                         pair[3][:, u % 2, 0:MEM].rearrange("p (k c) -> p k c", k=MT),
                                         ACT.Copy).then_inc(x_tr_made, 1)
                    if u % 4 == 3:
                        h = u // 4
                        act.wait_ge(x_out, h + 1)
                        nc.scalar.activation(yx_hi[:, 2 * h:2 * h + 2, :], pair[h % 2][:, :, :], ACT.Copy)\
                            .then_inc(x_yh, 1)

            def out_act():
                act.wait_ge(mg_made, MERGES)
                for k in range(4):
                    nc.scalar.activation(mg_hi[:, 2 * k:2 * k + 2, :], merged[:, 2 * k:2 * k + 2, :], ACT.Copy)\
                        .then_inc(mgh_made, 1)
                for m in range(4):
                    next_hi()

            hi_at(0, 0)
            hi_at(0, 1)
            norm(n_ffn[0], xt_made, KD)
            norm_hi(n_ffn[0])
            ffn_act(ffn[0])
            if "A" in stages:
                bias_act()
            if "M" in stages:
                norm(n_mix, ffn[0].x_added, 4)
                norm_hi(n_mix)
                gates_act()
                for h in range(M_HEADS):
                    head_act(h)
                merge_act(0, 0)
            if "A" in stages:
                attention_act()
                merge_act(1, 4)
            if "X" in stages:
                cross_act()
                merge_act(2, 8)
            if "M" in stages:
                out_act()
            if "ffn2" in stages:
                norm(n_ffn[1], x_mixed if "M" in stages else ffn[0].x_added, 4)
                norm_hi(n_ffn[1])
                ffn_act(ffn[1])
            norm(n_fin, ffn[1].x_added if "ffn2" in stages else x_mixed if "M" in stages else ffn[0].x_added, 4)
            for tt in range(NT):
                act.wait_ge(out_turned, 2 * tt + 2)
                nc.scalar.activation(o_tok[:, tt, S:2 * S], pair[2 + tt % 2][:, 1, :], ACT.Copy)\
                    .then_inc(out_hi_made, 1)

        @block.vector
        def _(dve):
            q = Progress()
            dve.wait_ge(par_turned, 1)
            nc.vector.tensor_copy(par[:, 0:104], pair[3][:, 0, 0:104])
            nc.vector.tensor_copy(par[:, 104:168], pair[3][:, 0, 128:192]).then_inc(par_made, 1)
            for k in range(KD):
                dve.wait_ge(xt_turned, k + 1)
                nc.vector.tensor_copy(xT[:, k, :], pair[(k // 2) % 2][:, k % 2, :]).then_inc(xt_made, 1)

            def lo_at(b, o, step=0, i=0):
                n, slot = b + o, (b + o) % 2
                dve.wait_ge(hi_made, (n + 1) + step * i if step else n + 1)
                nc.vector.tensor_tensor(w_lo[slot][:, :], w_raw[slot][:, :], w_hi[slot][:, :].bitcast(F32),
                                        ALU.subtract).then_inc(lo_made, 1)

            def norm_raw(s, gain, last=False):
                dve.wait_ge(s.r_made, 1)
                for k in range(KD):
                    nc.vector.scalar_tensor_tensor(out=sq[:, k, :], in0=xT[:, k, :], scalar=pcol(gain, k),
                                                   in1=rinv[:, :], op0=ALU.mult, op1=ALU.mult)\
                        .then_inc(s.raw_made, 1)

            def norm_lo(s):
                for k in range(KD):
                    dve.wait_ge(s.hi_made, k + 1)
                    nc.vector.tensor_tensor(h_lo[:, k, :], sq[:, k, :], h_hi[:, k, :].bitcast(F32),
                                            ALU.subtract).then_inc(s.ready, 1)

            def ffn_dve(s):
                b = q.block
                with dve.Fori(0, F // COLS) as i:
                    lo_at(b, 2, 2, i)
                    dve.wait_ge(block_done, b + 2 + 2 * i)
                    dve.wait_ge(s.gate_made, i + 1)
                    nc.vector.tensor_tensor(act_f[:, :, :], gate_s[:, :, :], pair[1][:, :, :], ALU.mult)\
                        .then_inc(s.act_made, 1)
                    dve.wait_ge(s.act_hi, i + 1)
                    nc.vector.tensor_tensor(act_lo[:, bass.ds(2 * i, 2), :], act_f[:, :, :],
                                            act_hi[:, bass.ds(2 * i, 2), :].bitcast(F32), ALU.subtract)\
                        .then_inc(s.act_ready, 1)
                    lo_at(b, 3, 2, i)
                b = q.block = b + 2 * (F // COLS)
                last = b + 12 == TOTAL
                def down(i, loop, tail=False):
                    for m in range(2):
                        for c in range(3):
                            o = 3 * m + c
                            if c == 2:
                                dve.wait_ge(block_done, b + o + 1 + 6 * i)
                                xs = xT[:, bass.ds(4 * i + 2 * m, 2), :]
                                nc.vector.scalar_tensor_tensor(out=xs, in0=pair[2 + m][:, :, :], scalar=0.5,
                                                               in1=xs, op0=ALU.mult, op1=ALU.add)\
                                    .then_inc(s.x_added, 1)
                            if not (tail and o + 2 >= 6):
                                lo_at(b, o + 2, 6, i)
                with dve.Fori(0, 1 if last else 2) as i:
                    down(i, True)
                if last:
                    down(1, False, True)
                q.block = b + 12

            def next_lo():
                if q.block + 2 < TOTAL:
                    lo_at(q.block + 2, 0)
                q.block += 1

            def done(k=0):
                dve.wait_ge(block_done, q.block + 1 + k)

            chain = [0]

            def link(ins):
                chain[0] += 1
                ins.then_inc(chain_d, 1)
                dve.wait_ge(chain_d, chain[0])

            def bias_dve():
                v = nc.vector
                dve.wait_ge(ffn[0].x_added, 4)
                dve.wait_ge(thr_loaded, 16 * 29)
                link(v.tensor_tensor(rb_cur[:, :], rb_cur[:, :], rb_prev[:, :], ALU.subtract))
                link(v.tensor_scalar(rb_cur[:, :], rb_cur[:, :], 1.0 / A_SCALE, None, ALU.mult))
                for k in range(4):
                    link(v.memset(rb_cur[k * BUCKETS:k * BUCKETS + 1, :], HIDE))
                v.tensor_scalar(rb_base[:, :], rb_base[:, :], 1.0 / A_SCALE, None, ALU.mult).then_inc(pos_made, 1)
                link(v.memset(step_f[:, :], 0.0))
                for k in range(4):
                    ins = v.tensor_copy(step_f[k * BUCKETS:(k + 1) * BUCKETS, k:32:4],
                                        rb_cur[k * BUCKETS:(k + 1) * BUCKETS, :])
                link(ins)
                for part in range(3):
                    link(v.tensor_copy(step_b[part][:, :], step_f[:, :]))
                    if part < 2:
                        link(v.tensor_tensor(step_f[:, :], step_f[:, :], step_b[part][:, :], ALU.subtract))
                dve.wait_ge(pos_loaded, 16)
                v.tensor_scalar(pos_h[:, :], pos_i[:, :], 16, None, ALU.arith_shift_right)
                link(v.tensor_scalar(pos_l[:, :], pos_i[:, :], 65535, None, ALU.bitwise_and))
                v.tensor_copy(pos_hf[:, :], pos_h[:, :])
                link(v.tensor_copy(pos_lf[:, :], pos_l[:, :]))
                link(v.tensor_copy(smalls[0:1, 4:5], pos_hf[:, 0:1]))
                link(v.tensor_copy(smalls[0:1, 5:6], pos_lf[:, 0:1]))
                link(v.tensor_scalar(pos_hf[:, :], pos_hf[:, :], smalls[0:1, 4:5], None, ALU.subtract))
                link(v.tensor_scalar(pos_lf[:, :], pos_lf[:, :], smalls[0:1, 5:6], None, ALU.subtract))
                link(v.memset(sign_row[:, :], 1.0))
                link(v.memset(sign_row[:, 0:P:BUCKETS], -1.0))
                v.scalar_tensor_tensor(out=pos_r[:, :], in0=pos_hf[:, :], scalar=65536.0, in1=pos_lf[:, :],
                                       op0=ALU.mult, op1=ALU.add).then_inc(pos_made, 1)
                dve.wait_ge(pos_spread, 1)
                v.tensor_scalar(pq_s[:, :], pair[2][:, 0, :], thr[:, 0:1], None, ALU.subtract)
                for k in range(4):
                    r = slice(k * BUCKETS, (k + 1) * BUCKETS)
                    ins = v.tensor_copy(pk_s[r, :], pair[2][r, 0, k * KEYS4:(k + 1) * KEYS4])
                link(ins)
                for i in range(S // QSTEP):
                    if i >= 2:
                        dve.wait_ge(bias_summed, i - 1)
                    v.tensor_tensor(past[i % 2][:, :, :],
                                    pq_s[:, i * QSTEP:(i + 1) * QSTEP].unsqueeze(2).to_broadcast([P, QSTEP, KEYS4]),
                                    pk_s[:, :].unsqueeze(1).to_broadcast([P, QSTEP, KEYS4]),
                                    ALU.is_ge).then_inc(past_made, 1)

            def gates_dve():
                v = nc.vector
                link(v.memset(one_row[:, :], 1.0))
                dve.wait_ge(g_pre, 1)
                link(v.scalar_tensor_tensor(out=g_lf[:, :], in0=g_f[:, :], scalar=0.0, in1=g_ln[:, :],
                                            op0=ALU.min, op1=ALU.subtract))
                link(v.tensor_tensor_scan(g_b[:, :], one_row[:, :], g_lf[:, :], 0.0, ALU.mult, ALU.add))
                c_row = g_rows[:, 0, :]
                link(v.tensor_tensor(c_row, g_i[:, :], g_b[:, :], ALU.subtract))
                link(v.tensor_tensor_scan(g_m[:, :], c_row, c_row, 0.0, ALU.max, ALU.max))
                link(v.tensor_scalar(g_neg[:, :], g_m[:, :], -1.0, None, ALU.mult))
                v.memset(g_rows[:, 1, 0:P], 0.0)
                v.memset(g_rows[:, 3, S - P:S], 0.0)
                v.tensor_tensor(g_rows[:, 2, :], g_neg[:, :], g_b[:, :], ALU.subtract)
                for c in range(1, CHUNKS):
                    v.tensor_scalar(g_rows[:, 1, c * P:(c + 1) * P], g_neg[:, c * P:(c + 1) * P],
                                    g_m[:, c * P - 1:c * P], None, ALU.add)
                    v.tensor_scalar(g_rows[:, 3, (c - 1) * P:c * P], g_rows[:, 0, (c - 1) * P:c * P],
                                    g_m[:, c * P - 1:c * P], None, ALU.subtract)
                v.tensor_tensor(dec_row[:, :], g_m[:, P - 1:3 * P - 1:P], g_m[:, 2 * P - 1:4 * P - 1:P], ALU.subtract)\
                    .then_inc(g_arg, 1)
                next_lo()
                dve.wait_ge(g_exp, 1)
                for c in range(2):
                    ins = v.tensor_scalar(dec_diag[:, c, :], ident[0:M_HEADS, 0:M_HEADS], dec_row[:, c:c + 1], None,
                                          ALU.mult)
                ins.then_inc(g_diag, 1)
                dve.wait_ge(g_turned, 1)
                v.tensor_copy(decay, pair[1][:, 1, 0:8])
                v.tensor_copy(tokp[:, :, :, :].rearrange("p a c h -> p (a c h)"), pair[1][:, 0, 0:64])\
                    .then_inc(g_ready, 1)
                link(v.memset(xm_f[:, :, 0:3], 0.0))

            def head_dve(h):
                v = nc.vector
                if h > 0:
                    link(v.memset(xm_f[:, :, 0:3], 0.0))
                for m in range(2):
                    dve.wait_ge(xmh_made, 2 * h + m + 1)
                    v.tensor_tensor(xm_lo[:, 2 * m:2 * m + 2, :], xm_f[:, 2 * m:2 * m + 2, 3:3 + S],
                                    xm_hi[:, 2 * m:2 * m + 2, :].bitcast(F32), ALU.subtract).then_inc(xml_made, 1)
                    next_lo()
                for e in range(MK):
                    ins = v.tensor_scalar(conv[:, e, :], xm_f[:, e, 3:3 + S], pcol("m_conv_w", 48 + MK * h + e),
                                          pcol("m_conv_b", MK * h + e), ALU.mult, ALU.add)
                for tap in range(3):
                    link(ins)
                    for e in range(MK):
                        ins = v.scalar_tensor_tensor(out=conv[:, e, :], in0=xm_f[:, e, tap:tap + S],
                                                     scalar=pcol("m_conv_w", 16 * tap + MK * h + e),
                                                     in1=conv[:, e, :], op0=ALU.mult, op1=ALU.add)
                ins.then_inc(conv_made, 1)
                dve.wait_ge(xc_made, h + 1)
                v.tensor_tensor(xc_lo[:, :, :], conv[:, :, :], xc_hi[:, :, :].bitcast(F32), ALU.subtract)\
                    .then_inc(xcl_made, 1)
                next_lo()
                done()
                for j in range(2):
                    v.tensor_scalar(k_f[:, 2 * j:2 * j + 2, :], pair[j][:, :, :], M_HD ** -0.5, None, ALU.mult)\
                        .then_inc(k_made, 1)
                next_lo()
                next_lo()
                next_lo()
                next_lo()
                dve.wait_ge(negm_spread, h + 1)
                for c in range(CHUNKS):
                    ins = v.scalar_tensor_tensor(out=w_in_tr[:, c, :], in0=pair[3][:, 0, c * P:(c + 1) * P],
                                                 scalar=tokp[:, 0, c, h:h + 1], in1=mask[:, :],
                                                 op0=ALU.add, op1=ALU.add)
                ins.then_inc(w_arg, 1)
                dve.wait_ge(w_made, h + 1)
                for c in range(CHUNKS):
                    g = CHUNKS * h + c
                    dve.wait_ge(sc_ready, g + 1)
                    v.tensor_tensor(s_w[:, :], pair[2][:, 0, 0:P], w_in_tr[:, c, :], ALU.mult).then_inc(sw_made, 1)
                    dve.wait_ge(num_ready, g + 1)
                    if c == 0:
                        link(v.tensor_copy(den[:, 0:1], pair[1][:, 0, 0:1]))
                    else:
                        link(v.tensor_copy(den[:, 1:2], pair[1][:, 0, 0:1]))
                        link(v.scalar_tensor_tensor(out=den[:, 0:1], in0=pair[1][:, 0, 1:2],
                                                    scalar=tokp[:, 1, c, h:h + 1], in1=den[:, 1:2],
                                                    op0=ALU.mult, op1=ALU.add))
                    link(v.tensor_scalar(den[:, 3:4], den[:, 0:1], -1.0, tokp[:, 2, c, h:h + 1], ALU.mult, ALU.max))
                    link(v.tensor_tensor(den[:, 2:3], den[:, 0:1], den[:, 3:4], ALU.max))
                    v.reciprocal(den[:, 4:5], den[:, 2:3]).then_inc(r_made, 1)
                    if c > 0:
                        dve.wait_ge(r_made, g + 1)
                        link(v.tensor_tensor(den[:, 5:6], den[:, 4:5], tokp[:, 1, c, h:h + 1], ALU.mult))
                        dve.wait_ge(h_part, g + 1)
                        v.scalar_tensor_tensor(out=h_m[:, c, :], in0=pair[0][:, 1, :], scalar=den[:, 5:6],
                                               in1=h_m[:, c, :], op0=ALU.mult, op1=ALU.add).then_inc(h_made, 1)
                    if c < CHUNKS - 1:
                        for half in range(2):
                            dve.wait_ge(upd_ready, 2 * (3 * h + c) + half + 1)
                            cs = c_st[:, 2 * half:2 * half + 2, :]
                            ns = n_st[:, 2 * half:2 * half + 2]
                            if c == 0:
                                v.tensor_copy(ns, pair[1][:, 1, 2 * half:2 * half + 2])
                                v.tensor_copy(cs, pair[3][:, :, :]).then_inc(c_made, 1)
                            else:
                                dk = decay[:, (c - 1) * M_HEADS + h:(c - 1) * M_HEADS + h + 1]
                                v.scalar_tensor_tensor(out=ns, in0=ns, scalar=dk,
                                                       in1=pair[1][:, 1, 2 * half:2 * half + 2],
                                                       op0=ALU.mult, op1=ALU.add)
                                v.scalar_tensor_tensor(out=cs, in0=cs, scalar=dk, in1=pair[3][:, :, :],
                                                       op0=ALU.mult, op1=ALU.add).then_inc(c_made, 1)
                for e in range(MK):
                    dve.wait_ge(h_turned, MK * h + e + 1)
                    if e >= 2:
                        dve.wait_ge(ymh_made, MK * h + e - 1)
                    link(v.scalar_tensor_tensor(out=y_f[e % 2][:, :], in0=pair[2 + e // 2][:, e % 2, :],
                                                scalar=pcol("m_head_norm", MK * h + e), in1=o_sig[:, e, :],
                                                op0=ALU.mult, op1=ALU.mult))
                    v.engine_nop().then_inc(yf_made, 1)
                    dve.wait_ge(ymh_made, MK * h + e + 1)
                    v.tensor_tensor(ym_lo[:, e, :], y_f[e % 2][:, :], ym_hi[:, e, :].bitcast(F32), ALU.subtract)\
                        .then_inc(yml_made, 1)
                for m in range(2):
                    done()
                    for j in range(2):
                        ms = merged[:, 4 * m + 2 * j:4 * m + 2 * j + 2, :]
                        if h == 0:
                            ins = v.tensor_copy(ms, pair[2 * m + j][:, :, :])
                        else:
                            ins = v.tensor_tensor(ms, ms, pair[2 * m + j][:, :, :], ALU.add)
                        ins.then_inc(bm_added, 1)
                    next_lo()

            def merge_dve(gate, base):
                v = nc.vector
                for m in range(4):
                    ms = merged[:, 2 * m:2 * m + 2, :]
                    if gate == 0:
                        dve.wait_ge(g_sig_made, base + m + 1)
                        v.tensor_tensor(ms, ms, g_sig[:, :, :], ALU.mult).then_inc(mg_made, 1)
                        next_lo()
                    else:
                        next_lo()
                        done()
                        dve.wait_ge(g_sig_made, base + m + 1)
                        link(v.tensor_tensor(g_tmp[:, :, :], g_sig[:, :, :], pair[2 * (m % 2) + 1][:, :, :], ALU.mult))
                        v.tensor_tensor(ms, ms, g_tmp[:, :, :], ALU.add).then_inc(mg_made, 1)
                        next_lo()

            def attention_dve():
                v = nc.vector
                for _ in range(4):
                    next_lo()
                dve.wait_ge(g_exp, 3)
                link(v.tensor_tensor(smalls[:, 6:7], smalls[:, 3:4], smalls[:, 2:3], ALU.subtract))
                link(v.tensor_scalar(smalls[:, 6:7], smalls[:, 6:7], -LAM_INIT, None, ALU.add))
                g0 = PC["a_head_norm"][0]
                link(v.tensor_scalar(par[:, 168:176], par[:, g0:g0 + 8], 1.0 - LAM_INIT, None, ALU.mult))
                for hp in range(4):
                    next_lo()
                    done()
                    if hp:
                        dve.wait_ge(a_scored, 8 * hp)
                    v.tensor_copy(k_a[:, :, :], pair[1][:, :, :]).then_inc(ka_made, 1)
                    next_lo()
                    for u in range(8 * hp, 8 * hp + 8):
                        dve.wait_ge(a_scored, u + 1)
                        dve.wait_ge(bias_loaded[u % 4], 16 * (u // 4 + 1))
                        b = u % 2
                        for j in range(2):
                            link(v.tensor_tensor_reduce(probs[b][:, j, :], pair[2 + b][:, j, :], bias_sb[u % 4][:, :],
                                                        1.0, HIDE * 10, ALU.add, ALU.max, smalls[:, 16 + j:17 + j]))
                            v.tensor_scalar(smalls[:, 8 + 2 * b + j:9 + 2 * b + j], smalls[:, 16 + j:17 + j],
                                            -A_SCALE, None, ALU.mult).then_inc(a_shifted, 1)
                        dve.wait_ge(a_exp, 2 * u + 2)
                        link(v.reciprocal(smalls[:, 18:20], smalls[:, 12 + 2 * b:14 + 2 * b]))
                        link(v.tensor_tensor(smalls[:, 19:20], smalls[:, 19:20], smalls[:, 6:7], ALU.mult))
                        if u >= 2:
                            dve.wait_ge(a_turned, u - 1)
                        link(v.tensor_scalar(a_mix[b][:, :], probs[b][:, 0, :], smalls[:, 18:19], None, ALU.mult))
                        v.scalar_tensor_tensor(out=a_mix[b][:, :], in0=probs[b][:, 1, :], scalar=smalls[:, 19:20],
                                               in1=a_mix[b][:, :], op0=ALU.mult, op1=ALU.add).then_inc(a_mixed, 1)
                        if u % 4 == 3:
                            e = u // 4
                            dve.wait_ge(a_r, e + 1)
                            v.scalar_tensor_tensor(out=y_af[:, :], in0=o_a[:, :], scalar=par[:, 168 + e:169 + e],
                                                   in1=o_ln[:, :], op0=ALU.mult, op1=ALU.mult).then_inc(a_y, 1)
                            dve.wait_ge(a_yh, e + 1)
                            v.tensor_tensor(ya_lo[:, e, :], y_af[:, :], ya_hi[:, e, :].bitcast(F32), ALU.subtract)\
                                .then_inc(a_yl, 1)

            def cross_dve():
                v = nc.vector
                for k in range(KD):
                    dve.wait_ge(mem_turned, k + 1)
                    link(v.tensor_scalar(memn_f[:, k, :], pair[0][:, k % 2, 0:MEM], pcol("mem_norm", k), None, ALU.mult))
                    v.engine_nop().then_inc(memn_made, 1)
                    dve.wait_ge(memh_made, k + 1)
                    v.tensor_tensor(memn_lo[:, k, :], memn_f[:, k, :], memn_hi[:, k, :].bitcast(F32), ALU.subtract)\
                        .then_inc(meml_made, 1)
                for _ in range(12):
                    next_lo()
                for u in range(4 * X_HEADS):
                    b = u % 2
                    dve.wait_ge(x_scored, u + 1)
                    link(v.tensor_reduce(smalls[:, 28:29], pair[2][:, b, 0:MEM], AX.X, ALU.max))
                    v.tensor_scalar(smalls[:, 24 + b:25 + b], smalls[:, 28:29], -X_SCALE, None, ALU.mult)\
                        .then_inc(x_max, 1)
                    dve.wait_ge(x_exp, u + 1)
                    link(v.reciprocal(smalls[:, 30:31], smalls[:, 26 + b:27 + b]))
                    v.tensor_scalar(p_x[b][:, :], p_x[b][:, :], smalls[:, 30:31], None, ALU.mult).then_inc(x_norm, 1)
                    if u % 4 == 3:
                        h = u // 4
                        dve.wait_ge(x_yh, h + 1)
                        v.tensor_tensor(yx_lo[:, 2 * h:2 * h + 2, :], pair[h % 2][:, :, :],
                                        yx_hi[:, 2 * h:2 * h + 2, :].bitcast(F32), ALU.subtract).then_inc(x_yl, 1)

            def out_dve():
                v = nc.vector
                for k in range(4):
                    dve.wait_ge(mgh_made, k + 1)
                    v.tensor_tensor(mg_lo[:, 2 * k:2 * k + 2, :], merged[:, 2 * k:2 * k + 2, :],
                                    mg_hi[:, 2 * k:2 * k + 2, :].bitcast(F32), ALU.subtract).then_inc(mgl_made, 1)
                for m in range(4):
                    done()
                    xs = xT[:, 2 * m:2 * m + 2, :]
                    v.tensor_tensor(xs, xs, pair[m % 2][:, :, :], ALU.add).then_inc(x_mixed, 1)
                    next_lo()

            lo_at(0, 0)
            lo_at(0, 1)
            norm_raw(n_ffn[0], "ffn1_norm")
            norm_lo(n_ffn[0])
            ffn_dve(ffn[0])
            if "A" in stages:
                bias_dve()
            if "M" in stages:
                norm_raw(n_mix, "mix_norm")
                norm_lo(n_mix)
                gates_dve()
                for h in range(M_HEADS):
                    head_dve(h)
                merge_dve(0, 0)
            if "A" in stages:
                attention_dve()
                merge_dve(1, 4)
            if "X" in stages:
                cross_dve()
                merge_dve(2, 8)
            if "M" in stages:
                out_dve()
            if "ffn2" in stages:
                norm_raw(n_ffn[1], "ffn2_norm")
                norm_lo(n_ffn[1])
                ffn_dve(ffn[1])
            norm_raw(n_fin, "final_norm")
            for tt in range(NT):
                dve.wait_ge(out_turned, 2 * tt + 1)
                nc.vector.tensor_copy(o_tok[:, tt, 0:S], pair[2 + tt % 2][:, 0, :]).then_inc(out_lo_made, 1)

        @block.tensor
        def _(pe):
            q = Progress()
            pe.wait_ge(consts_made, 4)
            pe.wait_ge(prm_loaded, 160)
            nc.tensor.transpose(pair[3][:, 0, 0:104], prm1[:, :], ident[0:104, 0:104])
            nc.tensor.transpose(pair[3][:, 0, 128:192], prm2[:, :], ident[0:64, 0:64]).then_inc(par_turned, 1)
            pe.wait_ge(x_loaded, 16)
            for k in range(KD):
                if k >= 4:
                    pe.wait_ge(xt_made, k - 3)
                for a in range(NT):
                    last = nc.tensor.transpose(pair[(k // 2) % 2][:, k % 2, a * P:(a + 1) * P],
                                               x_tok[:, a, k * P:(k + 1) * P], ident[:, :])
                last.then_inc(xt_turned, 1)

            def norm_sum(s):
                for k in range(KD):
                    if k % 2 == 0:
                        pe.wait_ge(s.sq_made, k // 2 + 1)
                    last = nc.tensor.matmul(pair[3][:, 0, :], ones[:, :], sq[:, k, :], start=(k == 0),
                                            stop=(k == KD - 1))
                last.then_inc(s.sum_ready, 1)

            def product(out, w_h, w_l, x_h, x_l, first, last):
                nc.tensor.matmul(out, w_h, x_h, start=first, stop=False)
                nc.tensor.matmul(out, w_h, x_l, start=False, stop=False)
                return nc.tensor.matmul(out, w_l, x_h, start=False, stop=last)

            def narrow_block(slot, out, xs_hi, xs_lo, x0, kts, first, last):
                wh = w_hi[slot][:, 0:kts * COLS].rearrange("p (k c) -> p k c", c=COLS)
                wl = w_lo[slot][:, 0:kts * COLS].rearrange("p (k c) -> p k c", c=COLS)
                for j in range(2):
                    for k in range(kts):
                        mm = product(out[:, j, :], wh[:, k, j * P:(j + 1) * P], wl[:, k, j * P:(j + 1) * P],
                                     xs_hi[:, x0 + k, :], xs_lo[:, x0 + k, :],
                                     first and k == 0, last and k == kts - 1)
                mm.then_inc(block_done, 1)

            def ffn_pe(s, ready):
                b = q.block
                pe.wait_ge(ready, KD)
                for o in range(2):
                    pe.wait_ge(lo_made, b + o + 1)
                    narrow_block((b + o) % 2, pair[o], h_hi, h_lo, 0, KD, True, True)
                with pe.Fori(1, F // COLS) as i:
                    pe.wait_ge(lo_made, b + 1 + 2 * i)
                    pe.wait_ge(s.gate_made, i)
                    narrow_block(b % 2, pair[0], h_hi, h_lo, 0, KD, True, True)
                    pe.wait_ge(lo_made, b + 2 + 2 * i)
                    pe.wait_ge(s.act_made, i)
                    narrow_block((b + 1) % 2, pair[1], h_hi, h_lo, 0, KD, True, True)
                b = q.block = b + 2 * (F // COLS)
                for i in range(2):
                    for m in range(2):
                        for c, k0 in enumerate((0, 8, 16)):
                            o = 3 * m + c
                            kts = min(8, KF - k0)
                            pe.wait_ge(lo_made, b + o + 1 + 6 * i)
                            pe.wait_ge(s.act_ready, (k0 + kts) // 2)
                            if c == 0 and i:
                                pe.wait_ge(s.x_added, m + 1)
                            narrow_block((b + o) % 2, pair[2 + m], act_hi, act_lo, k0, kts, c == 0, c == 2)
                q.block = b + 12

            def claim(bank):
                if q.reader[bank]:
                    pe.wait_ge(*q.reader[bank])

            def claim_pair(k, sem_, value):
                claim(2 * k)
                claim(2 * k + 1)
                q.reader[2 * k] = q.reader[2 * k + 1] = (sem_, value)

            def next_narrow(k, xs_hi, xs_lo, reader, kts=KD, cols=None):
                claim_pair(k, *reader)
                pe.wait_ge(lo_made, q.block + 1)
                out = pair[k] if cols is None else pair[k][:, :, 0:cols]
                narrow_block(q.block % 2, out, xs_hi, xs_lo, 0, kts, True, True)
                q.block += 1

            def wide_slot():
                pe.wait_ge(lo_made, q.block + 1)
                b = q.block % 2
                q.block += 1
                return (w_hi[b][:, :].rearrange("p (k c) -> p k c", c=WIDE),
                        w_lo[b][:, :].rearrange("p (k c) -> p k c", c=WIDE))

            def wide_features(k, xs_hi, xs_lo):
                wh, wl = wide_slot()
                for m in range(4):
                    for kt in range(4):
                        mm = product(pair[k + m // 2][:, m % 2, :], wh[:, kt, m * P:(m + 1) * P],
                                     wl[:, kt, m * P:(m + 1) * P], xs_hi[:, kt, :], xs_lo[:, kt, :],
                                     kt == 0, kt == 3)
                mm.then_inc(block_done, 1)

            def wide_tokens(k, xs_hi, xs_lo, x0, tiles, first, last):
                wh, wl = wide_slot()
                for a in range(tiles):
                    out = pair[k + a // 2][:, a % 2, :]
                    for kt in range(4):
                        xh = xs_hi[:, x0 + kt, a * P:(a + 1) * P]
                        nc.tensor.matmul(out, xh, wh[:, kt, :], start=first and kt == 0, stop=False)
                        nc.tensor.matmul(out, xh, wl[:, kt, :], start=False, stop=False)
                        mm = nc.tensor.matmul(out, xs_lo[:, x0 + kt, a * P:(a + 1) * P], wh[:, kt, :],
                                              start=False, stop=last and kt == 3)
                mm.then_inc(block_done, 1)

            def bias_pe():
                pe.wait_ge(pos_made, 2)
                nc.tensor.matmul(pair[2][:, 0, :], sign_row[:, :], pos_r[:, :], start=True, stop=True)\
                    .then_inc(pos_spread, 1)
                for i in range(S // QSTEP):
                    pe.wait_ge(past_made, i + 1)
                    if i >= 2:
                        pe.wait_ge(bias_made, i - 1)
                    for j in range(4):
                        for part in range(3):
                            mm = nc.tensor.matmul(pair[i % 2][j * 32:(j + 1) * 32, 0, :], step_b[part][:, :],
                                                  past[i % 2][:, 4 * j:4 * j + 4, :].rearrange("p q c -> p (q c)"),
                                                  start=part == 0, stop=part == 2, tile_position=(0, 32 * j))
                    mm.then_inc(bias_summed, 1)
                q.reader[0] = (bias_made, S // QSTEP)
                q.reader[2] = (bias_made, S // QSTEP)

            def gates_pe():
                claim_pair(0, g_pre, 1)
                pe.wait_ge(n_mix.ready, KD)
                pe.wait_ge(lo_made, q.block + 1)
                b = q.block % 2
                wh = w_hi[b][:, :].rearrange("p (k c) -> p k c", c=COLS)
                wl = w_lo[b][:, :].rearrange("p (k c) -> p k c", c=COLS)
                for j in range(2):
                    c0 = j * M_HEADS
                    for k in range(KD):
                        mm = product(pair[0][:, j, :], wh[:, k, c0:c0 + P], wl[:, k, c0:c0 + P],
                                     h_hi[:, k, :], h_lo[:, k, :], k == 0, k == KD - 1)
                mm.then_inc(block_done, 1)
                q.block += 1
                claim_pair(1, g_ready, 1)
                pe.wait_ge(g_diag, 1)
                nc.tensor.matmul(pair[1][:, 1, 0:8], ones[0:M_HEADS, :],
                                 dec_diag[:, :, :].rearrange("p c h -> p (c h)"), start=True, stop=True)
                pe.wait_ge(g_exp, 2)
                for a in range(4):
                    for c in range(CHUNKS):
                        col = (a * CHUNKS + c) * M_HEADS
                        mm = nc.tensor.transpose(pair[1][:, 0, col:col + M_HEADS],
                                                 g_rows[:, a, c * P:(c + 1) * P], ident[0:M_HEADS, 0:M_HEADS])
                mm.then_inc(g_turned, 1)

            def head_pe(h):
                for m in range(2):
                    next_narrow(m, h_hi, h_lo, (xmh_made, 2 * h + m + 1))
                pe.wait_ge(xcl_made, h + 1)
                for k in range(2):
                    claim_pair(2 + k, q_made, 2 * h + k + 1)
                wide_features(2, xc_hi, xc_lo)
                for k in range(2):
                    claim_pair(k, k_made, 2 * h + k + 1)
                wide_features(0, xc_hi, xc_lo)
                pe.wait_ge(xml_made, 2 * h + 2)
                for k in range(2):
                    claim_pair(2 + k, v_made, 2 * h + k + 1)
                wide_tokens(2, xm_hi, xm_lo, 0, NT, True, True)
                for m in range(2):
                    next_narrow(m, h_hi, h_lo, (o_made, 2 * h + m + 1))
                claim(6)
                if h == 0:
                    pe.wait_ge(consts_made, 8)
                nc.tensor.matmul(pair[3][:, 0, :], sel[:, h, :], g_neg[:, :], start=True, stop=True)\
                    .then_inc(negm_spread, 1)
                for bank in range(6):
                    claim(bank)
                for c in range(CHUNKS):
                    g = CHUNKS * h + c
                    cs = slice(c * P, (c + 1) * P)
                    if c > 0:
                        pe.wait_ge(sw_made, g)
                    for k in range(MK):
                        mm = nc.tensor.matmul(pair[2][:, 0, 0:P], k_f[:, k, cs], q_f[:, k, cs], start=k == 0,
                                              stop=k == MK - 1)
                    mm.then_inc(sc_ready, 1)
                    if c < CHUNKS - 1:
                        if c > 0:
                            pe.wait_ge(kws_made, 3 * h + c)
                        for k in range(MK):
                            mm = nc.tensor.transpose(pair[2][:, 1, k * P:(k + 1) * P], k_f[:, k, cs], ident[:, :])
                        mm.then_inc(kt_ready, 1)
                    if c > 0:
                        pe.wait_ge(h_part, g)
                        if c > 1:
                            pe.wait_ge(h_made, 3 * h + c - 1)
                        pe.wait_ge(c_made, 2 * (3 * h + c))
                        for k in range(MK):
                            nc.tensor.matmul(pair[0][:, 1, :], q_f[:, k, cs], c_st[:, k, :], start=k == 0,
                                             stop=k == MK - 1)
                        for k in range(MK):
                            nc.tensor.matmul(pair[1][:, 0, 1:2], q_f[:, k, cs], n_st[:, k:k + 1], start=k == 0,
                                             stop=k == MK - 1)
                    pe.wait_ge(sw_made, g + 1)
                    nc.tensor.matmul(pair[1][:, 0, 0:1], s_w[:, :], ones[:, 0:1], start=True, stop=True)
                    nc.tensor.matmul(pair[0][:, 0, :], s_w[:, :], v_f[:, c, :], start=True, stop=True)\
                        .then_inc(num_ready, 1)
                    if c < CHUNKS - 1:
                        pe.wait_ge(kws_made, 3 * h + c + 1)
                        if c == 0:
                            pe.wait_ge(w_arg, h + 1)
                        for half in range(2):
                            if 2 * c + half >= 1:
                                pe.wait_ge(c_made, 2 * (3 * h + c) + half)
                            for j in range(2):
                                ks = slice((2 * half + j) * P, (2 * half + j + 1) * P)
                                nc.tensor.matmul(pair[1][:, 1, 2 * half + j:2 * half + j + 1], k_ws[:, ks],
                                                 ones[:, 0:1], start=True, stop=True)
                                mm = nc.tensor.matmul(pair[3][:, j, :], k_ws[:, ks], v_f[:, c, :], start=True,
                                                      stop=True)
                            mm.then_inc(upd_ready, 1)
                pe.wait_ge(c_made, 6 * (h + 1))
                for e in range(MK):
                    if e == 0:
                        pe.wait_ge(hn_made, CHUNKS * (h + 1))
                    for c in range(CHUNKS):
                        mm = nc.tensor.transpose(pair[2 + e // 2][:, e % 2, c * P:(c + 1) * P],
                                                 h_m[:, c, e * P:(e + 1) * P], ident[:, :])
                    mm.then_inc(h_turned, 1)
                pe.wait_ge(yml_made, MK * (h + 1))
                for bank in range(8):
                    q.reader[bank] = None
                for m in range(2):
                    for k in range(2):
                        claim_pair(2 * m + k, bm_added, 4 * h + 2 * m + k + 1)
                    wide_features(2 * m, ym_hi, ym_lo)

            def merge_pe(gate, base, xs_hi, xs_lo):
                for m in range(4):
                    next_narrow(2 * (m % 2), h_hi, h_lo, (g_sig_made, base + m + 1))
                    if gate:
                        next_narrow(2 * (m % 2) + 1, xs_hi, xs_lo, (mg_made, base + m + 1))

            def attention_pe():
                for nh in range(2):
                    for k in range(2):
                        claim_pair(2 * nh + k, va_made, 2 * nh + k + 1)
                    wide_tokens(2 * nh, h_hi, h_lo, 0, NT, True, False)
                    wide_tokens(2 * nh, h_hi, h_lo, 4, NT, False, True)
                pe.wait_ge(lam_loaded, 64)
                claim(7)
                for j in range(2):
                    lq = smalls[0:A_QK, 32 + 2 * j:33 + 2 * j]
                    mm = nc.tensor.matmul(pair[3][:, 1, j:j + 1], lq.to_broadcast([A_QK, P]),
                                          smalls[0:A_QK, 33 + 2 * j:34 + 2 * j], start=True, stop=True)
                mm.then_inc(lam_summed, 1)
                q.reader[7] = (g_exp, 3)

                def scores(u):
                    hh, qt = (u // 4) % 2, u % 4
                    b = u % 2
                    if u < 2:
                        claim(4 + 2 * b)
                        claim(5 + 2 * b)
                    else:
                        pe.wait_ge(a_shifted, 2 * (u - 2) + 2)
                    for j in range(2):
                        r = slice(j * A_QK, (j + 1) * A_QK)
                        mm = nc.tensor.matmul(pair[2 + b][:, j, :], q_a[r, hh, qt * P:(qt + 1) * P],
                                              k_a[r, hh, :], start=True, stop=True)
                    mm.then_inc(a_scored, 1)

                for hp in range(4):
                    next_narrow(0, h_hi, h_lo, (qa_made, hp + 1))
                    next_narrow(1, h_hi, h_lo, (ka_made, hp + 1))
                    pe.wait_ge(qa_made, hp + 1)
                    pe.wait_ge(ka_made, hp + 1)
                    scores(8 * hp)
                    for u in range(8 * hp, 8 * hp + 8):
                        if u < 8 * hp + 7:
                            scores(u + 1)
                        pe.wait_ge(a_mixed, u + 1)
                        if u >= 2:
                            pe.wait_ge(a_tr_made, u - 1)
                        for k in range(NT):
                            mm = nc.tensor.transpose(pair[0][:, u % 2, k * P:(k + 1) * P],
                                                     a_mix[u % 2][:, k * P:(k + 1) * P], ident[:, :])
                        mm.then_inc(a_turned, 1)
                        if u % 4 == 3:
                            e = u // 4
                            pe.wait_ge(a_tr_made, u + 1)
                            if e:
                                pe.wait_ge(a_sq, e)
                            for k in range(NT):
                                mm = nc.tensor.matmul(pair[1][:, 0, :], va[:, k, e * P:(e + 1) * P], a_tr[:, k, :],
                                                      start=k == 0, stop=k == NT - 1)
                            mm.then_inc(a_out, 1)
                            pe.wait_ge(a_sq, e + 1)
                            if e:
                                pe.wait_ge(a_r, e)
                            nc.tensor.matmul(pair[1][:, 1, :], ones[:, :], o_sq[:, :], start=True, stop=True)\
                                .then_inc(a_sum, 1)
                    q.reader[0] = q.reader[1] = (a_tr_made, 8 * hp + 8)
                    q.reader[2] = q.reader[3] = (a_r, 2 * hp + 2)
                q.reader[4] = q.reader[5] = q.reader[6] = q.reader[7] = (a_shifted, 64)
                pe.wait_ge(a_yl, A_HEADS)

            def cross_pe():
                claim(0)
                claim(1)
                pe.wait_ge(mem_r, MT)
                for k in range(KD):
                    if k >= 2:
                        pe.wait_ge(memn_made, k - 1)
                    for a in range(MT):
                        mm = nc.tensor.transpose(pair[0][:, k % 2, a * P:(a + 1) * P],
                                                 mem_tok[:, a, k * P:(k + 1) * P], ident[:, :])
                    mm.then_inc(mem_turned, 1)
                q.reader[0] = q.reader[1] = (memn_made, KD)
                pe.wait_ge(meml_made, KD)
                for m in range(4):
                    next_narrow(m % 2, memn_hi, memn_lo, (kx_made, m + 1), cols=MEM)
                for nh in range(2):
                    claim_pair(2 + nh, vx_made, nh + 1)
                    wide_tokens(2 + nh, memn_hi, memn_lo, 0, MT, True, False)
                    wide_tokens(2 + nh, memn_hi, memn_lo, 4, MT, False, True)
                for m in range(4):
                    next_narrow(m % 2, h_hi, h_lo, (qx_made, m + 1))

                def scores(u):
                    h, qt = u // 4, u % 4
                    if u < 2:
                        claim(4 + u)
                        claim(6 + u)
                        pe.wait_ge(qx_made, 4)
                    else:
                        pe.wait_ge(x_exp, u - 1)
                    for k in range(2):
                        mm = nc.tensor.matmul(pair[2][:, u % 2, 0:MEM], q_x[:, 2 * h + k, qt * P:(qt + 1) * P],
                                              k_x[:, 2 * h + k, :], start=k == 0, stop=k == 1)
                    mm.then_inc(x_scored, 1)

                scores(0)
                for u in range(4 * X_HEADS):
                    if u + 1 < 4 * X_HEADS:
                        scores(u + 1)
                    pe.wait_ge(x_norm, u + 1)
                    if u >= 2:
                        pe.wait_ge(x_tr_made, u - 1)
                    for a in range(MT):
                        mm = nc.tensor.transpose(pair[3][:, u % 2, a * P:(a + 1) * P],
                                                 p_x[u % 2][:, a * P:(a + 1) * P], ident[:, :])
                    mm.then_inc(x_turned, 1)
                    if u % 4 == 3:
                        h = u // 4
                        pe.wait_ge(x_tr_made, u + 1)
                        claim_pair(h % 2, x_yl, h + 1)
                        for j in range(2):
                            for a in range(MT):
                                mm = nc.tensor.matmul(pair[h % 2][:, j, :], v_x[:, a, (2 * h + j) * P:(2 * h + j + 1) * P],
                                                      p_tr[:, a, :], start=a == 0, stop=a == MT - 1)
                        mm.then_inc(x_out, 1)
                q.reader[4] = q.reader[5] = (x_exp, 4 * X_HEADS)
                q.reader[6] = q.reader[7] = (x_tr_made, 4 * X_HEADS)
                pe.wait_ge(x_yl, X_HEADS)

            def out_pe():
                pe.wait_ge(mgl_made, 4)
                for m in range(4):
                    next_narrow(m % 2, mg_hi, mg_lo, (x_mixed, m + 1))

            norm_sum(n_ffn[0])
            ffn_pe(ffn[0], n_ffn[0].ready)
            if "A" in stages:
                bias_pe()
            if "M" in stages:
                norm_sum(n_mix)
                gates_pe()
                for h in range(M_HEADS):
                    head_pe(h)
                merge_pe(0, 0, None, None)
            if "A" in stages:
                attention_pe()
                merge_pe(1, 4, ya_hi, ya_lo)
            if "X" in stages:
                cross_pe()
                merge_pe(2, 8, yx_hi, yx_lo)
            if "M" in stages:
                out_pe()
            if "ffn2" in stages:
                norm_sum(n_ffn[1])
                ffn_pe(ffn[1], n_ffn[1].ready)
            norm_sum(n_fin)
            for a in range(NT):
                for half in range(2):
                    pe.wait_ge(n_fin.raw_made, 4 * half + 4)
                    if a >= 2:
                        pe.wait_ge(out_hi_made if half else out_lo_made, a - 1)
                    for k in range(4 * half, 4 * half + 4):
                        last = nc.tensor.transpose(pair[2 + a % 2][:, half, (k % 4) * P:(k % 4 + 1) * P],
                                                   sq[:, k, a * P:(a + 1) * P], ident[:, :])
                    last.then_inc(out_turned, 1)


_INS = ["x", "mem", "positions", "rel_bias", "ffn1_norm", "ffn1_w_gu", "ffn1_w_down", "mix_norm", "mem_norm",
        "w_in", "b_if", "b_gate", "m_conv_w", "m_conv_b", "m_wq", "m_wk", "m_wv", "m_head_norm",
        "a_lam_q1", "a_lam_k1", "a_lam_q2", "a_lam_k2", "a_head_norm", "w_mem_kv", "w_branch_m",
        "w_branch_a", "w_branch_x", "w_out", "ffn2_norm", "ffn2_w_gu", "ffn2_w_down", "final_norm"]
_STAGES = ("M", "A", "X", "ffn2")


def _thresholds():
    n = np.arange(1, 256)
    large = 16 + (np.log(np.maximum(n, 1) / np.float32(16)) / np.log(128 / 16) * 16).astype(np.int32)
    bucket = np.where(n < 16, n, np.minimum(large, BUCKETS - 1))
    first = [0.5] + [float(n[np.argmax(bucket >= b)]) for b in range(1, BUCKETS)]
    return np.tile(np.array(first, np.float32), 4).reshape(P, 1)


def kernel(**inputs):
    import concourse.bacc as _bacc
    from concourse import mybir as _mybir
    from concourse.bass_utils import run_bass_kernel_spmd as _run

    nc = _bacc.Bacc("TRN2", target_bir_lowering=False, num_devices=1)
    arrays, t = {}, {}
    inputs["thresholds"] = _thresholds()
    for name in _INS + ["thresholds"]:
        a = np.ascontiguousarray(inputs[name])
        if a.ndim > 1 and a.shape[0] == 1:
            a = a.reshape(a.shape[1:])
        arrays[f"in_{name}"] = a
        t[name] = nc.dram_tensor(f"in_{name}", a.shape, _mybir.dt.from_np(a.dtype), kind="ExternalInput").ap()
    out = nc.dram_tensor("out", (S, D), F32, kind="ExternalOutput")
    t["out"] = out.ap()
    build(nc, t, _STAGES)
    r = _run(nc, [arrays], core_ids=[0])
    return r.results[0]["out"].reshape(1, S, D)
```

```python
from contextlib import ExitStack

import numpy as np

import concourse.bass as bass
from concourse import mybir

F32 = mybir.dt.float32
F32R = mybir.dt.float32r
BF16 = mybir.dt.bfloat16
I32 = mybir.dt.int32
ALU = mybir.AluOpType
ACT = mybir.ActivationFunctionType
AX = mybir.AxisListType

P = 128
S = 512
D = 1024
KD = D // P
NT = S // P
F = 2816
KF = F // P
COLS = 256
EPS = 1e-6
KB = 1024
MEM = 256
MT = MEM // P
M_HEADS = 4
M_HD = 2 * D // M_HEADS
MK = M_HD // P
CHUNKS = S // P
A_HEADS = 8
A_QK = 64
X_HEADS = 4
X_HD = D // X_HEADS
BUCKETS = 32
LAM_INIT = 0.2
A_SCALE = A_QK ** -0.5
X_SCALE = X_HD ** -0.5
HIDE = -1e30
KEYS4 = S // 4
QSTEP = 16
BSTEPS = S // QSTEP
C_XM, C_O, C_IF = 0, 2 * D, 4 * D
C_QA = C_IF + 2 * M_HEADS
C_KA, C_VA, C_QX, C_G = C_QA + D, C_QA + 2 * D, C_QA + 3 * D, C_QA + 4 * D
WIDE = 512
HEAD_BLOCKS = 9


class Progress:

    def __init__(self):
        self.block = 0
        self.reader = [None] * 8


def build(nc, t):
    ctx = ExitStack()
    with ctx:
        def sem(name):
            return ctx.enter_context(nc.semaphore(name))

        base = -(-nc.sbuf_base // 64) * 64

        def at(name, kb, shape, dtype=F32):
            return nc.alloc_sbuf_tensor_at(name, shape, dtype, offset=base + int(kb * KB))

        xT = at("xT", 0, [P, KD, S])
        w_raw = [at(f"w_raw{i}", 16 + 8 * i, [P, 2048]) for i in range(2)]
        w_hi = [at(f"w_hi{i}", 32 + 8 * i, [P, 2048], F32R) for i in range(2)]
        w_lo = [at(f"w_lo{i}", 48 + 8 * i, [P, 2048], F32R) for i in range(2)]
        h_hi = at("h_hi", 64, [P, KD, S], F32R)
        h_lo = at("h_lo", 80, [P, KD, S], F32R)
        merged = at("merged", 96, [P, KD, S])
        ident = at("ident", 112, [P, P])
        ones = at("ones", 112.5, [P, P])
        par = at("par", 113, [P, 176])
        eps_c = at("eps_c", 114, [P, 1])
        smalls = at("smalls", 114.0625, [P, 40])
        mask = at("mask", 114.25, [P, P])
        Z = 115
        sq = at("sq", Z, [P, KD, S])
        act_hi = at("act_hi", Z, [P, KF, S], F32R)
        act_lo = at("act_lo", Z + 44, [P, KF, S], F32R)
        gate_s = at("gate_s", 96, [P, 2, S])
        act_f = at("act_f", 100, [P, 2, S])
        sq_pair = [at(f"sq_pair{i}", 96 + 4 * i, [P, 2, S]) for i in range(2)]
        rinv = at("rinv", 104, [P, S])
        lnv = at("lnv", 106, [P, S])
        x_tok = at("x_tok", Z + 32, [P, NT, D])
        prm1 = at("prm1", Z + 48, [104, P])
        prm2 = at("prm2", Z + 49, [64, P])
        past = [at(f"past{i}", 104 + 4 * i, [P, QSTEP, KEYS4], BF16) for i in range(2)]
        bias_out = at("bias_out", Z + 88, [P, S])
        pq_s = at("pq_s", Z + 90, [P, S])
        pk_s = at("pk_s", Z + 92, [P, KEYS4])
        step_b = [at(f"step_b{i}", 114.75 + 0.0625 * i, [P, 32], BF16) for i in range(3)]
        rb_base = smalls[:, 36:37]
        rb_cur = at("rb_cur", Z + 64, [P, A_HEADS])
        rb_prev = at("rb_prev", Z + 64.0625, [P, A_HEADS])
        thr = at("thr", Z + 64.125, [P, 1])
        step_f = at("step_f", Z + 64.25, [P, 32])
        sign_row = at("sign_row", Z + 65, [1, P])
        pos_i = at("pos_i", Z + 66, [1, S], I32)
        pos_h = at("pos_h", Z + 68, [1, S], I32)
        pos_l = at("pos_l", Z + 70, [1, S], I32)
        pos_hf = at("pos_hf", Z + 72, [1, S])
        pos_lf = at("pos_lf", Z + 74, [1, S])
        pos_r = at("pos_r", Z + 76, [1, S])
        g_i = at("g_i", Z + 40.5, [M_HEADS, S])
        g_f = at("g_f", Z + 42.5, [M_HEADS, S])
        g_abs = at("g_abs", Z + 44.5, [M_HEADS, S])
        g_ln = at("g_ln", Z + 46.5, [M_HEADS, S])
        g_lf = at("g_lf", Z + 48.5, [M_HEADS, S])
        g_b = at("g_b", Z + 50.5, [M_HEADS, S])
        g_m = at("g_m", Z + 52.5, [M_HEADS, S])
        g_rows = at("g_rows", Z + 72.5, [M_HEADS, 4, S])
        one_row = at("one_row", Z + 54.5, [M_HEADS, S])
        g_neg = at("g_neg", Z + 87.5, [M_HEADS, S])
        tokp = at("tokp", Z + 89.5, [P, 4, CHUNKS, M_HEADS])
        m_small = at("m_small", Z + 89.75, [P, 64])
        sel = at("sel", Z + 90.25, [M_HEADS, M_HEADS, P])
        decay = m_small[:, 0:8]
        dec_row = at("dec_row", Z + 92.25, [M_HEADS, 2])
        dec_diag = at("dec_diag", Z + 92.3125, [M_HEADS, 2, M_HEADS])
        xm_f = at("xm_f", Z, [P, MK, S + 4])
        xm_hi = at("xm_hi", Z + 8.5, [P, MK, S], F32R)
        xm_lo = at("xm_lo", Z + 16.5, [P, MK, S], F32R)
        xc_hi = at("xc_hi", Z + 24.5, [P, MK, S], F32R)
        xc_lo = at("xc_lo", Z + 32.5, [P, MK, S], F32R)
        q_f = at("q_f", Z + 40.5, [P, MK, S])
        k_f = at("k_f", Z + 48.5, [P, MK, S])
        v_f = at("v_f", Z + 56.5, [P, CHUNKS, M_HD])
        conv = at("conv", Z + 64.5, [P, MK, S])
        k_ws = at("k_ws", Z + 32.5, [P, CHUNKS - 1, M_HD])
        c_st = at("c_st", Z + 24.5, [P, MK, M_HD])
        h_m = at("h_m", Z + 64.5, [P, CHUNKS, M_HD])
        o_sig = at("o_sig", Z + 72.5, [P, MK, S])
        w_in_tr = at("w_in_tr", Z + 80.5, [P, CHUNKS, P])
        s_w = at("s_w", Z + 82.5, [P, CHUNKS, P])
        y_f = [at(f"y_f{i}", Z + 80.5 + 2 * i, [P, S]) for i in range(2)]
        h_sq = at("h_sq", Z + 84.5, [P, S])
        ym_hi = at("ym_hi", Z + 40.5, [P, MK, S], F32R)
        ym_lo = at("ym_lo", Z + 48.5, [P, MK, S], F32R)
        n_st = m_small[:, 8:12]
        sumsq = m_small[:, 12:16]
        den = m_small[:, 16:32]
        va = at("va", Z, [P, NT, D])
        q_a = [at(f"q_a{i}", Z + 16 + 8 * i, [P, 2, S]) for i in range(2)]
        k_a = [at(f"k_a{i}", Z + 20 + 8 * i, [P, 2, S]) for i in range(2)]
        ya_hi = at("ya_hi", Z + 32, [P, KD, S], F32R)
        ya_lo = at("ya_lo", Z + 48, [P, KD, S], F32R)
        bias_sb = [at(f"bias_sb{i}", Z + 64 + 2 * i, [P, S]) for i in range(4)]
        probs = [at(f"probs{i}", Z + 72 + 4 * i, [P, 2, S]) for i in range(2)]
        o_sq = at("o_sq", Z + 80, [P, S])
        y_af = at("y_af", Z + 82, [P, S])
        a_tr = at("a_tr", Z + 84, [P, NT, S])
        g_sig = at("g_sig", Z + 84, [P, 2, S])
        g_tmp = at("g_tmp", Z + 88, [P, 2, S])
        memn_hi = at("memn_hi", Z, [P, KD, MEM], F32R)
        memn_lo = at("memn_lo", Z + 8, [P, KD, MEM], F32R)
        k_x = at("k_x", Z + 16, [P, KD, MEM])
        v_x = at("v_x", Z + 24, [P, MT, D])
        q_x = at("q_x", Z + 32, [P, KD, S])
        mem_tok = at("mem_tok", Z + 16, [P, MT, D])
        memn_f = at("memn_f", Z + 24, [P, KD, MEM])
        mem_sq = at("mem_sq", Z + 64, [P, D])
        yx_hi = at("yx_hi", Z + 48, [P, KD, S], F32R)
        yx_lo = at("yx_lo", Z + 64, [P, KD, S], F32R)
        p_tr = at("p_tr", Z + 80, [P, MT, S])
        p_x = [at(f"p_x{i}", Z + 88 + i, [P, MEM]) for i in range(2)]
        mg_hi = at("mg_hi", Z, [P, KD, S], F32R)
        mg_lo = at("mg_lo", Z + 16, [P, KD, S], F32R)
        bias_dram = nc.dram_tensor("bias_dram", [A_HEADS * 4, S, KEYS4], F32, kind="Internal").ap()
        o_tok = at("o_tok", Z + 32, [P, NT, D])

        pair = [ctx.enter_context(nc.psum_tensor(f"pair{i}", [P, 2, S], F32)) for i in range(4)]

        PC = {}
        col = 0
        for name, n in (("ffn1_norm", 8), ("mix_norm", 8), ("mem_norm", 8), ("ffn2_norm", 8),
                        ("final_norm", 8), ("m_head_norm", 16), ("a_head_norm", 8), ("m_conv_b", 16),
                        ("b_gate", 24), ("m_conv_w", 64)):
            PC[name] = (col, n)
            col += n

        def pcol(name, k):
            return par[:, PC[name][0] + k:PC[name][0] + k + 1]

        raw_loaded = [sem(f"raw_loaded{i}") for i in range(2)]
        hi_made = sem("hi_made")
        lo_made = sem("lo_made")
        block_done = sem("block_done")
        consts_made = sem("consts_made")
        prm_loaded = sem("prm_loaded")
        x_loaded = sem("x_loaded")
        par_turned = sem("par_turned")
        par_made = sem("par_made")
        xt_turned = sem("xt_turned")
        xt_made = sem("xt_made")
        out_turned = sem("out_turned")
        out_lo_made = sem("out_lo_made")
        out_hi_made = sem("out_hi_made")
        out_stored = sem("out_stored")

        chain_d = sem("chain_d")
        chain_a = sem("chain_a")
        thr_loaded = sem("thr_loaded")
        pos_loaded = sem("pos_loaded")
        pos_made = sem("pos_made")
        pos_spread = sem("pos_spread")
        past_made = sem("past_made")
        bias_summed = sem("bias_summed")
        bias_made = sem("bias_made")
        bias_stored = sem("bias_stored")
        bif_loaded = sem("bif_loaded")
        g_pre = sem("g_pre")
        g_exp = sem("g_exp")
        g_arg = sem("g_arg")
        g_w = sem("g_w")
        g_diag = sem("g_diag")
        g_turned = sem("g_turned")
        g_ready = sem("g_ready")
        xm_made = sem("xm_made")
        xmh_made = sem("xmh_made")
        xml_made = sem("xml_made")
        conv_made = sem("conv_made")
        xc_made = sem("xc_made")
        xcl_made = sem("xcl_made")
        q_made = sem("q_made")
        k_made = sem("k_made")
        v_made = sem("v_made")
        o_made = sem("o_made")
        negm_spread = sem("negm_spread")
        w_arg = sem("w_arg")
        w_made = sem("w_made")
        sc_ready = sem("sc_ready")
        kt_ready = sem("kt_ready")
        sw_made = sem("sw_made")
        kws_made = sem("kws_made")
        num_ready = sem("num_ready")
        upd_ready = sem("upd_ready")
        c_made = sem("c_made")
        r_made = sem("r_made")
        h_part = sem("h_part")
        h_made = sem("h_made")
        hn_made = sem("hn_made")
        h_turned = sem("h_turned")
        yf_made = sem("yf_made")
        ymh_made = sem("ymh_made")
        yml_made = sem("yml_made")
        bm_added = sem("bm_added")
        g_sig_made = sem("g_sig_made")
        mg_made = sem("mg_made")
        lam_loaded = sem("lam_loaded")
        lam_summed = sem("lam_summed")
        va_made = sem("va_made")
        qa_made = sem("qa_made")
        ka_made = sem("ka_made")
        bias_loaded = [sem(f"bias_loaded{i}") for i in range(4)]
        a_scored = sem("a_scored")
        a_shifted = sem("a_shifted")
        a_exp = sem("a_exp")
        a_mixed = sem("a_mixed")
        a_turned = sem("a_turned")
        a_tr_made = sem("a_tr_made")
        a_out = sem("a_out")
        a_sq = sem("a_sq")
        a_sum = sem("a_sum")
        a_r = sem("a_r")
        a_y = sem("a_y")
        a_yh = sem("a_yh")
        a_yl = sem("a_yl")
        mem_loaded = sem("mem_loaded")
        mem_sq_made = sem("mem_sq_made")
        mem_r = sem("mem_r")
        mem_turned = sem("mem_turned")
        memn_made = sem("memn_made")
        memh_made = sem("memh_made")
        meml_made = sem("meml_made")
        kx_made = sem("kx_made")
        vx_made = sem("vx_made")
        qx_made = sem("qx_made")
        x_scored = sem("x_scored")
        x_max = sem("x_max")
        x_exp = sem("x_exp")
        x_norm = sem("x_norm")
        x_turned = sem("x_turned")
        x_tr_made = sem("x_tr_made")
        x_out = sem("x_out")
        x_yh = sem("x_yh")
        x_yl = sem("x_yl")
        mgh_made = sem("mgh_made")
        mgl_made = sem("mgl_made")
        x_mixed = sem("x_mixed")

        class NormSems:
            def __init__(self, name):
                self.sq_made = sem(f"{name}_sq_made")
                self.summed = sem(f"{name}_summed")
                self.sum_ready = sem(f"{name}_sum_ready")
                self.ln_made = sem(f"{name}_ln_made")
                self.r_made = sem(f"{name}_r_made")
                self.raw_made = sem(f"{name}_raw_made")
                self.hi_made = sem(f"{name}_hi_made")
                self.ready = sem(f"{name}_ready")

        class FfnSems:
            def __init__(self, name):
                self.gate_made = sem(f"{name}_gate_made")
                self.act_made = sem(f"{name}_act_made")
                self.act_hi = sem(f"{name}_act_hi")
                self.act_ready = sem(f"{name}_act_ready")
                self.x_added = sem(f"{name}_x_added")

        n_ffn = [NormSems(f"n_ffn{i}") for i in range(2)]
        n_mix = NormSems("n_mix")
        n_fin = NormSems("n_fin")
        ffn = [FfnSems(f"ffn{i}") for i in range(2)]

        block = ctx.enter_context(nc.Block())

        KT_BANK = (5, 7, 6)
        DOWN_PAIR = (2, 0, 2, 0)
        A_FILL = (1, 1, 1, 1, 2, 1, 1, 0)
        QA_UNIT, KA_UNIT = 3, 6
        X_FILL = (2, 1, 1, 0)
        QX_UNIT = 2
        X_OUT_PAIR = (1, 0, 1, 1)
        TOTAL = 2 * 34 + 1 + HEAD_BLOCKS * M_HEADS + 4 + 4 + 20 + 20
        MERGES = 12

        def inter(c):
            return pair[0][:, 0, :] if c == CHUNKS - 1 else pair[2][:, 0, :]

        def narrow(w, k0, kts, c0):
            return w[k0 * P:(k0 + kts) * P, bass.ds(c0, COLS)].rearrange("(k p) c -> p k c", p=P)

        @block.sync
        def _(sp):
            q = Progress()

            def load(n, slot, src, kts=8, width=COLS, peeled=False):
                if not peeled:
                    sp.wait_ge(lo_made, n - 1)
                dst = w_raw[slot][:, 0:kts * width].rearrange("p (k c) -> p k c", c=width)
                sp.dma_start(dst, src).then_inc(raw_loaded[slot], 16)

            def load_next(src, kts=8, width=COLS):
                load(q.block, q.block % 2, src, kts, width)
                q.block += 1

            def ffn_loads(w_gu, w_down):
                b = q.block
                first = 0
                if b == 0:
                    load(0, 0, narrow(w_gu, 0, KD, 0), peeled=True)
                    load(1, 1, narrow(w_gu, 0, KD, F), peeled=True)
                    first = 1
                with sp.Fori(first, F // COLS) as i:
                    load(b + 2 * i, b % 2, narrow(w_gu, 0, KD, i * COLS))
                    load(b + 2 * i + 1, (b + 1) % 2, narrow(w_gu, 0, KD, F + i * COLS))
                q.block = b + 2 * (F // COLS)
                for m in range(4):
                    for k0 in (0, 8, 16):
                        load_next(narrow(w_down, k0, min(8, KF - k0), m * COLS), min(8, KF - k0))

            def wide(w, k0, c0):
                return w[k0 * P:(k0 + 4) * P, c0:c0 + WIDE].rearrange("(k p) c -> p k c", p=P)

            def branch_loads(w, gate):
                def gate_load(m):
                    load_next(narrow(t["w_in"], 0, KD, C_G + gate * D + m * COLS))

                gate_load(0)
                for m in range(4):
                    if m < 3:
                        gate_load(m + 1)
                    if w is not None:
                        load_next(narrow(w, 0, KD, m * COLS))

            ffn_loads(t["ffn1_w_gu"], t["ffn1_w_down"])
            load_next(narrow(t["w_in"], 0, KD, C_IF))

            def xm_load(h, m):
                load_next(narrow(t["w_in"], 0, KD, C_XM + h * M_HD + m * COLS))

            xm_load(0, 0)
            xm_load(0, 1)
            for h in range(M_HEADS):
                load_next(t["m_wv"][h].rearrange("(k p) c -> p k c", p=P), 4, WIDE)
                for m in range(2):
                    load_next(narrow(t["w_in"], 0, KD, C_O + h * M_HD + m * COLS))
                for w in ("m_wq", "m_wk"):
                    load_next(t[w][h].rearrange("(k p) c -> p k c", p=P), 4, WIDE)
                if h < M_HEADS - 1:
                    xm_load(h + 1, 0)
                    xm_load(h + 1, 1)
                for m in range(2):
                    load_next(wide(t["w_branch_m"], h * MK, m * WIDE), 4, WIDE)
            branch_loads(None, 0)
            for nh in range(2):
                for kh in range(2):
                    load_next(wide(t["w_in"], 4 * kh, C_VA + nh * WIDE), 4, WIDE)
            for hp in range(4):
                load_next(narrow(t["w_in"], 0, KD, C_QA + hp * COLS))
                load_next(narrow(t["w_in"], 0, KD, C_KA + hp * COLS))
            branch_loads(t["w_branch_a"], 1)
            for m in range(4):
                load_next(narrow(t["w_mem_kv"], 0, KD, m * COLS))
            for nh in range(2):
                for kh in range(2):
                    load_next(wide(t["w_mem_kv"], 4 * kh, D + nh * WIDE), 4, WIDE)
            for m in range(4):
                load_next(narrow(t["w_in"], 0, KD, C_QX + m * COLS))
            branch_loads(t["w_branch_x"], 2)
            for m in range(4):
                load_next(narrow(t["w_out"], 0, KD, m * COLS))
            ffn_loads(t["ffn2_w_gu"], t["ffn2_w_down"])
            for tt in range(NT):
                sp.wait_ge(out_lo_made, tt + 1)
                sp.wait_ge(out_hi_made, tt + 1)
                sp.dma_start(t["out"][tt * P:(tt + 1) * P, :], o_tok[:, tt, :]).then_inc(out_stored, 16)
            sp.wait_ge(out_stored, 16 * NT)

        @block.gpsimd
        def _(pool):
            pool.memset(ident[:, :], 0.0).then_inc(consts_made, 1)
            pool.memset(ones[:, :], 1.0).then_inc(consts_made, 1)
            pool.memset(eps_c[:, :], EPS).then_inc(consts_made, 1)
            pool.wait_ge(consts_made, 3)
            pool.affine_select(out=ident[:, :], in_=ident[:, :], compare_op=ALU.not_equal, fill=1.0,
                               base=0, pattern=[[-1, P]], channel_multiplier=1).then_inc(consts_made, 1)
            pool.memset(mask[:, :], 0.0).then_inc(consts_made, 1)
            pool.wait_ge(consts_made, 5)
            pool.affine_select(out=mask[:, :], in_=mask[:, :], compare_op=ALU.is_ge, fill=HIDE,
                               base=0, pattern=[[1, P]], channel_multiplier=-1).then_inc(consts_made, 1)
            pool.dma_start(pos_i[:, :], t["positions"].rearrange("(a s) -> a s", a=1)).then_inc(pos_loaded, 16)
            for j, name in enumerate(("a_lam_q1", "a_lam_k1", "a_lam_q2", "a_lam_k2")):
                pool.dma_start(smalls[0:A_QK, 32 + j:33 + j], t[name].rearrange("(p a) -> p a", a=1))\
                    .then_inc(lam_loaded, 16)
            pool.dma_start(thr[:, :], t["thresholds"]).then_inc(thr_loaded, 16)
            for k in range(4):
                pool.dma_start(rb_cur[k * BUCKETS:(k + 1) * BUCKETS, :], t["rel_bias"]).then_inc(thr_loaded, 16)
                pool.dma_start(rb_prev[k * BUCKETS:k * BUCKETS + 1, :], t["rel_bias"][0:1, :])\
                    .then_inc(thr_loaded, 16)
                pool.dma_start(rb_prev[k * BUCKETS + 1:(k + 1) * BUCKETS, :], t["rel_bias"][0:BUCKETS - 1, :])\
                    .then_inc(thr_loaded, 16)
            for j in range(4):
                for k in range(4):
                    pool.dma_start(rb_base[j * 32 + k:j * 32 + 32:4, :],
                                   t["rel_bias"][0:1, :].rearrange("a h -> h a")).then_inc(thr_loaded, 16)
            pool.wait_ge(ffn[0].x_added, 4)
            pool.memset(sel[:, :, :], 0.0).then_inc(consts_made, 1)
            pool.wait_ge(consts_made, 7)
            pool.affine_select(out=sel[:, :, :], in_=sel[:, :, :], compare_op=ALU.not_equal, fill=1.0,
                               base=0, pattern=[[-1, M_HEADS], [0, P]], channel_multiplier=1)\
                .then_inc(consts_made, 1)
            pool.wait_ge(bias_stored, 64 * BSTEPS)
            pool.wait_ge(mg_made, 4)
            for u in range(4 * A_HEADS):
                if u >= 4:
                    pool.wait_ge(a_shifted, 2 * (u - 4) + 2)
                head = bias_dram[u // 4 * 4:u // 4 * 4 + 4, (u % 4) * P:(u % 4 + 1) * P, :]
                pool.dma_start(bias_sb[u % 4][:, :].rearrange("p (k c) -> p k c", k=4),
                               head.rearrange("k q c -> q k c")).then_inc(bias_loaded[u % 4], 16)

        @block.scalar
        def _(act):
            q = Progress()
            act.dma_start(x_tok[:, :, :], t["x"].rearrange("(a p) d -> p a d", p=P)).then_inc(x_loaded, 16)
            for name in ("ffn1_norm", "mix_norm", "mem_norm", "ffn2_norm", "final_norm", "m_head_norm",
                         "a_head_norm", "m_conv_b", "b_gate"):
                r, n = PC[name]
                act.dma_start(prm1[r:r + n, :], t[name].rearrange("(k p) -> k p", p=P)).then_inc(prm_loaded, 16)
            act.dma_start(prm2[:, :], t["m_conv_w"].rearrange("j (k p) -> (j k) p", p=P)).then_inc(prm_loaded, 16)

            def hi_at(b, o, step=0, i=0):
                n, slot = b + o, (b + o) % 2
                act.wait_ge(raw_loaded[slot], 16 * (n // 2 + 1) + (8 * step) * i if step else 16 * (n // 2 + 1))
                if n >= 2:
                    act.wait_ge(block_done, (n - 1) + step * i if step else n - 1)
                nc.scalar.activation(w_hi[slot][:, :], w_raw[slot][:, :], ACT.Copy).then_inc(hi_made, 1)

            def norm_r(s):
                act.wait_ge(s.sum_ready, 1)
                nc.scalar.activation(lnv[:, :], pair[1][:, 0, :], ACT.Ln, bias=eps_c[:, 0:1],
                                     scale=1.0 / D).then_inc(s.ln_made, 1)
                act.wait_ge(s.ln_made, 1)
                nc.scalar.activation(rinv[:, :], lnv[:, :], ACT.Exp, scale=-0.5).then_inc(s.r_made, 1)

            def norm_hi(s):
                norm_r(s)
                for k in range(KD):
                    act.wait_ge(s.raw_made, k + 1)
                    nc.scalar.activation(h_hi[:, k, :], sq[:, k, :], ACT.Copy).then_inc(s.hi_made, 1)

            def square_pair(s, g, x_sem):
                act.wait_ge(x_sem, g + 1)
                if g >= 2:
                    act.wait_ge(s.summed, g - 1)
                nc.scalar.activation(sq_pair[g % 2][:, :, :], xT[:, 2 * g:2 * g + 2, :], ACT.Square)\
                    .then_inc(s.sq_made, 1)

            def bias_step(i):
                act.wait_ge(bias_summed, i + 1)
                if not isinstance(i, int) or i:
                    act.wait_ge(bias_stored, 64 * i)
                nc.scalar.activation(bias_out[:, :], pair[3][:, 0, :], ACT.Identity,
                                     bias=rb_base).then_inc(bias_made, 1)
                act.wait_ge(bias_made, i + 1)
                for j in range(4):
                    act.dma_start(bias_dram[:, bass.ds(i * QSTEP + 4 * j, 4), :],
                                  bias_out[j * 32:(j + 1) * 32, :].rearrange("p (q c) -> p q c", q=4))\
                        .then_inc(bias_stored, 16)

            def gate_up_act(s, b, i, bias):
                act.wait_ge(block_done, b + 1 + 2 * i)
                nc.scalar.activation(gate_s[:, :, :], pair[0][:, :, :], ACT.Silu).then_inc(s.gate_made, 1)
                hi_at(b, 2, 2, i)
                if bias:
                    bias_step(2 * i)
                act.wait_ge(s.act_made, i + 1)
                nc.scalar.activation(act_hi[:, bass.ds(2 * i, 2), :], act_f[:, :, :], ACT.Copy)\
                    .then_inc(s.act_hi, 1)
                hi_at(b, 3, 2, i)
                if bias:
                    bias_step(2 * i + 1)

            def ffn_act(s, n_next, bias=False):
                b = q.block
                gate_up_act(s, b, 0, bias)
                with act.Fori(1, F // COLS) as i:
                    gate_up_act(s, b, i, bias)
                q.block = b + 2 * (F // COLS)
                for g in range(4):
                    for c in range(3):
                        next_hi()
                        step = 22 + 3 * g + c
                        if bias and step < BSTEPS:
                            bias_step(step)
                    square_pair(n_next, g, s.x_added)

            def next_hi():
                if q.block + 2 < TOTAL:
                    hi_at(q.block + 2, 0)
                q.block += 1

            def done(k=0):
                act.wait_ge(block_done, q.block + 1 + k)

            chain = [0]

            def link(ins):
                chain[0] += 1
                ins.then_inc(chain_a, 1)
                act.wait_ge(chain_a, chain[0])

            def gates_act():
                for j in range(2):
                    act.dma_start(smalls[0:M_HEADS, j:j + 1],
                                  t["b_if"][j * M_HEADS:(j + 1) * M_HEADS].rearrange("(h a) -> h a", a=1))\
                        .then_inc(bif_loaded, 16)
                act.wait_ge(bif_loaded, 32)
                done()
                nc.scalar.activation(g_i[:, :], pair[0][0:M_HEADS, 0, :], ACT.Identity, bias=smalls[0:M_HEADS, 0:1])
                nc.scalar.activation(g_f[:, :], pair[0][0:M_HEADS, 1, :], ACT.Identity, bias=smalls[0:M_HEADS, 1:2])
                link(nc.scalar.activation(g_abs[:, :], pair[0][0:M_HEADS, 1, :], ACT.Abs, bias=smalls[0:M_HEADS, 1:2]))
                link(nc.scalar.activation(g_abs[:, :], g_abs[:, :], ACT.Exp, scale=-1.0))
                nc.scalar.activation(g_ln[:, :], g_abs[:, :], ACT.Ln, bias=ones[0:M_HEADS, 0:1]).then_inc(g_pre, 1)
                next_hi()
                act.wait_ge(g_arg, 1)
                nc.scalar.activation(dec_row[:, :], dec_row[:, :], ACT.Exp).then_inc(g_exp, 1)
                nc.scalar.activation(g_rows[:, 1:4, :], g_rows[:, 1:4, :], ACT.Exp).then_inc(g_exp, 1)

            def xm_act(h, m):
                done()
                nc.scalar.activation(xm_f[:, 2 * m:2 * m + 2, 3:3 + S], pair[m][:, :, :], ACT.Copy)\
                    .then_inc(xm_made, 1)
                nc.scalar.activation(xm_hi[:, 2 * m:2 * m + 2, :], pair[m][:, :, :], ACT.Copy).then_inc(xmh_made, 1)
                next_hi()

            def head_act(h):
                if h == 0:
                    xm_act(0, 0)
                    xm_act(0, 1)
                act.wait_ge(conv_made, h + 1)
                link(nc.scalar.activation(conv[:, :, :], conv[:, :, :], ACT.Silu))
                nc.scalar.activation(xc_hi[:, :, :], conv[:, :, :], ACT.Copy).then_inc(xc_made, 1)
                done()
                for j in range(2):
                    nc.scalar.activation(v_f[:, 2 * j:2 * j + 2, :], pair[2 + j][:, :, :], ACT.Copy).then_inc(v_made, 1)
                next_hi()
                for m in range(2):
                    done()
                    nc.scalar.activation(o_sig[:, 2 * m:2 * m + 2, :], pair[m][:, :, :], ACT.Sigmoid).then_inc(o_made, 1)
                    next_hi()
                done()
                for j in range(2):
                    nc.scalar.activation(q_f[:, 2 * j:2 * j + 2, :], pair[2 + j][:, :, :], ACT.Copy).then_inc(q_made, 1)
                next_hi()
                next_hi()
                act.wait_ge(w_arg, h + 1)
                nc.scalar.activation(w_in_tr[:, :, :], w_in_tr[:, :, :], ACT.Exp).then_inc(w_made, 1)
                for c in range(CHUNKS - 1):
                    act.wait_ge(kt_ready, 3 * h + c + 1)
                    nc.scalar.activation(k_ws[:, c, :], pair[KT_BANK[c] // 2][:, KT_BANK[c] % 2, :], ACT.Copy,
                                         scale=tokp[:, 3, c, h:h + 1]).then_inc(kws_made, 1)
                for c in range(CHUNKS):
                    g = CHUNKS * h + c
                    act.wait_ge(r_made, g + 1)
                    nc.scalar.activation(h_m[:, c, :], pair[2 + c % 2][:, 1, :], ACT.Copy,
                                         scale=den[:, 8 * (c % 2) + 4:8 * (c % 2) + 5]).then_inc(h_part, 1)
                    if c > 0:
                        act.wait_ge(h_made, 3 * h + c)
                    else:
                        act.wait_ge(h_part, g + 1)
                    link(nc.scalar.activation(h_sq[:, :], h_m[:, c, :], ACT.Square, accum_out=sumsq[:, c:c + 1]))
                link(nc.scalar.activation(sumsq, sumsq, ACT.Ln, bias=eps_c[:, 0:1], scale=1.0 / M_HD))
                link(nc.scalar.activation(sumsq, sumsq, ACT.Exp, scale=-0.5))
                for c in range(CHUNKS):
                    nc.scalar.activation(h_m[:, c, :], h_m[:, c, :], ACT.Copy, scale=sumsq[:, c:c + 1])\
                        .then_inc(hn_made, 1)
                if h < M_HEADS - 1:
                    xm_act(h + 1, 0)
                for e in range(MK):
                    act.wait_ge(yf_made, MK * h + e + 1)
                    nc.scalar.activation(ym_hi[:, e, :], y_f[e % 2][:, :], ACT.Copy).then_inc(ymh_made, 1)
                if h < M_HEADS - 1:
                    xm_act(h + 1, 1)
                next_hi()
                next_hi()

            def memory_act():
                for k in range(KD):
                    act.wait_ge(memn_made, k + 1)
                    nc.scalar.activation(memn_hi[:, k, :], memn_f[:, k, :], ACT.Copy).then_inc(memh_made, 1)

            def gate_sigmoid(gate, base, m):
                if base + m >= 1:
                    act.wait_ge(mg_made, base + m)
                for j in range(2):
                    ins = nc.scalar.activation(g_sig[:, j, :], pair[2 * (m % 2)][:, j, :], ACT.Sigmoid,
                                               bias=pcol("b_gate", 8 * gate + 2 * m + j))
                ins.then_inc(g_sig_made, 1)

            def merge_act(gate, base, split=False):
                if not gate:
                    for m in range(4):
                        done()
                        gate_sigmoid(gate, base, m)
                        next_hi()
                    return
                gate_sigmoid(gate, base, 0)
                for m in range(4):
                    if m < 3:
                        next_hi()
                    next_hi()
                    if m < 3:
                        gate_sigmoid(gate, base, m + 1)
                    if split:
                        act.wait_ge(mg_made, base + m + 1)
                        nc.scalar.activation(mg_hi[:, 2 * m:2 * m + 2, :], merged[:, 2 * m:2 * m + 2, :], ACT.Copy)\
                            .then_inc(mgh_made, 1)

            def attention_act():
                for nh in range(2):
                    next_hi()
                    done()
                    for j in range(2):
                        nc.scalar.activation(va[:, 2 * j:2 * j + 2, nh * WIDE:(nh + 1) * WIDE],
                                             pair[2 * nh + j][:, :, :], ACT.Copy).then_inc(va_made, 1)
                    next_hi()
                act.wait_ge(lam_summed, 1)
                nc.scalar.activation(smalls[:, 2:4], pair[3][:, 1, 0:2], ACT.Exp).then_inc(g_exp, 1)
                done()
                nc.scalar.activation(q_a[0][:, :, :], pair[0][:, :, :], ACT.Copy).then_inc(qa_made, 1)
                next_hi()
                next_hi()

                def exps(u):
                    b = u % 2
                    for j in range(2):
                        act.wait_ge(a_shifted, 2 * u + j + 1)
                        nc.scalar.activation(probs[b][:, j, :], probs[b][:, j, :], ACT.Exp,
                                             bias=smalls[:, 8 + 2 * b + j:9 + 2 * b + j], scale=A_SCALE,
                                             accum_out=smalls[:, 12 + 2 * b + j:13 + 2 * b + j]).then_inc(a_exp, 1)

                def head_square(e):
                    act.wait_ge(a_out, e + 1)
                    if e:
                        act.wait_ge(a_y, e)
                    nc.scalar.activation(o_sq[:, :], pair[1][:, 1, :], ACT.Square).then_inc(a_sq, 1)

                def head_rms(e):
                    act.wait_ge(a_sum, e + 1)
                    link(nc.scalar.activation(o_sq[:, :], pair[1][:, 0, :], ACT.Ln, bias=eps_c[:, 0:1],
                                              scale=1.0 / P))
                    nc.scalar.activation(o_sq[:, :], o_sq[:, :], ACT.Exp, scale=-0.5).then_inc(a_r, 1)

                def head_hi(e):
                    act.wait_ge(a_y, e + 1)
                    nc.scalar.activation(ya_hi[:, e, :], y_af[:, :], ACT.Copy).then_inc(a_yh, 1)

                exps(0)
                for u in range(4 * A_HEADS):
                    e, hp = u // 4 - 1, u // 8
                    if u + 1 < 4 * A_HEADS:
                        exps(u + 1)
                    if u % 4 == 0 and e >= 0:
                        head_square(e)
                    if u % 4 == 1 and e >= 0:
                        head_rms(e)
                    act.wait_ge(a_turned, u + 1)
                    nc.scalar.activation(a_tr[:, :, (u % 4) * P:(u % 4 + 1) * P],
                                         pair[1][:, 0, :].rearrange("p (k c) -> p k c", k=NT),
                                         ACT.Copy).then_inc(a_tr_made, 1)
                    if u % 4 == 1 and e >= 0:
                        head_hi(e)
                    if u % 8 == QA_UNIT:
                        done()
                        if hp < 3:
                            nc.scalar.activation(q_a[(hp + 1) % 2][:, :, :], pair[0][:, :, :], ACT.Copy)\
                                .then_inc(qa_made, 1)
                        next_hi()
                    if u % 8 == KA_UNIT and hp < 3:
                        next_hi()
                    if u == 24:
                        act.wait_ge(a_scored, 24)
                        act.dma_start(mem_tok[:, :, :], t["mem"].rearrange("(a p) d -> p a d", p=P))\
                            .then_inc(mem_loaded, 16)
                    if u == 30:
                        act.wait_ge(mem_loaded, 16)
                        for a in range(MT):
                            link(nc.scalar.activation(mem_sq[:, :], mem_tok[:, a, :], ACT.Square,
                                                      accum_out=smalls[:, 20 + a:21 + a]))
                        link(nc.scalar.activation(smalls[:, 20:22], smalls[:, 20:22], ACT.Ln, bias=eps_c[:, 0:1],
                                                  scale=1.0 / D))
                        link(nc.scalar.activation(smalls[:, 20:22], smalls[:, 20:22], ACT.Exp, scale=-0.5))
                        for a in range(MT):
                            nc.scalar.activation(mem_tok[:, a, :], mem_tok[:, a, :], ACT.Copy,
                                                 scale=smalls[:, 20 + a:21 + a]).then_inc(mem_r, 1)
                head_square(A_HEADS - 1)
                head_rms(A_HEADS - 1)
                head_hi(A_HEADS - 1)

            def cross_act():
                for m in range(4):
                    done()
                    nc.scalar.activation(k_x[:, 2 * m:2 * m + 2, :], pair[m % 2][:, :, 0:MEM], ACT.Copy)\
                        .then_inc(kx_made, 1)
                    next_hi()
                for nh in range(2):
                    next_hi()
                    done()
                    nc.scalar.activation(v_x[:, :, nh * WIDE:(nh + 1) * WIDE], pair[2 + nh][:, :, :], ACT.Copy)\
                        .then_inc(vx_made, 1)
                    next_hi()
                def qx_act(m):
                    done()
                    nc.scalar.activation(q_x[:, 2 * m:2 * m + 2, :], pair[m % 2][:, :, :], ACT.Copy)\
                        .then_inc(qx_made, 1)
                    next_hi()

                def exps(u):
                    act.wait_ge(x_max, u + 1)
                    nc.scalar.activation(p_x[u % 2][:, :], pair[2][:, u % 2, 0:MEM], ACT.Exp,
                                         bias=smalls[:, 24 + u % 2:25 + u % 2], scale=X_SCALE,
                                         accum_out=smalls[:, 26 + u % 2:27 + u % 2]).then_inc(x_exp, 1)

                def head_hi(h):
                    act.wait_ge(x_out, h + 1)
                    nc.scalar.activation(yx_hi[:, 2 * h:2 * h + 2, :], pair[X_OUT_PAIR[h]][:, :, :], ACT.Copy)\
                        .then_inc(x_yh, 1)

                qx_act(0)
                exps(0)
                for u in range(4 * X_HEADS):
                    h = u // 4
                    if u + 1 < 4 * X_HEADS:
                        exps(u + 1)
                    if u % 4 == 0 and u:
                        head_hi(h - 1)
                    act.wait_ge(x_turned, u + 1)
                    nc.scalar.activation(p_tr[:, :, (u % 4) * P:(u % 4 + 1) * P],
                                         pair[3][:, u % 2, 0:MEM].rearrange("p (k c) -> p k c", k=MT),
                                         ACT.Copy).then_inc(x_tr_made, 1)
                    if u % 4 == QX_UNIT:
                        if h < X_HEADS - 1:
                            qx_act(h + 1)
                        else:
                            next_hi()
                head_hi(X_HEADS - 1)

            def out_act():
                for m in range(4):
                    next_hi()
                    square_pair(n_ffn[1], m, x_mixed)

            hi_at(0, 0)
            hi_at(0, 1)
            for g in range(4):
                act.wait_ge(xt_made, 2 * g + 2)
                nc.scalar.activation(sq[:, 2 * g:2 * g + 2, :], xT[:, 2 * g:2 * g + 2, :], ACT.Square)\
                    .then_inc(n_ffn[0].sq_made, 1)
            norm_hi(n_ffn[0])
            act.wait_ge(thr_loaded, 16 * 29)
            act.wait_ge(pos_made, 1)
            ffn_act(ffn[0], n_mix, bias=True)
            norm_hi(n_mix)
            gates_act()
            for h in range(M_HEADS):
                head_act(h)
            merge_act(0, 0)
            attention_act()
            memory_act()
            merge_act(1, 4)
            cross_act()
            merge_act(2, 8, split=True)
            out_act()
            norm_hi(n_ffn[1])
            ffn_act(ffn[1], n_fin)
            norm_r(n_fin)
            for tt in range(NT):
                act.wait_ge(out_turned, 2 * tt + 2)
                nc.scalar.activation(o_tok[:, tt, S:2 * S], pair[2 + tt % 2][:, 1, :], ACT.Copy)\
                    .then_inc(out_hi_made, 1)

        @block.vector
        def _(dve):
            q = Progress()
            dve.wait_ge(par_turned, 1)
            nc.vector.tensor_copy(par[:, 0:104], pair[3][:, 0, 0:104])
            nc.vector.tensor_copy(par[:, 104:168], pair[3][:, 0, 128:192]).then_inc(par_made, 1)
            for k in range(KD):
                dve.wait_ge(xt_turned, k + 1)
                nc.vector.tensor_copy(xT[:, k, :], pair[2 * (k // 2 % 2)][:, k % 2, :]).then_inc(xt_made, 1)

            def lo_at(b, o, step=0, i=0):
                n, slot = b + o, (b + o) % 2
                dve.wait_ge(hi_made, (n + 1) + step * i if step else n + 1)
                nc.vector.tensor_tensor(w_lo[slot][:, :], w_raw[slot][:, :], w_hi[slot][:, :].bitcast(F32),
                                        ALU.subtract).then_inc(lo_made, 1)

            def norm_raw(s, gain, k):
                nc.vector.scalar_tensor_tensor(out=sq[:, k, :], in0=xT[:, k, :], scalar=pcol(gain, k),
                                               in1=rinv[:, :], op0=ALU.mult, op1=ALU.mult)\
                    .then_inc(s.raw_made, 1)

            def norm_split(s, gain):
                dve.wait_ge(s.r_made, 1)
                norm_raw(s, gain, 0)
                for k in range(KD):
                    if k + 1 < KD:
                        norm_raw(s, gain, k + 1)
                    dve.wait_ge(s.hi_made, k + 1)
                    nc.vector.tensor_tensor(h_lo[:, k, :], sq[:, k, :], h_hi[:, k, :].bitcast(F32),
                                            ALU.subtract).then_inc(s.ready, 1)

            def bias_step(i, slot):
                if not isinstance(i, int) or i >= 2:
                    dve.wait_ge(bias_summed, i - 1)
                nc.vector.tensor_tensor(past[slot][:, :, :],
                                        pq_s[:, bass.ds(i * QSTEP, QSTEP)].unsqueeze(2)
                                        .to_broadcast([P, QSTEP, KEYS4]),
                                        pk_s[:, :].unsqueeze(1).to_broadcast([P, QSTEP, KEYS4]),
                                        ALU.is_ge).then_inc(past_made, 1)

            def gate_up_dve(s, b, i, bias):
                lo_at(b, 2, 2, i)
                if bias:
                    bias_step(2 * i + 1, 1)
                dve.wait_ge(block_done, b + 2 + 2 * i)
                dve.wait_ge(s.gate_made, i + 1)
                nc.vector.tensor_tensor(act_f[:, :, :], gate_s[:, :, :], pair[1][:, :, :], ALU.mult)\
                    .then_inc(s.act_made, 1)
                dve.wait_ge(s.act_hi, i + 1)
                nc.vector.tensor_tensor(act_lo[:, bass.ds(2 * i, 2), :], act_f[:, :, :],
                                        act_hi[:, bass.ds(2 * i, 2), :].bitcast(F32), ALU.subtract)\
                    .then_inc(s.act_ready, 1)
                lo_at(b, 3, 2, i)
                if bias:
                    bias_step(2 * i + 2, 0)

            def ffn_dve(s, bias=False):
                b = q.block
                if bias:
                    bias_step(0, 0)
                gate_up_dve(s, b, 0, bias)
                with dve.Fori(1, F // COLS) as i:
                    gate_up_dve(s, b, i, bias)
                q.block = b + 2 * (F // COLS)
                for g in range(4):
                    for c in range(3):
                        if c == 2:
                            done()
                            xs = xT[:, 2 * g:2 * g + 2, :]
                            nc.vector.scalar_tensor_tensor(out=xs, in0=pair[DOWN_PAIR[g]][:, :, :], scalar=0.5,
                                                           in1=xs, op0=ALU.mult, op1=ALU.add)\
                                .then_inc(s.x_added, 1)
                        next_lo()
                        step = 23 + 3 * g + c
                        if bias and step < BSTEPS:
                            bias_step(step, step % 2)

            def next_lo():
                if q.block + 2 < TOTAL:
                    lo_at(q.block + 2, 0)
                q.block += 1

            def done(k=0):
                dve.wait_ge(block_done, q.block + 1 + k)

            chain = [0]

            def link(ins):
                chain[0] += 1
                ins.then_inc(chain_d, 1)
                dve.wait_ge(chain_d, chain[0])

            def bias_dve():
                v = nc.vector
                dve.wait_ge(thr_loaded, 16 * 29)
                link(v.tensor_tensor(rb_cur[:, :], rb_cur[:, :], rb_prev[:, :], ALU.subtract))
                link(v.tensor_scalar(rb_cur[:, :], rb_cur[:, :], 1.0 / A_SCALE, None, ALU.mult))
                for k in range(4):
                    link(v.memset(rb_cur[k * BUCKETS:k * BUCKETS + 1, :], HIDE))
                v.tensor_scalar(rb_base, rb_base, 1.0 / A_SCALE, None, ALU.mult).then_inc(pos_made, 1)
                link(v.memset(step_f[:, :], 0.0))
                for k in range(4):
                    ins = v.tensor_copy(step_f[k * BUCKETS:(k + 1) * BUCKETS, k:32:4],
                                        rb_cur[k * BUCKETS:(k + 1) * BUCKETS, :])
                link(ins)
                for part in range(3):
                    link(v.tensor_copy(step_b[part][:, :], step_f[:, :]))
                    if part < 2:
                        link(v.tensor_tensor(step_f[:, :], step_f[:, :], step_b[part][:, :], ALU.subtract))
                dve.wait_ge(pos_loaded, 16)
                v.tensor_scalar(pos_h[:, :], pos_i[:, :], 16, None, ALU.arith_shift_right)
                link(v.tensor_scalar(pos_l[:, :], pos_i[:, :], 65535, None, ALU.bitwise_and))
                v.tensor_copy(pos_hf[:, :], pos_h[:, :])
                link(v.tensor_copy(pos_lf[:, :], pos_l[:, :]))
                link(v.tensor_copy(smalls[0:1, 4:5], pos_hf[:, 0:1]))
                link(v.tensor_copy(smalls[0:1, 5:6], pos_lf[:, 0:1]))
                link(v.tensor_scalar(pos_hf[:, :], pos_hf[:, :], smalls[0:1, 4:5], None, ALU.subtract))
                link(v.tensor_scalar(pos_lf[:, :], pos_lf[:, :], smalls[0:1, 5:6], None, ALU.subtract))
                link(v.memset(sign_row[:, :], 1.0))
                link(v.memset(sign_row[:, 0:P:BUCKETS], -1.0))
                v.scalar_tensor_tensor(out=pos_r[:, :], in0=pos_hf[:, :], scalar=65536.0, in1=pos_lf[:, :],
                                       op0=ALU.mult, op1=ALU.add).then_inc(pos_made, 1)
                dve.wait_ge(pos_spread, 1)
                v.tensor_scalar(pq_s[:, :], pair[2][:, 0, :], thr[:, 0:1], None, ALU.subtract)
                for k in range(4):
                    r = slice(k * BUCKETS, (k + 1) * BUCKETS)
                    ins = v.tensor_copy(pk_s[r, :], pair[2][r, 0, k * KEYS4:(k + 1) * KEYS4])
                link(ins)

            def gates_dve():
                dve.wait_ge(bias_stored, 64 * BSTEPS)
                v = nc.vector
                link(v.memset(one_row[:, :], 1.0))
                dve.wait_ge(g_pre, 1)
                link(v.scalar_tensor_tensor(out=g_lf[:, :], in0=g_f[:, :], scalar=0.0, in1=g_ln[:, :],
                                            op0=ALU.min, op1=ALU.subtract))
                link(v.tensor_tensor_scan(g_b[:, :], one_row[:, :], g_lf[:, :], 0.0, ALU.mult, ALU.add))
                c_row = g_rows[:, 0, :]
                link(v.tensor_tensor(c_row, g_i[:, :], g_b[:, :], ALU.subtract))
                link(v.tensor_tensor_scan(g_m[:, :], c_row, c_row, 0.0, ALU.max, ALU.max))
                link(v.tensor_scalar(g_neg[:, :], g_m[:, :], -1.0, None, ALU.mult))
                v.memset(g_rows[:, 1, 0:P], 0.0)
                v.memset(g_rows[:, 3, S - P:S], 0.0)
                v.tensor_tensor(g_rows[:, 2, :], g_neg[:, :], g_b[:, :], ALU.subtract)
                for c in range(1, CHUNKS):
                    v.tensor_scalar(g_rows[:, 1, c * P:(c + 1) * P], g_neg[:, c * P:(c + 1) * P],
                                    g_m[:, c * P - 1:c * P], None, ALU.add)
                    v.tensor_scalar(g_rows[:, 3, (c - 1) * P:c * P], g_rows[:, 0, (c - 1) * P:c * P],
                                    g_m[:, c * P - 1:c * P], None, ALU.subtract)
                v.tensor_tensor(dec_row[:, :], g_m[:, P - 1:3 * P - 1:P], g_m[:, 2 * P - 1:4 * P - 1:P], ALU.subtract)\
                    .then_inc(g_arg, 1)
                next_lo()
                dve.wait_ge(g_exp, 1)
                for c in range(2):
                    ins = v.tensor_scalar(dec_diag[:, c, :], ident[0:M_HEADS, 0:M_HEADS], dec_row[:, c:c + 1], None,
                                          ALU.mult)
                ins.then_inc(g_diag, 1)
                link(v.memset(xm_f[:, :, 0:3], 0.0))

            def gates_turn_dve():
                dve.wait_ge(g_turned, 1)
                nc.vector.tensor_copy(decay, pair[1][:, 1, 0:8])
                nc.vector.tensor_copy(tokp[:, :, :, :].rearrange("p a c h -> p (a c h)"), pair[1][:, 0, 0:64])\
                    .then_inc(g_ready, 1)

            def xm_dve(h, m):
                dve.wait_ge(xmh_made, 2 * h + m + 1)
                nc.vector.tensor_tensor(xm_lo[:, 2 * m:2 * m + 2, :], xm_f[:, 2 * m:2 * m + 2, 3:3 + S],
                                        xm_hi[:, 2 * m:2 * m + 2, :].bitcast(F32), ALU.subtract)\
                    .then_inc(xml_made, 1)
                next_lo()

            def conv_tap(h, tap):
                v = nc.vector
                if tap != 3:
                    dve.wait_ge(chain_d, chain[0])
                for e in range(MK):
                    w = pcol("m_conv_w", 16 * tap + MK * h + e)
                    if tap == 3:
                        ins = v.tensor_scalar(conv[:, e, :], xm_f[:, e, 3:3 + S], w, pcol("m_conv_b", MK * h + e),
                                              ALU.mult, ALU.add)
                    else:
                        ins = v.scalar_tensor_tensor(out=conv[:, e, :], in0=xm_f[:, e, tap:tap + S], scalar=w,
                                                     in1=conv[:, e, :], op0=ALU.mult, op1=ALU.add)
                if tap == 2:
                    ins.then_inc(conv_made, 1)
                else:
                    chain[0] += 1
                    ins.then_inc(chain_d, 1)

            def head_dve(h):
                v = nc.vector
                if h == 0:
                    xm_dve(0, 0)
                    xm_dve(0, 1)
                    for tap in (3, 0, 1, 2):
                        conv_tap(0, tap)
                dve.wait_ge(xc_made, h + 1)
                v.tensor_tensor(xc_lo[:, :, :], conv[:, :, :], xc_hi[:, :, :].bitcast(F32), ALU.subtract)\
                    .then_inc(xcl_made, 1)
                if h == 0:
                    next_lo()
                    gates_turn_dve()
                for _ in range(3 if h == 0 else 4):
                    next_lo()
                done()
                for j in range(2):
                    v.tensor_scalar(k_f[:, 2 * j:2 * j + 2, :], pair[j][:, :, :], M_HD ** -0.5, None, ALU.mult)\
                        .then_inc(k_made, 1)
                next_lo()
                dve.wait_ge(negm_spread, h + 1)
                for c in range(CHUNKS):
                    ins = v.scalar_tensor_tensor(out=w_in_tr[:, c, :], in0=pair[3][:, 0, c * P:(c + 1) * P],
                                                 scalar=tokp[:, 0, c, h:h + 1], in1=mask[:, :],
                                                 op0=ALU.add, op1=ALU.add)
                ins.then_inc(w_arg, 1)
                dve.wait_ge(w_made, h + 1)
                dve.wait_ge(sc_ready, h + 1)
                v.tensor_tensor(s_w[:, :, :], pair[2][:, 0, :].rearrange("p (c t) -> p c t", c=CHUNKS),
                                w_in_tr[:, :, :], ALU.mult).then_inc(sw_made, 1)
                small = pair[3][:, 0, :]
                for c in range(CHUNKS):
                    g = CHUNKS * h + c
                    d = den[:, 8 * (c % 2):8 * (c % 2) + 8]
                    if c > 0:
                        dve.wait_ge(num_ready, g + 1)
                    if c < CHUNKS - 1:
                        for half in range(2):
                            dve.wait_ge(upd_ready, 2 * (3 * h + c) + half + 1)
                            cs = c_st[:, 2 * half:2 * half + 2, :]
                            dk = decay[:, (c - 1) * M_HEADS + h:(c - 1) * M_HEADS + h + 1] if c else None
                            if half:
                                if c == 0:
                                    v.tensor_copy(n_st, small[:, 0:MK])
                                else:
                                    v.scalar_tensor_tensor(out=n_st, in0=n_st, scalar=dk, in1=small[:, 0:MK],
                                                           op0=ALU.mult, op1=ALU.add)
                            if c == 0:
                                v.tensor_copy(cs, pair[half][:, :, :]).then_inc(c_made, 1)
                            else:
                                v.scalar_tensor_tensor(out=cs, in0=cs, scalar=dk, in1=pair[half][:, :, :],
                                                       op0=ALU.mult, op1=ALU.add).then_inc(c_made, 1)
                    if c == 0:
                        dve.wait_ge(num_ready, g + 1)
                        link(v.tensor_copy(d[:, 0:1], small[:, 4:5]))
                    else:
                        link(v.tensor_copy(d[:, 1:2], small[:, 4:5]))
                        link(v.scalar_tensor_tensor(out=d[:, 0:1], in0=small[:, 5:6],
                                                    scalar=tokp[:, 1, c, h:h + 1], in1=d[:, 1:2],
                                                    op0=ALU.mult, op1=ALU.add))
                    link(v.tensor_scalar(d[:, 3:4], d[:, 0:1], -1.0, tokp[:, 2, c, h:h + 1], ALU.mult, ALU.max))
                    link(v.tensor_tensor(d[:, 2:3], d[:, 0:1], d[:, 3:4], ALU.max))
                    v.reciprocal(d[:, 4:5], d[:, 2:3]).then_inc(r_made, 1)
                    if c > 0:
                        dve.wait_ge(r_made, g + 1)
                        link(v.tensor_tensor(d[:, 5:6], d[:, 4:5], tokp[:, 1, c, h:h + 1], ALU.mult))
                        dve.wait_ge(h_part, g + 1)
                        v.scalar_tensor_tensor(out=h_m[:, c, :], in0=inter(c), scalar=d[:, 5:6],
                                               in1=h_m[:, c, :], op0=ALU.mult, op1=ALU.add).then_inc(h_made, 1)
                if h < M_HEADS - 1:
                    xm_dve(h + 1, 0)
                for e in range(MK):
                    dve.wait_ge(h_turned, MK * h + e + 1)
                    if e >= 2:
                        dve.wait_ge(yml_made, MK * h + e - 1)
                    v.scalar_tensor_tensor(out=y_f[e % 2][:, :], in0=pair[2 + e // 2][:, e % 2, :],
                                           scalar=pcol("m_head_norm", MK * h + e), in1=o_sig[:, e, :],
                                           op0=ALU.mult, op1=ALU.mult).then_inc(yf_made, 1)
                    if e > 0:
                        y_lo(h, e - 1)
                y_lo(h, MK - 1)
                if h < M_HEADS - 1:
                    xm_dve(h + 1, 1)
                    conv_tap(h + 1, 3)
                    conv_tap(h + 1, 0)
                for m in range(2):
                    done()
                    for j in range(2):
                        ms = merged[:, 4 * m + 2 * j:4 * m + 2 * j + 2, :]
                        if h == 0:
                            ins = v.tensor_copy(ms, pair[2 * m + j][:, :, :])
                        else:
                            ins = v.tensor_tensor(ms, ms, pair[2 * m + j][:, :, :], ALU.add)
                        ins.then_inc(bm_added, 1)
                    next_lo()
                    if h < M_HEADS - 1:
                        conv_tap(h + 1, 1 + m)

            def y_lo(h, e):
                dve.wait_ge(ymh_made, MK * h + e + 1)
                nc.vector.tensor_tensor(ym_lo[:, e, :], y_f[e % 2][:, :], ym_hi[:, e, :].bitcast(F32), ALU.subtract)\
                    .then_inc(yml_made, 1)

            def merge_dve(gate, base, split=False):
                v = nc.vector
                for m in range(4):
                    ms = merged[:, 2 * m:2 * m + 2, :]
                    if gate == 0:
                        dve.wait_ge(g_sig_made, base + m + 1)
                        v.tensor_tensor(ms, ms, g_sig[:, :, :], ALU.mult).then_inc(mg_made, 1)
                        next_lo()
                        continue
                    if m < 3:
                        next_lo()
                    done()
                    dve.wait_ge(g_sig_made, base + m + 1)
                    link(v.tensor_tensor(g_tmp[:, :, :], g_sig[:, :, :], pair[2 * (m % 2) + 1][:, :, :], ALU.mult))
                    v.tensor_tensor(ms, ms, g_tmp[:, :, :], ALU.add).then_inc(mg_made, 1)
                    next_lo()
                    if split:
                        dve.wait_ge(mgh_made, m + 1)
                        v.tensor_tensor(mg_lo[:, 2 * m:2 * m + 2, :], ms,
                                        mg_hi[:, 2 * m:2 * m + 2, :].bitcast(F32), ALU.subtract).then_inc(mgl_made, 1)

            def attention_dve():
                v = nc.vector
                for _ in range(4):
                    next_lo()
                dve.wait_ge(g_exp, 3)
                link(v.tensor_tensor(smalls[:, 6:7], smalls[:, 3:4], smalls[:, 2:3], ALU.subtract))
                link(v.tensor_scalar(smalls[:, 6:7], smalls[:, 6:7], -LAM_INIT, None, ALU.add))
                g0 = PC["a_head_norm"][0]
                link(v.tensor_scalar(par[:, 168:176], par[:, g0:g0 + 8], 1.0 - LAM_INIT, None, ALU.mult))
                next_lo()
                done()
                v.tensor_copy(k_a[0][:, :, :], pair[1][:, :, :]).then_inc(ka_made, 1)
                next_lo()

                def shifts(u):
                    b = u % 2
                    dve.wait_ge(a_scored, u + 1)
                    dve.wait_ge(bias_loaded[u % 4], 16 * (u // 4 + 1))
                    if u >= 2:
                        dve.wait_ge(a_turned, u - 1)
                    for j in range(2):
                        top = smalls[:, 28 + 2 * b + j:29 + 2 * b + j]
                        link(v.tensor_tensor_reduce(probs[b][:, j, :], pair[2 + b][:, j, :], bias_sb[u % 4][:, :],
                                                    1.0, HIDE * 10, ALU.add, ALU.max, top))
                        v.tensor_scalar(smalls[:, 8 + 2 * b + j:9 + 2 * b + j], top, -A_SCALE, None, ALU.mult)\
                            .then_inc(a_shifted, 1)

                def head_y(e):
                    dve.wait_ge(a_r, e + 1)
                    if e:
                        dve.wait_ge(a_yl, e)
                    v.scalar_tensor_tensor(out=y_af[:, :], in0=pair[1][:, 1, :], scalar=par[:, 168 + e:169 + e],
                                           in1=o_sq[:, :], op0=ALU.mult, op1=ALU.mult).then_inc(a_y, 1)

                def head_lo(e):
                    dve.wait_ge(a_yh, e + 1)
                    v.tensor_tensor(ya_lo[:, e, :], y_af[:, :], ya_hi[:, e, :].bitcast(F32), ALU.subtract)\
                        .then_inc(a_yl, 1)

                shifts(0)
                for u in range(4 * A_HEADS):
                    b, e, hp = u % 2, u // 4 - 1, u // 8
                    if u + 1 < 4 * A_HEADS:
                        shifts(u + 1)
                    dve.wait_ge(a_exp, 2 * u + 2)
                    r = smalls[:, 16 + 2 * b:18 + 2 * b]
                    link(v.reciprocal(r, smalls[:, 12 + 2 * b:14 + 2 * b]))
                    link(v.tensor_tensor(r[:, 1:2], r[:, 1:2], smalls[:, 6:7], ALU.mult))
                    link(v.tensor_scalar(probs[b][:, 0, :], probs[b][:, 0, :], r[:, 0:1], None, ALU.mult))
                    v.scalar_tensor_tensor(out=probs[b][:, 0, :], in0=probs[b][:, 1, :], scalar=r[:, 1:2],
                                           in1=probs[b][:, 0, :], op0=ALU.mult, op1=ALU.add).then_inc(a_mixed, 1)
                    if u % 4 == 1 and e >= 0:
                        head_y(e)
                    if u % 4 == 2 and e >= 0:
                        head_lo(e)
                    if u % 8 == QA_UNIT:
                        next_lo()
                    if u % 8 == KA_UNIT and hp < 3:
                        done()
                        v.tensor_copy(k_a[(hp + 1) % 2][:, :, :], pair[0][:, :, :]).then_inc(ka_made, 1)
                        next_lo()
                for k in range(KD):
                    if k % 4 == 0:
                        dve.wait_ge(mem_turned, k // 4 + 1)
                    v.tensor_scalar(memn_f[:, k, :], pair[2 + k // 4][:, k // 2 % 2, k % 2 * MEM:(k % 2 + 1) * MEM],
                                    pcol("mem_norm", k), None, ALU.mult).then_inc(memn_made, 1)
                head_y(A_HEADS - 1)
                head_lo(A_HEADS - 1)
                for k in range(KD):
                    dve.wait_ge(memh_made, k + 1)
                    v.tensor_tensor(memn_lo[:, k, :], memn_f[:, k, :], memn_hi[:, k, :].bitcast(F32), ALU.subtract)\
                        .then_inc(meml_made, 1)

            def cross_dve():
                v = nc.vector
                for _ in range(9):
                    next_lo()

                def maxima(u):
                    b = u % 2
                    dve.wait_ge(x_scored, u + 1)
                    link(v.tensor_reduce(smalls[:, 28 + b:29 + b], pair[2][:, b, 0:MEM], AX.X, ALU.max))
                    v.tensor_scalar(smalls[:, 24 + b:25 + b], smalls[:, 28 + b:29 + b], -X_SCALE, None, ALU.mult)\
                        .then_inc(x_max, 1)

                def head_lo(h):
                    dve.wait_ge(x_yh, h + 1)
                    v.tensor_tensor(yx_lo[:, 2 * h:2 * h + 2, :], pair[X_OUT_PAIR[h]][:, :, :],
                                    yx_hi[:, 2 * h:2 * h + 2, :].bitcast(F32), ALU.subtract).then_inc(x_yl, 1)

                maxima(0)
                for u in range(4 * X_HEADS):
                    b = u % 2
                    if u + 1 < 4 * X_HEADS:
                        maxima(u + 1)
                    dve.wait_ge(x_exp, u + 1)
                    link(v.reciprocal(smalls[:, 30 + b:31 + b], smalls[:, 26 + b:27 + b]))
                    v.tensor_scalar(p_x[b][:, :], p_x[b][:, :], smalls[:, 30 + b:31 + b], None, ALU.mult).then_inc(x_norm, 1)
                    if u % 4 == QX_UNIT:
                        next_lo()
                    if u % 4 == 0 and u:
                        head_lo(u // 4 - 1)
                head_lo(X_HEADS - 1)

            def out_dve():
                v = nc.vector
                for m in range(4):
                    done()
                    xs = xT[:, 2 * m:2 * m + 2, :]
                    v.tensor_tensor(xs, xs, pair[2 + m % 2][:, :, :], ALU.add).then_inc(x_mixed, 1)
                    next_lo()

            lo_at(0, 0)
            lo_at(0, 1)
            norm_split(n_ffn[0], "ffn1_norm")
            bias_dve()
            ffn_dve(ffn[0], bias=True)
            norm_split(n_mix, "mix_norm")
            gates_dve()
            for h in range(M_HEADS):
                head_dve(h)
            merge_dve(0, 0)
            attention_dve()
            merge_dve(1, 4)
            cross_dve()
            merge_dve(2, 8, split=True)
            out_dve()
            norm_split(n_ffn[1], "ffn2_norm")
            ffn_dve(ffn[1])
            dve.wait_ge(n_fin.r_made, 1)
            for k in range(KD):
                norm_raw(n_fin, "final_norm", k)
            for tt in range(NT):
                dve.wait_ge(out_turned, 2 * tt + 1)
                nc.vector.tensor_copy(o_tok[:, tt, 0:S], pair[2 + tt % 2][:, 0, :]).then_inc(out_lo_made, 1)

        @block.tensor
        def _(pe):
            q = Progress()
            pe.wait_ge(consts_made, 4)
            pe.wait_ge(prm_loaded, 160)
            nc.tensor.transpose(pair[3][:, 0, 0:104], prm1[:, :], ident[0:104, 0:104])
            nc.tensor.transpose(pair[3][:, 0, 128:192], prm2[:, :], ident[0:64, 0:64]).then_inc(par_turned, 1)
            pe.wait_ge(x_loaded, 16)
            for k in range(KD):
                if k >= 4:
                    pe.wait_ge(xt_made, k - 3)
                for a in range(NT):
                    last = nc.tensor.transpose(pair[2 * (k // 2 % 2)][:, k % 2, a * P:(a + 1) * P],
                                               x_tok[:, a, k * P:(k + 1) * P], ident[:, :])
                last.then_inc(xt_turned, 1)

            def sum_pair(s, g, src):
                pe.wait_ge(s.sq_made, g + 1)
                for j in range(2):
                    mm = nc.tensor.matmul(pair[1][:, 0, :], ones[:, :], src[:, j, :], start=g == 0 and j == 0,
                                          stop=g == 3 and j == 1)
                mm.then_inc(s.sum_ready if g == 3 else s.summed, 1)

            def product(out, w_h, w_l, x_h, x_l, first, last):
                nc.tensor.matmul(out, w_h, x_h, start=first, stop=False)
                nc.tensor.matmul(out, w_h, x_l, start=False, stop=False)
                return nc.tensor.matmul(out, w_l, x_h, start=False, stop=last)

            def narrow_block(slot, out, xs_hi, xs_lo, x0, kts, first, last, ready=None):
                wh = w_hi[slot][:, 0:kts * COLS].rearrange("p (k c) -> p k c", c=COLS)
                wl = w_lo[slot][:, 0:kts * COLS].rearrange("p (k c) -> p k c", c=COLS)
                for k in range(kts):
                    if ready and k % ready[1] == 0:
                        pe.wait_ge(ready[0], k // ready[1] + 1)
                    for j in range(2):
                        mm = product(out[:, j, :], wh[:, k, j * P:(j + 1) * P], wl[:, k, j * P:(j + 1) * P],
                                     xs_hi[:, x0 + k, :], xs_lo[:, x0 + k, :],
                                     first and k == 0, last and k == kts - 1)
                mm.then_inc(block_done, 1)

            def bias_step(i, slot):
                pe.wait_ge(past_made, i + 1)
                if not isinstance(i, int) or i:
                    pe.wait_ge(bias_made, i)
                for j in range(4):
                    for part in range(3):
                        mm = nc.tensor.matmul(pair[3][j * 32:(j + 1) * 32, 0, :], step_b[part][:, :],
                                              past[slot][:, 4 * j:4 * j + 4, :].rearrange("p q c -> p (q c)"),
                                              start=part == 0, stop=part == 2, tile_position=(0, 32 * j))
                mm.then_inc(bias_summed, 1)

            def ffn_pe(s, n_in, n_next, bias=False):
                b = q.block
                for o in range(2):
                    pe.wait_ge(lo_made, b + o + 1)
                    if o == 1:
                        pe.wait_ge(n_in.ln_made, 1)
                    narrow_block((b + o) % 2, pair[o], h_hi, h_lo, 0, KD, True, True,
                                 (n_in.ready, 1) if o == 0 else None)
                    if bias:
                        bias_step(o, o)
                with pe.Fori(1, F // COLS) as i:
                    pe.wait_ge(lo_made, b + 1 + 2 * i)
                    pe.wait_ge(s.gate_made, i)
                    narrow_block(b % 2, pair[0], h_hi, h_lo, 0, KD, True, True)
                    if bias:
                        bias_step(2 * i, 0)
                    pe.wait_ge(lo_made, b + 2 + 2 * i)
                    pe.wait_ge(s.act_made, i)
                    narrow_block((b + 1) % 2, pair[1], h_hi, h_lo, 0, KD, True, True)
                    if bias:
                        bias_step(2 * i + 1, 1)
                b = q.block = b + 2 * (F // COLS)
                for g in range(4):
                    for c, k0 in enumerate((0, 8, 16)):
                        o = 3 * g + c
                        kts = min(8, KF - k0)
                        pe.wait_ge(lo_made, b + o + 1)
                        pe.wait_ge(s.act_ready, (k0 + kts) // 2)
                        if c == 0 and g >= 2:
                            pe.wait_ge(s.x_added, g - 1)
                        narrow_block((b + o) % 2, pair[DOWN_PAIR[g]], act_hi, act_lo, k0, kts, c == 0, c == 2)
                        if c == 0 and g:
                            if g == 1:
                                pe.wait_ge(s.act_made, F // COLS)
                            sum_pair(n_next, g - 1, sq_pair[(g - 1) % 2])
                        if bias and 22 + o < BSTEPS:
                            bias_step(22 + o, o % 2)
                sum_pair(n_next, 3, sq_pair[1])
                q.block = b + 12

            def claim(bank):
                if q.reader[bank]:
                    pe.wait_ge(*q.reader[bank])

            def claim_pair(k, sem_, value):
                claim(2 * k)
                claim(2 * k + 1)
                q.reader[2 * k] = q.reader[2 * k + 1] = (sem_, value)

            def next_narrow(k, xs_hi, xs_lo, reader, cols=None, ready=None):
                claim_pair(k, *reader)
                pe.wait_ge(lo_made, q.block + 1)
                out = pair[k] if cols is None else pair[k][:, :, 0:cols]
                narrow_block(q.block % 2, out, xs_hi, xs_lo, 0, KD, True, True, ready)
                q.block += 1

            def wide_slot():
                pe.wait_ge(lo_made, q.block + 1)
                b = q.block % 2
                q.block += 1
                return (w_hi[b][:, :].rearrange("p (k c) -> p k c", c=WIDE),
                        w_lo[b][:, :].rearrange("p (k c) -> p k c", c=WIDE))

            def wide_features(k, xs_hi, xs_lo):
                wh, wl = wide_slot()
                for m in range(4):
                    for kt in range(4):
                        mm = product(pair[k + m // 2][:, m % 2, :], wh[:, kt, m * P:(m + 1) * P],
                                     wl[:, kt, m * P:(m + 1) * P], xs_hi[:, kt, :], xs_lo[:, kt, :],
                                     kt == 0, kt == 3)
                mm.then_inc(block_done, 1)

            def wide_tokens(k, xs_hi, xs_lo, x0, tiles, first, last):
                wh, wl = wide_slot()
                for a in range(tiles):
                    out = pair[k + a // 2][:, a % 2, :]
                    for kt in range(4):
                        xh = xs_hi[:, x0 + kt, a * P:(a + 1) * P]
                        nc.tensor.matmul(out, xh, wh[:, kt, :], start=first and kt == 0, stop=False)
                        nc.tensor.matmul(out, xh, wl[:, kt, :], start=False, stop=False)
                        mm = nc.tensor.matmul(out, xs_lo[:, x0 + kt, a * P:(a + 1) * P], wh[:, kt, :],
                                              start=False, stop=last and kt == 3)
                mm.then_inc(block_done, 1)

            def gates_pe():
                claim_pair(0, g_pre, 1)
                pe.wait_ge(lo_made, q.block + 1)
                b = q.block % 2
                wh = w_hi[b][:, :].rearrange("p (k c) -> p k c", c=COLS)
                wl = w_lo[b][:, :].rearrange("p (k c) -> p k c", c=COLS)
                for j in range(2):
                    c0 = j * M_HEADS
                    for k in range(KD):
                        if j == 0:
                            pe.wait_ge(n_mix.ready, k + 1)
                        mm = product(pair[0][:, j, :], wh[:, k, c0:c0 + P], wl[:, k, c0:c0 + P],
                                     h_hi[:, k, :], h_lo[:, k, :], k == 0, k == KD - 1)
                mm.then_inc(block_done, 1)
                q.block += 1

            def gates_turn_pe():
                claim_pair(1, g_ready, 1)
                pe.wait_ge(g_diag, 1)
                nc.tensor.matmul(pair[1][:, 1, 0:8], ones[0:M_HEADS, :],
                                 dec_diag[:, :, :].rearrange("p c h -> p (c h)"), start=True, stop=True)
                pe.wait_ge(g_exp, 2)
                for a in range(4):
                    for c in range(CHUNKS):
                        col = (a * CHUNKS + c) * M_HEADS
                        mm = nc.tensor.transpose(pair[1][:, 0, col:col + M_HEADS],
                                                 g_rows[:, a, c * P:(c + 1) * P], ident[0:M_HEADS, 0:M_HEADS])
                mm.then_inc(g_turned, 1)

            def head_pe(h):
                if h == 0:
                    for m in range(2):
                        next_narrow(m, h_hi, h_lo, (xmh_made, m + 1))
                pe.wait_ge(xml_made, 2 * h + 2)
                for k in range(2):
                    claim_pair(2 + k, v_made, 2 * h + k + 1)
                wide_tokens(2, xm_hi, xm_lo, 0, NT, True, True)
                if h == 0:
                    gates_turn_pe()
                for m in range(2):
                    next_narrow(m, h_hi, h_lo, (o_made, 2 * h + m + 1))
                pe.wait_ge(xcl_made, h + 1)
                for k in range(2):
                    claim_pair(2 + k, q_made, 2 * h + k + 1)
                wide_features(2, xc_hi, xc_lo)
                for k in range(2):
                    claim_pair(k, k_made, 2 * h + k + 1)
                wide_features(0, xc_hi, xc_lo)
                claim(6)
                if h == 0:
                    pe.wait_ge(consts_made, 8)
                nc.tensor.matmul(pair[3][:, 0, :], sel[:, h, :], g_neg[:, :], start=True, stop=True)\
                    .then_inc(negm_spread, 1)
                for bank in (4, 5, 7, 0, 1, 2, 3):
                    claim(bank)
                def chunk(c):
                    return slice(c * P, (c + 1) * P)
                for c in range(CHUNKS):
                    for k in range(MK):
                        mm = nc.tensor.matmul(pair[2][:, 0, chunk(c)], k_f[:, k, chunk(c)], q_f[:, k, chunk(c)],
                                              start=k == 0, stop=k == MK - 1)
                mm.then_inc(sc_ready, 1)
                for c in range(CHUNKS - 1):
                    if KT_BANK[c] == 6:
                        pe.wait_ge(w_arg, h + 1)
                    for k in range(MK):
                        mm = nc.tensor.transpose(pair[KT_BANK[c] // 2][:, KT_BANK[c] % 2, k * P:(k + 1) * P],
                                                 k_f[:, k, chunk(c)], ident[:, :])
                    mm.then_inc(kt_ready, 1)
                small = pair[3][:, 0, :]

                for c in range(CHUNKS):
                    g = CHUNKS * h + c
                    if c < CHUNKS - 1:
                        pe.wait_ge(kws_made, 3 * h + c + 1)
                        for half in range(2):
                            if c > 0:
                                pe.wait_ge(c_made, 2 * (3 * h + c - 1) + half + 1)
                            for j in range(2):
                                ks = slice((2 * half + j) * P, (2 * half + j + 1) * P)
                                mm = nc.tensor.matmul(pair[half][:, j, :], k_ws[:, c, ks], v_f[:, c, :], start=True,
                                                      stop=True)
                            if half == 0:
                                mm.then_inc(upd_ready, 1)
                        if c == 0:
                            pe.wait_ge(kws_made, 3 * h + 3)
                        else:
                            pe.wait_ge(r_made, g)
                        for k in range(MK):
                            mm = nc.tensor.matmul(small[:, k:k + 1], k_ws[:, c, k * P:(k + 1) * P], ones[:, 0:1],
                                                  start=True, stop=True)
                        mm.then_inc(upd_ready, 1)
                    if c == 0:
                        pe.wait_ge(sw_made, h + 1)
                    else:
                        if c == 2:
                            pe.wait_ge(h_made, 3 * h + 1)
                        if c == CHUNKS - 1:
                            pe.wait_ge(c_made, 6 * (h + 1))
                            pe.wait_ge(r_made, g)
                        for k in range(MK):
                            nc.tensor.matmul(inter(c), q_f[:, k, chunk(c)], c_st[:, k, :], start=k == 0,
                                             stop=k == MK - 1)
                    if c == 0:
                        pe.wait_ge(c_made, 2 * 3 * h + 2)
                    if c > 0:
                        for k in range(MK):
                            nc.tensor.matmul(small[:, 5:6], q_f[:, k, chunk(c)], n_st[:, k:k + 1], start=k == 0,
                                             stop=k == MK - 1)
                    if c > 1:
                        pe.wait_ge(h_part, g - 1)
                    nc.tensor.matmul(small[:, 4:5], s_w[:, c, :], ones[:, 0:1], start=True, stop=True)
                    nc.tensor.matmul(pair[2 + c % 2][:, 1, :], s_w[:, c, :], v_f[:, c, :], start=True, stop=True)\
                        .then_inc(num_ready, 1)
                q.reader[0] = (h_made, 3 * (h + 1))
                q.reader[1] = q.reader[2] = q.reader[3] = (c_made, 6 * (h + 1))
                if h < M_HEADS - 1:
                    next_narrow(0, h_hi, h_lo, (xmh_made, 2 * h + 3))
                pe.wait_ge(hn_made, CHUNKS * (h + 1))
                for e in range(MK):
                    for c in range(CHUNKS):
                        mm = nc.tensor.transpose(pair[2 + e // 2][:, e % 2, c * P:(c + 1) * P],
                                                 h_m[:, c, e * P:(e + 1) * P], ident[:, :])
                    mm.then_inc(h_turned, 1)
                if h < M_HEADS - 1:
                    next_narrow(1, h_hi, h_lo, (xmh_made, 2 * h + 4))
                pe.wait_ge(yml_made, MK * (h + 1))
                q.reader[4] = q.reader[5] = q.reader[6] = q.reader[7] = None
                for m in range(2):
                    for k in range(2):
                        claim_pair(2 * m + k, bm_added, 4 * h + 2 * m + k + 1)
                    wide_features(2 * m, ym_hi, ym_lo)

            def filler(reader):
                b = q.block % 2
                out = pair[reader[0]]
                wh = w_hi[b][:, :].rearrange("p (k c) -> p k c", c=COLS)
                wl = w_lo[b][:, :].rearrange("p (k c) -> p k c", c=COLS)
                for piece in range(4):
                    if piece == 0:
                        claim_pair(*reader)
                        pe.wait_ge(lo_made, q.block + 1)
                    for k in range(2 * piece, 2 * piece + 2):
                        for j in range(2):
                            mm = product(out[:, j, :], wh[:, k, j * P:(j + 1) * P], wl[:, k, j * P:(j + 1) * P],
                                         h_hi[:, k, :], h_lo[:, k, :], k == 0, k == KD - 1)
                    if piece == 3:
                        mm.then_inc(block_done, 1)
                        q.block += 1
                    yield

            def merge_pe(gate, base, xs_hi, xs_lo, ready=None):
                def gate_block(m):
                    next_narrow(2 * (m % 2), h_hi, h_lo, (g_sig_made, base + m + 1))

                if not gate:
                    for m in range(4):
                        gate_block(m)
                    return
                for m in range(4):
                    if m < 3:
                        gate_block(m + 1)
                    if m == 0:
                        pe.wait_ge(*ready)
                    next_narrow(2 * (m % 2) + 1, xs_hi, xs_lo, (mg_made, base + m + 1))

            def attention_pe():
                for nh in range(2):
                    for k in range(2):
                        claim_pair(2 * nh + k, va_made, 2 * nh + k + 1)
                    wide_tokens(2 * nh, h_hi, h_lo, 0, NT, True, False)
                    wide_tokens(2 * nh, h_hi, h_lo, 4, NT, False, True)
                pe.wait_ge(lam_loaded, 64)
                claim(7)
                for j in range(2):
                    lq = smalls[0:A_QK, 32 + 2 * j:33 + 2 * j]
                    mm = nc.tensor.matmul(pair[3][:, 1, j:j + 1], lq.to_broadcast([A_QK, P]),
                                          smalls[0:A_QK, 33 + 2 * j:34 + 2 * j], start=True, stop=True)
                mm.then_inc(lam_summed, 1)
                q.reader[7] = (g_exp, 3)

                def scores(u):
                    hh, qt, hb = (u // 4) % 2, u % 4, (u // 8) % 2
                    b = u % 2
                    if u < 2:
                        claim(4 + 2 * b)
                        claim(5 + 2 * b)
                    else:
                        pe.wait_ge(a_shifted, 2 * (u - 2) + 2)
                    if u % 8 == 0:
                        pe.wait_ge(qa_made, u // 8 + 1)
                        pe.wait_ge(ka_made, u // 8 + 1)
                    for j in range(2):
                        r = slice(j * A_QK, (j + 1) * A_QK)
                        mm = nc.tensor.matmul(pair[2 + b][:, j, :], q_a[hb][r, hh, qt * P:(qt + 1) * P],
                                              k_a[hb][r, hh, :], start=True, stop=True)
                    mm.then_inc(a_scored, 1)

                next_narrow(0, h_hi, h_lo, (qa_made, 1))
                next_narrow(1, h_hi, h_lo, (ka_made, 1))
                def head_out(e):
                    pe.wait_ge(a_tr_made, 4 * e + 4)
                    if e:
                        pe.wait_ge(a_y, e)
                    for k in range(NT):
                        mm = nc.tensor.matmul(pair[1][:, 1, :], va[:, k, e * P:(e + 1) * P], a_tr[:, k, :],
                                              start=k == 0, stop=k == NT - 1)
                    mm.then_inc(a_out, 1)

                def head_sum(e, turned):
                    pe.wait_ge(a_tr_made, turned)
                    pe.wait_ge(a_sq, e + 1)
                    nc.tensor.matmul(pair[1][:, 0, :], ones[:, :], o_sq[:, :], start=True, stop=True)\
                        .then_inc(a_sum, 1)

                claim(2)
                claim(3)
                scores(0)
                for u in range(4 * A_HEADS):
                    hp, e = u // 8, u // 4 - 1
                    if u % 8 == 0:
                        readers = [(0, qa_made, hp + 2), (0, ka_made, hp + 2)] if hp < 3 else [(0, g_sig_made, 5)]
                        pieces = (None for r in readers for _ in filler(r))
                    if u + 1 < 4 * A_HEADS:
                        scores(u + 1)
                    if u % 4 == 1 and e >= 0:
                        head_sum(e, u)
                    for _ in range(A_FILL[u % 8]):
                        next(pieces, None)
                    if u % 4 == 0 and e >= 0:
                        head_out(e)
                    pe.wait_ge(a_mixed, u + 1)
                    if u % 4 == 1 and e >= 0:
                        pe.wait_ge(a_r, e + 1)
                    elif u:
                        pe.wait_ge(a_tr_made, u)
                    for k in range(NT):
                        mm = nc.tensor.transpose(pair[1][:, 0, k * P:(k + 1) * P],
                                                 probs[u % 2][:, 0, k * P:(k + 1) * P], ident[:, :])
                    mm.then_inc(a_turned, 1)
                pe.wait_ge(mem_r, MT)
                pe.wait_ge(a_shifted, 64)
                for k in range(KD):
                    for a in range(MT):
                        col = (k % 2) * MEM + a * P
                        mm = nc.tensor.transpose(pair[2 + k // 4][:, k // 2 % 2, col:col + P],
                                                 mem_tok[:, a, k * P:(k + 1) * P], ident[:, :])
                    if k % 4 == 3:
                        mm.then_inc(mem_turned, 1)
                head_out(A_HEADS - 1)
                head_sum(A_HEADS - 1, 4 * A_HEADS)
                q.reader[2] = q.reader[3] = (a_y, A_HEADS)
                q.reader[4] = q.reader[5] = (memn_made, 4)
                q.reader[6] = q.reader[7] = (memn_made, KD)

            def cross_pe():
                pe.wait_ge(meml_made, KD)
                for m in range(4):
                    next_narrow(m % 2, memn_hi, memn_lo, (kx_made, m + 1), cols=MEM)
                for nh in range(2):
                    claim_pair(2 + nh, vx_made, nh + 1)
                    wide_tokens(2 + nh, memn_hi, memn_lo, 0, MT, True, False)
                    wide_tokens(2 + nh, memn_hi, memn_lo, 4, MT, False, True)
                next_narrow(0, h_hi, h_lo, (qx_made, 1))

                def scores(u):
                    h, qt = u // 4, u % 4
                    if u < 2:
                        claim(4 + u)
                        claim(6 + u)
                    else:
                        pe.wait_ge(x_exp, u - 1)
                    if qt == 0:
                        pe.wait_ge(qx_made, h + 1)
                    for k in range(2):
                        mm = nc.tensor.matmul(pair[2][:, u % 2, 0:MEM], q_x[:, 2 * h + k, qt * P:(qt + 1) * P],
                                              k_x[:, 2 * h + k, :], start=k == 0, stop=k == 1)
                    mm.then_inc(x_scored, 1)

                def head_out(h):
                    pe.wait_ge(x_tr_made, 4 * h + 4)
                    claim_pair(X_OUT_PAIR[h], x_yl, h + 1)
                    for j in range(2):
                        for a in range(MT):
                            mm = nc.tensor.matmul(pair[X_OUT_PAIR[h]][:, j, :],
                                                  v_x[:, a, (2 * h + j) * P:(2 * h + j + 1) * P],
                                                  p_tr[:, a, :], start=a == 0, stop=a == MT - 1)
                    mm.then_inc(x_out, 1)

                scores(0)
                for u in range(4 * X_HEADS):
                    if u % 4 == 0:
                        h = u // 4
                        pieces = filler(((h + 1) % 2, qx_made, h + 2) if h < X_HEADS - 1 else (0, g_sig_made, 9))
                    if u + 1 < 4 * X_HEADS:
                        scores(u + 1)
                    for _ in range(X_FILL[u % 4]):
                        next(pieces)
                    if u % 4 == 0 and u:
                        head_out(u // 4 - 1)
                    pe.wait_ge(x_norm, u + 1)
                    if u >= 2:
                        pe.wait_ge(x_tr_made, u - 1)
                    for a in range(MT):
                        mm = nc.tensor.transpose(pair[3][:, u % 2, a * P:(a + 1) * P],
                                                 p_x[u % 2][:, a * P:(a + 1) * P], ident[:, :])
                    mm.then_inc(x_turned, 1)
                head_out(X_HEADS - 1)
                q.reader[4] = q.reader[5] = (x_exp, 4 * X_HEADS)
                q.reader[6] = q.reader[7] = (x_tr_made, 4 * X_HEADS)

            def out_pe():
                for m in range(4):
                    next_narrow(2 + m % 2, mg_hi, mg_lo, (x_mixed, m + 1), ready=(mgl_made, 2) if m == 0 else None)
                    if m == 0:
                        claim(2)
                    if m:
                        sum_pair(n_ffn[1], m - 1, sq_pair[(m - 1) % 2])
                sum_pair(n_ffn[1], 3, sq_pair[1])

            for g in range(4):
                sum_pair(n_ffn[0], g, sq[:, 2 * g:2 * g + 2, :])
            pe.wait_ge(pos_made, 2)
            nc.tensor.matmul(pair[2][:, 0, :], sign_row[:, :], pos_r[:, :], start=True, stop=True)\
                .then_inc(pos_spread, 1)
            ffn_pe(ffn[0], n_ffn[0], n_mix, bias=True)
            gates_pe()
            for h in range(M_HEADS):
                head_pe(h)
            merge_pe(0, 0, None, None)
            attention_pe()
            merge_pe(1, 4, ya_hi, ya_lo, (a_yl, A_HEADS))
            cross_pe()
            merge_pe(2, 8, yx_hi, yx_lo, (x_yl, X_HEADS))
            out_pe()
            ffn_pe(ffn[1], n_ffn[1], n_fin)
            for a in range(NT):
                for half in range(2):
                    pe.wait_ge(n_fin.raw_made, 4 * half + 4)
                    if a >= 2:
                        pe.wait_ge(out_hi_made if half else out_lo_made, a - 1)
                    for k in range(4 * half, 4 * half + 4):
                        last = nc.tensor.transpose(pair[2 + a % 2][:, half, (k % 4) * P:(k % 4 + 1) * P],
                                                   sq[:, k, a * P:(a + 1) * P], ident[:, :])
                    last.then_inc(out_turned, 1)


_INS = ["x", "mem", "positions", "rel_bias", "ffn1_norm", "ffn1_w_gu", "ffn1_w_down", "mix_norm", "mem_norm",
        "w_in", "b_if", "b_gate", "m_conv_w", "m_conv_b", "m_wq", "m_wk", "m_wv", "m_head_norm",
        "a_lam_q1", "a_lam_k1", "a_lam_q2", "a_lam_k2", "a_head_norm", "w_mem_kv", "w_branch_m",
        "w_branch_a", "w_branch_x", "w_out", "ffn2_norm", "ffn2_w_gu", "ffn2_w_down", "final_norm"]


def _thresholds():
    n = np.arange(1, 256)
    large = 16 + (np.log(np.maximum(n, 1) / np.float32(16)) / np.log(128 / 16) * 16).astype(np.int32)
    bucket = np.where(n < 16, n, np.minimum(large, BUCKETS - 1))
    first = [0.5] + [float(n[np.argmax(bucket >= b)]) for b in range(1, BUCKETS)]
    return np.tile(np.array(first, np.float32), 4).reshape(P, 1)


def kernel(**inputs):
    import concourse.bacc as _bacc
    from concourse import mybir as _mybir
    from concourse.bass_utils import run_bass_kernel_spmd as _run

    nc = _bacc.Bacc("TRN2", target_bir_lowering=False, num_devices=1)
    arrays, t = {}, {}
    inputs["thresholds"] = _thresholds()
    for name in _INS + ["thresholds"]:
        a = np.ascontiguousarray(inputs[name])
        if a.ndim > 1 and a.shape[0] == 1:
            a = a.reshape(a.shape[1:])
        arrays[f"in_{name}"] = a
        t[name] = nc.dram_tensor(f"in_{name}", a.shape, _mybir.dt.from_np(a.dtype), kind="ExternalInput").ap()
    out = nc.dram_tensor("out", (S, D), F32, kind="ExternalOutput")
    t["out"] = out.ap()
    build(nc, t)
    r = _run(nc, [arrays], core_ids=[0])
    return r.results[0]["out"].reshape(1, S, D)
```

```python
from contextlib import ExitStack

import numpy as np

import concourse.bass as bass
from concourse import mybir

F32 = mybir.dt.float32
F32R = mybir.dt.float32r
BF16 = mybir.dt.bfloat16
I32 = mybir.dt.int32
ALU = mybir.AluOpType
ACT = mybir.ActivationFunctionType
AX = mybir.AxisListType

P = 128
S = 512
D = 1024
KD = D // P
NT = S // P
F = 2816
KF = F // P
COLS = 256
EPS = 1e-6
KB = 1024
MEM = 256
MT = MEM // P
M_HEADS = 4
M_HD = 2 * D // M_HEADS
MK = M_HD // P
CHUNKS = S // P
A_HEADS = 8
A_QK = 64
X_HEADS = 4
X_HD = D // X_HEADS
BUCKETS = 32
LAM_INIT = 0.2
A_SCALE = A_QK ** -0.5
X_SCALE = X_HD ** -0.5
HIDE = -1e30
KEYS4 = S // 4
QSTEP = 16
BSTEPS = S // QSTEP
C_XM, C_O, C_IF = 0, 2 * D, 4 * D
C_QA = C_IF + 2 * M_HEADS
C_KA, C_VA, C_QX, C_G = C_QA + D, C_QA + 2 * D, C_QA + 3 * D, C_QA + 4 * D
WIDE = 512
HEAD_BLOCKS = 9


class Progress:

    def __init__(self):
        self.block = 0
        self.reader = [None] * 8


def build(nc, t):
    ctx = ExitStack()
    with ctx:
        def sem(name):
            return ctx.enter_context(nc.semaphore(name))

        base = -(-nc.sbuf_base // 64) * 64

        def at(name, kb, shape, dtype=F32):
            return nc.alloc_sbuf_tensor_at(name, shape, dtype, offset=base + int(kb * KB))

        xT = at("xT", 0, [P, KD, S])
        w_raw = [at(f"w_raw{i}", 16 + 8 * i, [P, 2048]) for i in range(2)]
        w_hi = [at(f"w_hi{i}", 32 + 8 * i, [P, 2048], F32R) for i in range(2)]
        w_lo = [at(f"w_lo{i}", 48 + 8 * i, [P, 2048], F32R) for i in range(2)]
        h_hi = at("h_hi", 64, [P, KD, S], F32R)
        h_lo = at("h_lo", 80, [P, KD, S], F32R)
        merged = at("merged", 96, [P, KD, S])
        ident = at("ident", 112, [P, P])
        ones = at("ones", 112.5, [P, P])
        par = at("par", 113, [P, 176])
        eps_c = at("eps_c", 114, [P, 1])
        smalls = at("smalls", 114.0625, [P, 40])
        mask = at("mask", 114.25, [P, P])
        Z = 115
        sq = at("sq", Z, [P, KD, S])
        act_hi = at("act_hi", Z, [P, KF, S], F32R)
        act_lo = at("act_lo", Z + 44, [P, KF, S], F32R)
        gate_s = at("gate_s", 96, [P, 2, S])
        act_f = at("act_f", 100, [P, 2, S])
        sq_pair = [at(f"sq_pair{i}", 96 + 4 * i, [P, 2, S]) for i in range(2)]
        rinv = at("rinv", 104, [P, S])
        lnv = at("lnv", 106, [P, S])
        x_tok = at("x_tok", Z + 32, [P, NT, D])
        prm1 = at("prm1", Z + 48, [104, P])
        prm2 = at("prm2", Z + 49, [64, P])
        past = [at(f"past{i}", 104 + 4 * i, [P, QSTEP, KEYS4], BF16) for i in range(2)]
        bias_out = at("bias_out", Z + 88, [P, S])
        pq_s = at("pq_s", Z + 90, [P, S])
        pk_s = at("pk_s", Z + 92, [P, KEYS4])
        step_b = [at(f"step_b{i}", 114.75 + 0.0625 * i, [P, 32], BF16) for i in range(3)]
        rb_base = smalls[:, 36:37]
        rb_cur = at("rb_cur", Z + 64, [P, A_HEADS])
        rb_prev = at("rb_prev", Z + 64.0625, [P, A_HEADS])
        thr = at("thr", Z + 64.125, [P, 1])
        step_f = at("step_f", Z + 64.25, [P, 32])
        sign_row = at("sign_row", Z + 65, [1, P])
        pos_i = at("pos_i", Z + 66, [1, S], I32)
        pos_h = at("pos_h", Z + 68, [1, S], I32)
        pos_l = at("pos_l", Z + 70, [1, S], I32)
        pos_hf = at("pos_hf", Z + 72, [1, S])
        pos_lf = at("pos_lf", Z + 74, [1, S])
        pos_r = at("pos_r", Z + 76, [1, S])
        g_i = at("g_i", Z + 40.5, [M_HEADS, S])
        g_f = at("g_f", Z + 42.5, [M_HEADS, S])
        g_abs = at("g_abs", Z + 44.5, [M_HEADS, S])
        g_ln = at("g_ln", Z + 46.5, [M_HEADS, S])
        g_lf = at("g_lf", Z + 48.5, [M_HEADS, S])
        g_b = at("g_b", Z + 50.5, [M_HEADS, S])
        g_m = at("g_m", Z + 52.5, [M_HEADS, S])
        g_rows = at("g_rows", Z + 72.5, [M_HEADS, 4, S])
        one_row = at("one_row", Z + 54.5, [M_HEADS, S])
        g_neg = at("g_neg", Z + 87.5, [M_HEADS, S])
        tokp = at("tokp", Z + 89.5, [P, 4, CHUNKS, M_HEADS])
        m_small = at("m_small", Z + 89.75, [P, 64])
        sel = at("sel", Z + 90.25, [M_HEADS, M_HEADS, P])
        decay = m_small[:, 0:8]
        dec_row = at("dec_row", Z + 92.25, [M_HEADS, 2])
        dec_diag = at("dec_diag", Z + 92.3125, [M_HEADS, 2, M_HEADS])
        xm_f = at("xm_f", Z, [P, MK, S + 4])
        xm_hi = at("xm_hi", Z + 8.5, [P, MK, S], F32R)
        xm_lo = at("xm_lo", Z + 16.5, [P, MK, S], F32R)
        xc_hi = at("xc_hi", Z + 24.5, [P, MK, S], F32R)
        xc_lo = at("xc_lo", Z + 32.5, [P, MK, S], F32R)
        q_f = at("q_f", Z + 40.5, [P, MK, S])
        k_f = at("k_f", Z + 48.5, [P, MK, S])
        v_f = at("v_f", Z + 56.5, [P, CHUNKS, M_HD])
        conv = at("conv", Z + 64.5, [P, MK, S])
        k_ws = at("k_ws", Z + 32.5, [P, CHUNKS - 1, M_HD])
        c_st = [at(f"c_st{i}", Z + (24.5, 16.5)[i], [P, MK, M_HD]) for i in range(2)]
        h_m = at("h_m", Z + 64.5, [P, CHUNKS, M_HD])
        o_sig = at("o_sig", Z + 72.5, [P, MK, S])
        w_in_tr = at("w_in_tr", Z + 80.5, [P, CHUNKS, P])
        s_w = at("s_w", Z + 82.5, [P, CHUNKS, P])
        y_f = [at(f"y_f{i}", Z + 80.5 + 2 * i, [P, S]) for i in range(2)]
        h_sq = at("h_sq", Z + 84.5, [P, S])
        ym_hi = at("ym_hi", Z + 40.5, [P, MK, S], F32R)
        ym_lo = at("ym_lo", Z + 48.5, [P, MK, S], F32R)
        n_st = [m_small[:, 8:12], m_small[:, 32:36]]
        sumsq = m_small[:, 12:16]
        den = m_small[:, 16:32]
        va = at("va", Z, [P, NT, D])
        q_a = [at(f"q_a{i}", Z + 16 + 8 * i, [P, 2, S]) for i in range(2)]
        k_a = [at(f"k_a{i}", Z + 20 + 8 * i, [P, 2, S]) for i in range(2)]
        ya_hi = at("ya_hi", Z + 32, [P, KD, S], F32R)
        ya_lo = at("ya_lo", Z + 48, [P, KD, S], F32R)
        bias_sb = [at(f"bias_sb{i}", Z + 64 + 2 * i, [P, S]) for i in range(4)]
        probs = [at(f"probs{i}", Z + 72 + 4 * i, [P, 2, S]) for i in range(2)]
        o_sq = at("o_sq", Z + 80, [P, S])
        y_af = at("y_af", Z + 82, [P, S])
        a_tr = at("a_tr", Z + 84, [P, NT, S])
        g_sig_m = at("g_sig_m", Z, [P, KD, S])
        g_sig = at("g_sig", Z + 84, [P, 2, S])
        g_tmp = at("g_tmp", Z + 88, [P, 2, S])
        memn_hi = at("memn_hi", Z, [P, KD, MEM], F32R)
        memn_lo = at("memn_lo", Z + 8, [P, KD, MEM], F32R)
        k_x = at("k_x", Z + 16, [P, KD, MEM])
        v_x = at("v_x", Z + 24, [P, MT, D])
        q_x = at("q_x", Z + 32, [P, KD, S])
        mem_tok = at("mem_tok", Z + 16, [P, MT, D])
        memn_f = at("memn_f", Z + 24, [P, KD, MEM])
        mem_sq = at("mem_sq", Z + 62, [P, D], BF16)
        yx_hi = at("yx_hi", Z + 48, [P, KD, S], F32R)
        yx_lo = at("yx_lo", Z + 64, [P, KD, S], F32R)
        p_tr = at("p_tr", Z + 80, [P, MT, S])
        p_x = [at(f"p_x{i}", Z + 88 + i, [P, MEM]) for i in range(2)]
        mg_hi = at("mg_hi", Z, [P, KD, S], F32R)
        mg_lo = at("mg_lo", Z + 16, [P, KD, S], F32R)
        bias_dram = nc.dram_tensor("bias_dram", [A_HEADS * 4, S, KEYS4], F32, kind="Internal").ap()
        o_tok = at("o_tok", Z + 32, [P, NT, D])

        pair = [ctx.enter_context(nc.psum_tensor(f"pair{i}", [P, 2, S], F32)) for i in range(4)]

        PC = {}
        col = 0
        for name, n in (("ffn1_norm", 8), ("mix_norm", 8), ("mem_norm", 8), ("ffn2_norm", 8),
                        ("final_norm", 8), ("m_head_norm", 16), ("a_head_norm", 8), ("m_conv_b", 16),
                        ("b_gate", 24), ("m_conv_w", 64)):
            PC[name] = (col, n)
            col += n

        def pcol(name, k):
            return par[:, PC[name][0] + k:PC[name][0] + k + 1]

        raw_loaded = [sem(f"raw_loaded{i}") for i in range(2)]
        hi_made = sem("hi_made")
        lo_made = sem("lo_made")
        block_done = sem("block_done")
        consts_made = sem("consts_made")
        prm_loaded = sem("prm_loaded")
        x_loaded = [sem(f"x_loaded{i}") for i in range(2)]
        par_turned = sem("par_turned")
        par_made = sem("par_made")
        xt_turned = sem("xt_turned")
        xt_made = sem("xt_made")
        out_turned = sem("out_turned")
        out_lo_made = sem("out_lo_made")
        out_hi_made = sem("out_hi_made")
        out_stored = sem("out_stored")

        chain_d = sem("chain_d")
        chain_a = sem("chain_a")
        thr_loaded = sem("thr_loaded")
        pos_loaded = sem("pos_loaded")
        pos_made = sem("pos_made")
        pos_spread = sem("pos_spread")
        past_made = sem("past_made")
        bias_summed = sem("bias_summed")
        bias_made = sem("bias_made")
        bias_stored = sem("bias_stored")
        bif_loaded = sem("bif_loaded")
        g_pre = sem("g_pre")
        g_exp = sem("g_exp")
        g_arg = sem("g_arg")
        g_diag = sem("g_diag")
        g_turned = sem("g_turned")
        g_ready = sem("g_ready")
        xmh_made = sem("xmh_made")
        xml_made = sem("xml_made")
        conv_made = sem("conv_made")
        xc_made = sem("xc_made")
        xcl_made = sem("xcl_made")
        q_made = sem("q_made")
        k_made = sem("k_made")
        v_made = sem("v_made")
        o_made = sem("o_made")
        negm_spread = sem("negm_spread")
        w_arg = sem("w_arg")
        w_made = sem("w_made")
        sc_ready = sem("sc_ready")
        kt_ready = sem("kt_ready")
        sw_made = sem("sw_made")
        kws_made = sem("kws_made")
        num_ready = sem("num_ready")
        upd_ready = sem("upd_ready")
        n_made = sem("n_made")
        c_made = sem("c_made")
        r_made = sem("r_made")
        h_part = sem("h_part")
        h_made = sem("h_made")
        hn_made = sem("hn_made")
        h_turned = sem("h_turned")
        yf_made = sem("yf_made")
        ymh_made = sem("ymh_made")
        yml_made = sem("yml_made")
        bm_added = sem("bm_added")
        g_sig_made = sem("g_sig_made")
        mg_made = sem("mg_made")
        lam_loaded = sem("lam_loaded")
        lam_summed = sem("lam_summed")
        va_made = sem("va_made")
        qa_made = sem("qa_made")
        ka_made = sem("ka_made")
        bias_loaded = [sem(f"bias_loaded{i}") for i in range(4)]
        a_scored = sem("a_scored")
        a_shifted = sem("a_shifted")
        a_exp = sem("a_exp")
        a_mixed = sem("a_mixed")
        a_turned = sem("a_turned")
        a_tr_made = sem("a_tr_made")
        a_out = sem("a_out")
        a_sq = sem("a_sq")
        a_sum = sem("a_sum")
        a_r = sem("a_r")
        a_y = sem("a_y")
        a_yh = sem("a_yh")
        a_yl = sem("a_yl")
        mem_loaded = sem("mem_loaded")
        mem_r = sem("mem_r")
        mem_turned = sem("mem_turned")
        memn_made = sem("memn_made")
        memh_made = sem("memh_made")
        meml_made = sem("meml_made")
        kx_made = sem("kx_made")
        vx_made = sem("vx_made")
        qx_made = sem("qx_made")
        x_scored = sem("x_scored")
        x_max = sem("x_max")
        x_exp = sem("x_exp")
        x_norm = sem("x_norm")
        x_turned = sem("x_turned")
        x_tr_made = sem("x_tr_made")
        x_out = sem("x_out")
        x_yh = sem("x_yh")
        x_yl = sem("x_yl")
        mgh_made = sem("mgh_made")
        mgl_made = sem("mgl_made")
        x_mixed = sem("x_mixed")

        class NormSems:
            def __init__(self, name):
                self.sq_made = sem(f"{name}_sq_made")
                self.folded = sem(f"{name}_folded")
                self.summed = sem(f"{name}_summed")
                self.sum_ready = sem(f"{name}_sum_ready")
                self.ln_made = sem(f"{name}_ln_made")
                self.r_made = sem(f"{name}_r_made")
                self.raw_made = sem(f"{name}_raw_made")
                self.hi_made = sem(f"{name}_hi_made")
                self.ready = sem(f"{name}_ready")

        class FfnSems:
            def __init__(self, name):
                self.gate_made = sem(f"{name}_gate_made")
                self.act_made = sem(f"{name}_act_made")
                self.act_hi = sem(f"{name}_act_hi")
                self.act_ready = sem(f"{name}_act_ready")
                self.x_added = sem(f"{name}_x_added")

        n_ffn = [NormSems(f"n_ffn{i}") for i in range(2)]
        n_mix = NormSems("n_mix")
        n_fin = NormSems("n_fin")
        ffn = [FfnSems(f"ffn{i}") for i in range(2)]

        block = ctx.enter_context(nc.Block())

        O_PAIR = (2, 0)
        KT_BANK = (5, 7, 6)
        DOWN_PAIR = (2, 0, 2, 0)
        A_FILL = (2, 1, 1, 2, 2, 0, 0, 0)
        QA_UNIT, KA_UNIT = 2, 4
        X_FILL = (3, 1, 0, 0)
        QX_UNIT = 1
        X_OUT_PAIR = (1, 0, 1, 1)
        FFN_BLOCKS = 2 * (F // COLS) + 3 * (D // COLS)
        TOTAL = 2 * FFN_BLOCKS + 1 + HEAD_BLOCKS * M_HEADS + 2 * (4 + 8) + 6 * (D // COLS)

        def inter(c):
            return pair[1][:, 0, :] if c == CHUNKS - 1 else pair[2][:, 0, :]

        def narrow(w, k0, kts, c0):
            return w[k0 * P:(k0 + kts) * P, bass.ds(c0, COLS)].rearrange("(k p) c -> p k c", p=P)

        @block.sync
        def _(sp):
            q = Progress()
            for i in range(2):
                half = slice(i * D // 2, (i + 1) * D // 2)
                sp.dma_start(x_tok[:, :, half], t["x"].rearrange("(a p) d -> p a d", p=P)[:, :, half])\
                    .then_inc(x_loaded[i], 16)

            def load(n, slot, src, kts=8, width=COLS, peeled=False):
                if not peeled:
                    sp.wait_ge(lo_made, n - 1)
                dst = w_raw[slot][:, 0:kts * width].rearrange("p (k c) -> p k c", c=width)
                sp.dma_start(dst, src).then_inc(raw_loaded[slot], 16)

            def load_next(src, kts=8, width=COLS):
                load(q.block, q.block % 2, src, kts, width)
                q.block += 1

            def bias_loads():
                sp.dma_start(thr[:, :], t["thresholds"]).then_inc(thr_loaded, 16)
                for k in range(4):
                    sp.dma_start(rb_cur[k * BUCKETS:(k + 1) * BUCKETS, :], t["rel_bias"]).then_inc(thr_loaded, 16)
                    sp.dma_start(rb_prev[k * BUCKETS:k * BUCKETS + 1, :], t["rel_bias"][0:1, :])\
                        .then_inc(thr_loaded, 16)
                    sp.dma_start(rb_prev[k * BUCKETS + 1:(k + 1) * BUCKETS, :], t["rel_bias"][0:BUCKETS - 1, :])\
                        .then_inc(thr_loaded, 16)
                for j in range(4):
                    for k in range(4):
                        sp.dma_start(rb_base[j * 32 + k:j * 32 + 32:4, :],
                                     t["rel_bias"][0:1, :].rearrange("a h -> h a")).then_inc(thr_loaded, 16)

            def ffn_loads(w_gu, w_down):
                b = q.block
                first = 0
                if b == 0:
                    load(0, 0, narrow(w_gu, 0, KD, 0), peeled=True)
                    load(1, 1, narrow(w_gu, 0, KD, F), peeled=True)
                    bias_loads()
                    first = 1
                with sp.Fori(first, F // COLS) as i:
                    load(b + 2 * i, b % 2, narrow(w_gu, 0, KD, i * COLS))
                    load(b + 2 * i + 1, (b + 1) % 2, narrow(w_gu, 0, KD, F + i * COLS))
                q.block = b + 2 * (F // COLS)
                for m in range(4):
                    for k0 in (0, 8, 16):
                        load_next(narrow(w_down, k0, min(8, KF - k0), m * COLS), min(8, KF - k0))

            def wide(w, k0, c0):
                return w[k0 * P:(k0 + 4) * P, c0:c0 + WIDE].rearrange("(k p) c -> p k c", p=P)

            def gate_load(gate, m):
                load_next(narrow(t["w_in"], 0, KD, C_G + gate * D + m * COLS))

            def branch_loads(w, gate):
                gate_load(gate, 0)
                for m in range(4):
                    if m < 3:
                        gate_load(gate, m + 1)
                    load_next(narrow(w, 0, KD, m * COLS))

            ffn_loads(t["ffn1_w_gu"], t["ffn1_w_down"])
            load_next(narrow(t["w_in"], 0, KD, C_IF))

            def xm_load(h, m):
                load_next(narrow(t["w_in"], 0, KD, C_XM + h * M_HD + m * COLS))

            xm_load(0, 0)
            xm_load(0, 1)
            for h in range(M_HEADS):
                load_next(t["m_wv"][h].rearrange("(k p) c -> p k c", p=P), 4, WIDE)
                load_next(narrow(t["w_in"], 0, KD, C_O + h * M_HD))
                for w in ("m_wk", "m_wq"):
                    load_next(t[w][h].rearrange("(k p) c -> p k c", p=P), 4, WIDE)
                load_next(narrow(t["w_in"], 0, KD, C_O + h * M_HD + COLS))
                for m in range(2):
                    if h < M_HEADS - 1:
                        xm_load(h + 1, m)
                    else:
                        gate_load(0, m)
                for m in range(2):
                    load_next(wide(t["w_branch_m"], h * MK, m * WIDE), 4, WIDE)
            gate_load(0, 2)
            gate_load(0, 3)
            for nh in range(2):
                for kh in range(2):
                    load_next(wide(t["w_in"], 4 * kh, C_VA + nh * WIDE), 4, WIDE)
            for hp in range(4):
                load_next(narrow(t["w_in"], 0, KD, C_QA + hp * COLS))
                load_next(narrow(t["w_in"], 0, KD, C_KA + hp * COLS))
            branch_loads(t["w_branch_a"], 1)
            for m in range(4):
                load_next(narrow(t["w_mem_kv"], 0, KD, m * COLS))
            for nh in range(2):
                for kh in range(2):
                    load_next(wide(t["w_mem_kv"], 4 * kh, D + nh * WIDE), 4, WIDE)
            for m in range(4):
                load_next(narrow(t["w_in"], 0, KD, C_QX + m * COLS))
            branch_loads(t["w_branch_x"], 2)
            for m in range(4):
                load_next(narrow(t["w_out"], 0, KD, m * COLS))
            ffn_loads(t["ffn2_w_gu"], t["ffn2_w_down"])
            for half, made in enumerate((out_lo_made, out_hi_made)):
                cols = slice(half * D // 2, (half + 1) * D // 2)
                for a in range(NT):
                    sp.wait_ge(made, a + 1)
                    sp.dma_start(t["out"][a * P:(a + 1) * P, cols], o_tok[:, a, cols]).then_inc(out_stored, 16)
            sp.wait_ge(out_stored, 16 * 2 * NT)

        @block.gpsimd
        def _(pool):
            pool.memset(ident[:, :], 0.0).then_inc(consts_made, 1)
            pool.memset(ones[:, :], 1.0).then_inc(consts_made, 1)
            pool.memset(eps_c[:, :], EPS).then_inc(consts_made, 1)
            pool.wait_ge(consts_made, 3)
            pool.affine_select(out=ident[:, :], in_=ident[:, :], compare_op=ALU.not_equal, fill=1.0,
                               base=0, pattern=[[-1, P]], channel_multiplier=1).then_inc(consts_made, 1)
            pool.memset(mask[:, :], 0.0).then_inc(consts_made, 1)
            pool.wait_ge(consts_made, 5)
            pool.affine_select(out=mask[:, :], in_=mask[:, :], compare_op=ALU.is_ge, fill=HIDE,
                               base=0, pattern=[[1, P]], channel_multiplier=-1).then_inc(consts_made, 1)
            pool.dma_start(pos_i[:, :], t["positions"].rearrange("(a s) -> a s", a=1)).then_inc(pos_loaded, 16)
            for j, name in enumerate(("a_lam_q1", "a_lam_k1", "a_lam_q2", "a_lam_k2")):
                pool.dma_start(smalls[0:A_QK, 32 + j:33 + j], t[name].rearrange("(p a) -> p a", a=1))\
                    .then_inc(lam_loaded, 16)
            pool.wait_ge(ffn[0].x_added, 4)
            pool.memset(sel[:, :, :], 0.0).then_inc(consts_made, 1)
            pool.wait_ge(consts_made, 7)
            pool.affine_select(out=sel[:, :, :], in_=sel[:, :, :], compare_op=ALU.not_equal, fill=1.0,
                               base=0, pattern=[[-1, M_HEADS], [0, P]], channel_multiplier=1)\
                .then_inc(consts_made, 1)
            pool.wait_ge(bias_stored, 64 * BSTEPS)
            pool.wait_ge(mg_made, 4)
            for u in range(4 * A_HEADS):
                if u >= 4:
                    pool.wait_ge(a_shifted, 2 * (u - 4) + 2)
                head = bias_dram[u // 4 * 4:u // 4 * 4 + 4, (u % 4) * P:(u % 4 + 1) * P, :]
                pool.dma_start(bias_sb[u % 4][:, :].rearrange("p (k c) -> p k c", k=4),
                               head.rearrange("k q c -> q k c")).then_inc(bias_loaded[u % 4], 16)

        @block.scalar
        def _(act):
            q = Progress()
            for name in ("ffn1_norm", "mix_norm", "mem_norm", "ffn2_norm", "final_norm", "m_head_norm",
                         "a_head_norm", "m_conv_b", "b_gate"):
                r, n = PC[name]
                act.dma_start(prm1[r:r + n, :], t[name].rearrange("(k p) -> k p", p=P)).then_inc(prm_loaded, 16)
            act.dma_start(prm2[:, :], t["m_conv_w"].rearrange("j (k p) -> (j k) p", p=P)).then_inc(prm_loaded, 16)

            def hi_at(b, o, step=0, i=0):
                n, slot = b + o, (b + o) % 2
                act.wait_ge(raw_loaded[slot], 16 * (n // 2 + 1) + (8 * step) * i if step else 16 * (n // 2 + 1))
                if n >= 2:
                    act.wait_ge(block_done, (n - 1) + step * i if step else n - 1)
                nc.scalar.activation(w_hi[slot][:, :], w_raw[slot][:, :], ACT.Copy).then_inc(hi_made, 1)

            def norm_r(s):
                act.wait_ge(s.sum_ready, 1)
                nc.scalar.activation(lnv[:, :], pair[1][:, 0, :], ACT.Ln, bias=eps_c[:, 0:1],
                                     scale=1.0 / D).then_inc(s.ln_made, 1)
                act.wait_ge(s.ln_made, 1)
                nc.scalar.activation(rinv[:, :], lnv[:, :], ACT.Exp, scale=-0.5).then_inc(s.r_made, 1)

            def norm_hi(s):
                norm_r(s)
                for k in range(KD):
                    act.wait_ge(s.raw_made, k + 1)
                    nc.scalar.activation(h_hi[:, k, :], sq[:, k, :], ACT.Copy).then_inc(s.hi_made, 1)

            def square_pair(s, g, x_sem):
                act.wait_ge(x_sem, g + 1)
                if g >= 2:
                    act.wait_ge(s.summed, g - 1)
                nc.scalar.activation(sq_pair[g % 2][:, :, :], xT[:, 2 * g:2 * g + 2, :], ACT.Square)\
                    .then_inc(s.sq_made, 1)

            def bias_step(i):
                act.wait_ge(bias_summed, i + 1)
                if not isinstance(i, int) or i:
                    act.wait_ge(bias_stored, 64 * i)
                nc.scalar.activation(bias_out[:, :], pair[3][:, 0, :], ACT.Identity,
                                     bias=rb_base).then_inc(bias_made, 1)
                act.wait_ge(bias_made, i + 1)
                for j in range(4):
                    act.dma_start(bias_dram[:, bass.ds(i * QSTEP + 4 * j, 4), :],
                                  bias_out[j * 32:(j + 1) * 32, :].rearrange("p (q c) -> p q c", q=4))\
                        .then_inc(bias_stored, 16)

            def gate_up_act(s, b, i, bias):
                act.wait_ge(block_done, b + 1 + 2 * i)
                nc.scalar.activation(gate_s[:, :, :], pair[0][:, :, :], ACT.Silu).then_inc(s.gate_made, 1)
                hi_at(b, 2, 2, i)
                if bias:
                    bias_step(2 * i)
                act.wait_ge(s.act_made, i + 1)
                nc.scalar.activation(act_hi[:, bass.ds(2 * i, 2), :], act_f[:, :, :], ACT.Copy)\
                    .then_inc(s.act_hi, 1)
                hi_at(b, 3, 2, i)
                if bias:
                    bias_step(2 * i + 1)

            def ffn_act(s, n_next, bias=False):
                b = q.block
                gate_up_act(s, b, 0, bias)
                with act.Fori(1, F // COLS) as i:
                    gate_up_act(s, b, i, bias)
                q.block = b + 2 * (F // COLS)
                for g in range(4):
                    for c in range(3):
                        if g == 3 and c == 2:
                            square_pair(n_next, g, s.x_added)
                        next_hi()
                        step = 22 + 3 * g + c
                        if bias and step < BSTEPS:
                            bias_step(step)
                    if g < 3:
                        square_pair(n_next, g, s.x_added)

            def next_hi():
                if q.block + 2 < TOTAL:
                    hi_at(q.block + 2, 0)
                q.block += 1

            def done(k=0):
                act.wait_ge(block_done, q.block + 1 + k)

            chain = [0]

            def link(ins):
                chain[0] += 1
                ins.then_inc(chain_a, 1)
                act.wait_ge(chain_a, chain[0])

            def gates_act():
                for j in range(2):
                    act.dma_start(smalls[0:M_HEADS, j:j + 1],
                                  t["b_if"][j * M_HEADS:(j + 1) * M_HEADS].rearrange("(h a) -> h a", a=1))\
                        .then_inc(bif_loaded, 16)
                act.wait_ge(bif_loaded, 32)
                done()
                nc.scalar.activation(g_i[:, :], pair[2][0:M_HEADS, 0, :], ACT.Identity, bias=smalls[0:M_HEADS, 0:1])
                nc.scalar.activation(g_f[:, :], pair[2][0:M_HEADS, 1, :], ACT.Identity, bias=smalls[0:M_HEADS, 1:2])
                link(nc.scalar.activation(g_abs[:, :], pair[2][0:M_HEADS, 1, :], ACT.Abs, bias=smalls[0:M_HEADS, 1:2]))
                link(nc.scalar.activation(g_abs[:, :], g_abs[:, :], ACT.Exp, scale=-1.0))
                nc.scalar.activation(g_ln[:, :], g_abs[:, :], ACT.Ln, bias=ones[0:M_HEADS, 0:1]).then_inc(g_pre, 1)
                next_hi()
                act.wait_ge(g_arg, 1)
                nc.scalar.activation(dec_row[:, :], dec_row[:, :], ACT.Exp).then_inc(g_exp, 1)
                nc.scalar.activation(g_rows[:, 1:4, :], g_rows[:, 1:4, :], ACT.Exp).then_inc(g_exp, 1)

            def xm_act(h, m):
                done()
                nc.scalar.activation(xm_f[:, 2 * m:2 * m + 2, 3:3 + S], pair[m][:, :, :], ACT.Copy)
                nc.scalar.activation(xm_hi[:, 2 * m:2 * m + 2, :], pair[m][:, :, :], ACT.Copy).then_inc(xmh_made, 1)
                next_hi()

            def head_act(h):
                if h == 0:
                    xm_act(0, 0)
                    xm_act(0, 1)
                act.wait_ge(conv_made, h + 1)
                link(nc.scalar.activation(conv[:, :, :], conv[:, :, :], ACT.Silu))
                nc.scalar.activation(xc_hi[:, :, :], conv[:, :, :], ACT.Copy).then_inc(xc_made, 1)
                def o_act(m):
                    nc.scalar.activation(o_sig[:, 2 * m:2 * m + 2, :], pair[O_PAIR[m]][:, :, :], ACT.Sigmoid)\
                        .then_inc(o_made, 1)

                done()
                for j in range(2):
                    nc.scalar.activation(v_f[:, 2 * j:2 * j + 2, :], pair[j][:, :, :], ACT.Copy).then_inc(v_made, 1)
                next_hi()
                done()
                o_act(0)
                next_hi()
                next_hi()
                done()
                for j in range(2):
                    nc.scalar.activation(q_f[:, 2 * j:2 * j + 2, :], pair[2 + j][:, :, :], ACT.Copy).then_inc(q_made, 1)
                next_hi()
                act.wait_ge(w_arg, h + 1)
                nc.scalar.activation(w_in_tr[:, :, :], w_in_tr[:, :, :], ACT.Exp).then_inc(w_made, 1)
                done()
                o_act(1)
                for c in range(CHUNKS - 1):
                    act.wait_ge(kt_ready, 3 * h + c + 1)
                    nc.scalar.activation(k_ws[:, c, :], pair[KT_BANK[c] // 2][:, KT_BANK[c] % 2, :], ACT.Copy,
                                         scale=tokp[:, 3, c, h:h + 1]).then_inc(kws_made, 1)
                next_hi()
                for c in range(CHUNKS):
                    g = CHUNKS * h + c
                    act.wait_ge(r_made, g + 1)
                    nc.scalar.activation(h_m[:, c, :], pair[2 + c % 2][:, 1, :], ACT.Copy,
                                         scale=den[:, 8 * (c % 2) + 4:8 * (c % 2) + 5]).then_inc(h_part, 1)
                    if c > 0:
                        act.wait_ge(h_made, 3 * h + c)
                    else:
                        act.wait_ge(h_part, g + 1)
                    link(nc.scalar.activation(h_sq[:, :], h_m[:, c, :], ACT.Square, accum_out=sumsq[:, c:c + 1]))
                link(nc.scalar.activation(sumsq, sumsq, ACT.Ln, bias=eps_c[:, 0:1], scale=1.0 / M_HD))
                link(nc.scalar.activation(sumsq, sumsq, ACT.Exp, scale=-0.5))
                for c in range(CHUNKS):
                    nc.scalar.activation(h_m[:, c, :], h_m[:, c, :], ACT.Copy, scale=sumsq[:, c:c + 1])\
                        .then_inc(hn_made, 1)
                if h < M_HEADS - 1:
                    xm_act(h + 1, 0)
                else:
                    gate_m_act(0)
                for e in range(MK):
                    act.wait_ge(yf_made, MK * h + e + 1)
                    nc.scalar.activation(ym_hi[:, e, :], y_f[e % 2][:, :], ACT.Copy).then_inc(ymh_made, 1)
                if h < M_HEADS - 1:
                    xm_act(h + 1, 1)
                else:
                    gate_m_act(1)
                next_hi()
                next_hi()

            def gate_m_act(m):
                done()
                for j in range(2):
                    ins = nc.scalar.activation(g_sig_m[:, 2 * m + j, :], pair[m % 2][:, j, :], ACT.Sigmoid,
                                               bias=pcol("b_gate", 2 * m + j))
                ins.then_inc(g_sig_made, 1)
                next_hi()

            def memory_act():
                for k in range(KD):
                    act.wait_ge(memn_made, k + 1)
                    nc.scalar.activation(memn_hi[:, k, :], memn_f[:, k, :], ACT.Copy).then_inc(memh_made, 1)

            def gate_sigmoid(gate, base, m):
                act.wait_ge(mg_made, base + m)
                for j in range(2):
                    ins = nc.scalar.activation(g_sig[:, j, :], pair[2 * (m % 2)][:, j, :], ACT.Sigmoid,
                                               bias=pcol("b_gate", 8 * gate + 2 * m + j))
                ins.then_inc(g_sig_made, 1)

            def merge_act(gate, base, split=False):
                gate_sigmoid(gate, base, 0)
                for m in range(4):
                    if m < 3:
                        next_hi()
                    next_hi()
                    if m < 3:
                        gate_sigmoid(gate, base, m + 1)
                    if split:
                        act.wait_ge(mg_made, base + m + 1)
                        nc.scalar.activation(mg_hi[:, 2 * m:2 * m + 2, :], merged[:, 2 * m:2 * m + 2, :], ACT.Copy)\
                            .then_inc(mgh_made, 1)

            def attention_act():
                act.wait_ge(lam_summed, 1)
                nc.scalar.activation(smalls[:, 2:4], pair[3][:, 1, 0:2], ACT.Exp).then_inc(g_exp, 1)
                for nh in range(2):
                    next_hi()
                    done()
                    for j in range(2):
                        nc.scalar.activation(va[:, 2 * j:2 * j + 2, nh * WIDE:(nh + 1) * WIDE],
                                             pair[2 * nh + j][:, :, :], ACT.Copy).then_inc(va_made, 1)
                    next_hi()
                done()
                nc.scalar.activation(q_a[0][:, :, :], pair[0][:, :, :], ACT.Copy).then_inc(qa_made, 1)
                next_hi()
                next_hi()

                def exps(u):
                    b = u % 2
                    for j in range(2):
                        act.wait_ge(a_shifted, 2 * u + j + 1)
                        nc.scalar.activation(probs[b][:, j, :], probs[b][:, j, :], ACT.Exp,
                                             bias=smalls[:, 8 + 2 * b + j:9 + 2 * b + j], scale=A_SCALE,
                                             accum_out=smalls[:, 12 + 2 * b + j:13 + 2 * b + j]).then_inc(a_exp, 1)

                def head_square(e):
                    act.wait_ge(a_out, e + 1)
                    if e:
                        act.wait_ge(a_yl, e)
                    nc.scalar.activation(y_af[:, :], pair[1][:, 1, :], ACT.Copy)
                    nc.scalar.activation(o_sq[:, :], pair[1][:, 1, :], ACT.Square).then_inc(a_sq, 1)

                def head_rms(e, memory=False):
                    act.wait_ge(a_sum, e + 1)
                    if memory:
                        nc.scalar.activation(smalls[:, 20:22], smalls[:, 20:22], ACT.Ln, bias=eps_c[:, 0:1],
                                             scale=1.0 / D)
                    link(nc.scalar.activation(o_sq[:, :], pair[1][:, 1, :], ACT.Ln, bias=eps_c[:, 0:1],
                                              scale=1.0 / P))
                    nc.scalar.activation(o_sq[:, :], o_sq[:, :], ACT.Exp, scale=-0.5).then_inc(a_r, 1)
                    if memory:
                        link(nc.scalar.activation(smalls[:, 20:22], smalls[:, 20:22], ACT.Exp, scale=-0.5))

                def head_hi(e):
                    act.wait_ge(a_y, e + 1)
                    nc.scalar.activation(ya_hi[:, e, :], y_af[:, :], ACT.Copy).then_inc(a_yh, 1)

                exps(0)
                for u in range(4 * A_HEADS):
                    e, hp = u // 4 - 1, u // 8
                    if u + 1 < 4 * A_HEADS:
                        exps(u + 1)
                    if u % 8 == QA_UNIT + 1 or (u % 8 == 0 and u):
                        next_hi()
                    if u % 4 == 0 and e >= 0:
                        head_square(e)
                    if u % 8 == QA_UNIT and hp < 3:
                        done()
                        nc.scalar.activation(q_a[(hp + 1) % 2][:, :, :], pair[0][:, :, :], ACT.Copy)\
                            .then_inc(qa_made, 1)
                    act.wait_ge(a_turned, u + 1)
                    nc.scalar.activation(a_tr[:, :, (u % 4) * P:(u % 4 + 1) * P],
                                         pair[1][:, 0, :].rearrange("p (k c) -> p k c", k=NT),
                                         ACT.Copy).then_inc(a_tr_made, 1)
                    if u % 4 == 1 and e >= 0:
                        head_rms(e, memory=u == 25)
                    if u % 4 == 2 and e >= 0:
                        head_hi(e)
                    if u == 22:
                        act.wait_ge(a_scored, 24)
                        act.dma_start(mem_tok[:, :, :], t["mem"].rearrange("(a p) d -> p a d", p=P))\
                            .then_inc(mem_loaded, 16)
                    if u == 24:
                        act.wait_ge(mem_loaded, 16)
                        for a in range(MT):
                            link(nc.scalar.activation(mem_sq[:, :], mem_tok[:, a, :], ACT.Square,
                                                      accum_out=smalls[:, 20 + a:21 + a]))
                    if u in (26, 27):
                        a = u - 26
                        nc.scalar.activation(mem_tok[:, a, :], mem_tok[:, a, :], ACT.Copy,
                                             scale=smalls[:, 20 + a:21 + a]).then_inc(mem_r, 1)
                head_square(A_HEADS - 1)
                head_rms(A_HEADS - 1)
                head_hi(A_HEADS - 1)

            def cross_act():
                for m in range(4):
                    done()
                    nc.scalar.activation(k_x[:, 2 * m:2 * m + 2, :], pair[m % 2][:, :, 0:MEM], ACT.Copy)\
                        .then_inc(kx_made, 1)
                    next_hi()
                for nh in range(2):
                    next_hi()
                    done()
                    nc.scalar.activation(v_x[:, :, nh * WIDE:(nh + 1) * WIDE], pair[2 + nh][:, :, :], ACT.Copy)\
                        .then_inc(vx_made, 1)
                    next_hi()
                def qx_act(m):
                    done()
                    nc.scalar.activation(q_x[:, 2 * m:2 * m + 2, :], pair[m % 2][:, :, :], ACT.Copy)\
                        .then_inc(qx_made, 1)

                def exps(u):
                    act.wait_ge(x_max, u + 1)
                    nc.scalar.activation(p_x[u % 2][:, :], pair[2][:, u % 2, 0:MEM], ACT.Exp,
                                         bias=smalls[:, 24 + u % 2:25 + u % 2], scale=X_SCALE,
                                         accum_out=smalls[:, 26 + u % 2:27 + u % 2]).then_inc(x_exp, 1)

                def head_hi(h):
                    act.wait_ge(x_out, h + 1)
                    nc.scalar.activation(yx_hi[:, 2 * h:2 * h + 2, :], pair[X_OUT_PAIR[h]][:, :, :], ACT.Copy)\
                        .then_inc(x_yh, 1)

                qx_act(0)
                next_hi()
                exps(0)
                for u in range(4 * X_HEADS):
                    h = u // 4
                    if u + 1 < 4 * X_HEADS:
                        exps(u + 1)
                    if u % 4 == 0 and u:
                        next_hi()
                        head_hi(h - 1)
                    if u % 4 == QX_UNIT and h < X_HEADS - 1:
                        qx_act(h + 1)
                    act.wait_ge(x_turned, u + 1)
                    nc.scalar.activation(p_tr[:, :, (u % 4) * P:(u % 4 + 1) * P],
                                         pair[3][:, u % 2, 0:MEM].rearrange("p (k c) -> p k c", k=MT),
                                         ACT.Copy).then_inc(x_tr_made, 1)
                head_hi(X_HEADS - 1)
                next_hi()

            def out_act():
                for m in range(4):
                    if m < 3:
                        next_hi()
                    square_pair(n_ffn[1], m, x_mixed)
                next_hi()

            for g in range(4):
                act.wait_ge(xt_made, 2 * g + 2)
                nc.scalar.activation(sq[:, 2 * g:2 * g + 2, :], xT[:, 2 * g:2 * g + 2, :], ACT.Square)\
                    .then_inc(n_ffn[0].sq_made, 1)
            hi_at(0, 0)
            norm_hi(n_ffn[0])
            hi_at(0, 1)
            act.wait_ge(thr_loaded, 16 * 29)
            act.wait_ge(pos_made, 2)
            ffn_act(ffn[0], n_mix, bias=True)
            norm_hi(n_mix)
            gates_act()
            for h in range(M_HEADS):
                head_act(h)
            gate_m_act(2)
            gate_m_act(3)
            attention_act()
            memory_act()
            merge_act(1, 4)
            cross_act()
            merge_act(2, 8, split=True)
            out_act()
            norm_hi(n_ffn[1])
            ffn_act(ffn[1], n_fin)
            norm_r(n_fin)
            for a in range(NT):
                act.wait_ge(out_turned, a + 1)
                nc.scalar.activation(o_tok[:, a, 0:D // 2], pair[a][:, 0, :], ACT.Copy).then_inc(out_lo_made, 1)

        @block.vector
        def _(dve):
            q = Progress()
            def fold(s, g, squares):
                dve.wait_ge(s.sq_made, g + 1)
                nc.vector.tensor_tensor(squares[:, 0, :], squares[:, 0, :], squares[:, 1, :], ALU.add)\
                    .then_inc(s.folded, 1)

            for k in range(KD):
                dve.wait_ge(xt_turned, k + 1)
                nc.vector.tensor_copy(xT[:, k, :], pair[2 * (k // 2 % 2)][:, k % 2, :]).then_inc(xt_made, 1)
                if k % 2 and k > 1:
                    fold(n_ffn[0], k // 2 - 1, sq[:, k - 3:k - 1, :])
            fold(n_ffn[0], 3, sq[:, 6:8, :])
            def lo_at(b, o, step=0, i=0):
                n, slot = b + o, (b + o) % 2
                dve.wait_ge(hi_made, (n + 1) + step * i if step else n + 1)
                nc.vector.tensor_tensor(w_lo[slot][:, :], w_raw[slot][:, :], w_hi[slot][:, :].bitcast(F32),
                                        ALU.subtract).then_inc(lo_made, 1)

            def norm_raw(s, gain, k):
                nc.vector.scalar_tensor_tensor(out=sq[:, k, :], in0=xT[:, k, :], scalar=pcol(gain, k),
                                               in1=rinv[:, :], op0=ALU.mult, op1=ALU.mult)\
                    .then_inc(s.raw_made, 1)

            def norm_split(s, gain):
                dve.wait_ge(s.r_made, 1)
                norm_raw(s, gain, 0)
                for k in range(KD):
                    if k + 1 < KD:
                        norm_raw(s, gain, k + 1)
                    dve.wait_ge(s.hi_made, k + 1)
                    nc.vector.tensor_tensor(h_lo[:, k, :], sq[:, k, :], h_hi[:, k, :].bitcast(F32),
                                            ALU.subtract).then_inc(s.ready, 1)

            def bias_step(i, slot):
                if not isinstance(i, int) or i >= 2:
                    dve.wait_ge(bias_summed, i - 1)
                nc.vector.tensor_tensor(past[slot][:, :, :],
                                        pq_s[:, bass.ds(i * QSTEP, QSTEP)].unsqueeze(2)
                                        .to_broadcast([P, QSTEP, KEYS4]),
                                        pk_s[:, :].unsqueeze(1).to_broadcast([P, QSTEP, KEYS4]),
                                        ALU.is_ge).then_inc(past_made, 1)

            def gate_up_dve(s, b, i, bias):
                lo_at(b, 2, 2, i)
                if bias:
                    bias_step(2 * i + 1, 1)
                dve.wait_ge(block_done, b + 2 + 2 * i)
                dve.wait_ge(s.gate_made, i + 1)
                nc.vector.tensor_tensor(act_f[:, :, :], gate_s[:, :, :], pair[1][:, :, :], ALU.mult)\
                    .then_inc(s.act_made, 1)
                dve.wait_ge(s.act_hi, i + 1)
                nc.vector.tensor_tensor(act_lo[:, bass.ds(2 * i, 2), :], act_f[:, :, :],
                                        act_hi[:, bass.ds(2 * i, 2), :].bitcast(F32), ALU.subtract)\
                    .then_inc(s.act_ready, 1)
                lo_at(b, 3, 2, i)
                if bias:
                    bias_step(2 * i + 2, 0)

            def ffn_dve(s, n_next, bias=False):
                b = q.block
                if bias:
                    bias_step(0, 0)
                gate_up_dve(s, b, 0, bias)
                with dve.Fori(1, F // COLS) as i:
                    gate_up_dve(s, b, i, bias)
                q.block = b + 2 * (F // COLS)
                for g in range(4):
                    for c in range(3):
                        if c == 2:
                            done()
                            xs = xT[:, 2 * g:2 * g + 2, :]
                            nc.vector.scalar_tensor_tensor(out=xs, in0=pair[DOWN_PAIR[g]][:, :, :], scalar=0.5,
                                                           in1=xs, op0=ALU.mult, op1=ALU.add)\
                                .then_inc(s.x_added, 1)
                            if g == 3:
                                fold(n_next, 3, sq_pair[1])
                        next_lo()
                        if c == 0 and g:
                            fold(n_next, g - 1, sq_pair[(g - 1) % 2])
                        step = 23 + 3 * g + c
                        if bias and step < BSTEPS:
                            bias_step(step, step % 2)

            def next_lo():
                if q.block + 2 < TOTAL:
                    lo_at(q.block + 2, 0)
                q.block += 1

            def done(k=0):
                dve.wait_ge(block_done, q.block + 1 + k)

            chain = [0]

            def link(ins):
                chain[0] += 1
                ins.then_inc(chain_d, 1)
                dve.wait_ge(chain_d, chain[0])

            def positions_dve():
                v = nc.vector
                dve.wait_ge(pos_loaded, 16)
                v.tensor_scalar(pos_h[:, :], pos_i[:, :], 16, None, ALU.arith_shift_right)
                link(v.tensor_scalar(pos_l[:, :], pos_i[:, :], 65535, None, ALU.bitwise_and))
                v.tensor_copy(pos_hf[:, :], pos_h[:, :])
                link(v.tensor_copy(pos_lf[:, :], pos_l[:, :]))
                link(v.tensor_copy(smalls[0:1, 4:5], pos_hf[:, 0:1]))
                link(v.tensor_copy(smalls[0:1, 5:6], pos_lf[:, 0:1]))
                link(v.tensor_scalar(pos_hf[:, :], pos_hf[:, :], smalls[0:1, 4:5], None, ALU.subtract))
                link(v.tensor_scalar(pos_lf[:, :], pos_lf[:, :], smalls[0:1, 5:6], None, ALU.subtract))
                link(v.memset(sign_row[:, :], 1.0))
                link(v.memset(sign_row[:, 0:P:BUCKETS], -1.0))
                v.scalar_tensor_tensor(out=pos_r[:, :], in0=pos_hf[:, :], scalar=65536.0, in1=pos_lf[:, :],
                                       op0=ALU.mult, op1=ALU.add).then_inc(pos_made, 1)

            def bias_dve():
                v = nc.vector
                dve.wait_ge(thr_loaded, 16 * 29)
                link(v.tensor_tensor(rb_cur[:, :], rb_cur[:, :], rb_prev[:, :], ALU.subtract))
                link(v.tensor_scalar(rb_cur[:, :], rb_cur[:, :], 1.0 / A_SCALE, None, ALU.mult))
                for k in range(4):
                    link(v.memset(rb_cur[k * BUCKETS:k * BUCKETS + 1, :], HIDE))
                v.tensor_scalar(rb_base, rb_base, 1.0 / A_SCALE, None, ALU.mult).then_inc(pos_made, 1)
                link(v.memset(step_f[:, :], 0.0))
                for k in range(4):
                    ins = v.tensor_copy(step_f[k * BUCKETS:(k + 1) * BUCKETS, k:32:4],
                                        rb_cur[k * BUCKETS:(k + 1) * BUCKETS, :])
                link(ins)
                for part in range(3):
                    link(v.tensor_copy(step_b[part][:, :], step_f[:, :]))
                    if part < 2:
                        link(v.tensor_tensor(step_f[:, :], step_f[:, :], step_b[part][:, :], ALU.subtract))
                dve.wait_ge(pos_spread, 1)
                v.tensor_scalar(pq_s[:, :], pair[2][:, 0, :], thr[:, 0:1], None, ALU.subtract)
                for k in range(4):
                    r = slice(k * BUCKETS, (k + 1) * BUCKETS)
                    ins = v.tensor_copy(pk_s[r, :], pair[2][r, 0, k * KEYS4:(k + 1) * KEYS4])
                link(ins)

            def gates_dve():
                dve.wait_ge(bias_stored, 64 * BSTEPS)
                v = nc.vector
                link(v.memset(one_row[:, :], 1.0))
                dve.wait_ge(g_pre, 1)
                link(v.scalar_tensor_tensor(out=g_lf[:, :], in0=g_f[:, :], scalar=0.0, in1=g_ln[:, :],
                                            op0=ALU.min, op1=ALU.subtract))
                link(v.tensor_tensor_scan(g_b[:, :], one_row[:, :], g_lf[:, :], 0.0, ALU.mult, ALU.add))
                c_row = g_rows[:, 0, :]
                link(v.tensor_tensor(c_row, g_i[:, :], g_b[:, :], ALU.subtract))
                link(v.tensor_tensor_scan(g_m[:, :], c_row, c_row, 0.0, ALU.max, ALU.max))
                link(v.tensor_scalar(g_neg[:, :], g_m[:, :], -1.0, None, ALU.mult))
                v.memset(g_rows[:, 1, 0:P], 0.0)
                v.memset(g_rows[:, 3, S - P:S], 0.0)
                v.tensor_tensor(g_rows[:, 2, :], g_neg[:, :], g_b[:, :], ALU.subtract)
                for c in range(1, CHUNKS):
                    v.tensor_scalar(g_rows[:, 1, c * P:(c + 1) * P], g_neg[:, c * P:(c + 1) * P],
                                    g_m[:, c * P - 1:c * P], None, ALU.add)
                    v.tensor_scalar(g_rows[:, 3, (c - 1) * P:c * P], g_rows[:, 0, (c - 1) * P:c * P],
                                    g_m[:, c * P - 1:c * P], None, ALU.subtract)
                v.tensor_tensor(dec_row[:, :], g_m[:, P - 1:3 * P - 1:P], g_m[:, 2 * P - 1:4 * P - 1:P], ALU.subtract)\
                    .then_inc(g_arg, 1)
                next_lo()
                dve.wait_ge(g_exp, 1)
                for c in range(2):
                    ins = v.tensor_scalar(dec_diag[:, c, :], ident[0:M_HEADS, 0:M_HEADS], dec_row[:, c:c + 1], None,
                                          ALU.mult)
                ins.then_inc(g_diag, 1)
                link(v.memset(xm_f[:, :, 0:3], 0.0))

            def gates_turn_dve():
                dve.wait_ge(g_turned, 1)
                nc.vector.tensor_copy(decay, pair[3][:, 1, 0:8])
                nc.vector.tensor_copy(tokp[:, :, :, :].rearrange("p a c h -> p (a c h)"), pair[3][:, 0, 0:64])\
                    .then_inc(g_ready, 1)

            def xm_lo_dve(h, m):
                dve.wait_ge(xmh_made, 2 * h + m + 1)
                nc.vector.tensor_tensor(xm_lo[:, 2 * m:2 * m + 2, :], xm_f[:, 2 * m:2 * m + 2, 3:3 + S],
                                        xm_hi[:, 2 * m:2 * m + 2, :].bitcast(F32), ALU.subtract)\
                    .then_inc(xml_made, 1)

            def conv_tap(h, tap):
                v = nc.vector
                if tap != 3:
                    dve.wait_ge(chain_d, chain[0])
                for e in range(MK):
                    w = pcol("m_conv_w", 16 * tap + MK * h + e)
                    if tap == 3:
                        ins = v.tensor_scalar(conv[:, e, :], xm_f[:, e, 3:3 + S], w, pcol("m_conv_b", MK * h + e),
                                              ALU.mult, ALU.add)
                    else:
                        ins = v.scalar_tensor_tensor(out=conv[:, e, :], in0=xm_f[:, e, tap:tap + S], scalar=w,
                                                     in1=conv[:, e, :], op0=ALU.mult, op1=ALU.add)
                if tap == 2:
                    ins.then_inc(conv_made, 1)
                else:
                    chain[0] += 1
                    ins.then_inc(chain_d, 1)

            def head_dve(h):
                v = nc.vector
                if h == 0:
                    for m in range(2):
                        xm_lo_dve(0, m)
                        next_lo()
                    for tap in (3, 0, 1, 2):
                        conv_tap(0, tap)
                dve.wait_ge(xc_made, h + 1)
                v.tensor_tensor(xc_lo[:, :, :], conv[:, :, :], xc_hi[:, :, :].bitcast(F32), ALU.subtract)\
                    .then_inc(xcl_made, 1)
                next_lo()
                if h == 0:
                    gates_turn_dve()
                next_lo()
                done()
                for j in range(2):
                    v.tensor_scalar(k_f[:, 2 * j:2 * j + 2, :], pair[j][:, :, :], M_HD ** -0.5, None, ALU.mult)\
                        .then_inc(k_made, 1)
                next_lo()
                next_lo()
                dve.wait_ge(negm_spread, h + 1)
                for c in range(CHUNKS):
                    ins = v.scalar_tensor_tensor(out=w_in_tr[:, c, :], in0=pair[1][:, 0, c * P:(c + 1) * P],
                                                 scalar=tokp[:, 0, c, h:h + 1], in1=mask[:, :],
                                                 op0=ALU.add, op1=ALU.add)
                ins.then_inc(w_arg, 1)
                dve.wait_ge(w_made, h + 1)
                dve.wait_ge(sc_ready, h + 1)
                v.tensor_tensor(s_w[:, :, :], pair[2][:, 0, :].rearrange("p (c t) -> p c t", c=CHUNKS),
                                w_in_tr[:, :, :], ALU.mult).then_inc(sw_made, 1)
                next_lo()
                small = pair[3][:, 0, :]
                for c in range(CHUNKS):
                    g = CHUNKS * h + c
                    d = den[:, 8 * (c % 2):8 * (c % 2) + 8]
                    if c < CHUNKS - 1:
                        new_c, old_c = c_st[c % 2], c_st[1 - c % 2]
                        new_n, old_n = n_st[c % 2], n_st[1 - c % 2]
                        if c == 2:
                            dve.wait_ge(num_ready, g)
                        for half in range(2):
                            dve.wait_ge(upd_ready, 2 * (3 * h + c) + half + 1)
                            hs = slice(2 * half, 2 * half + 2)
                            dk = decay[:, (c - 1) * M_HEADS + h:(c - 1) * M_HEADS + h + 1] if c else None
                            if half:
                                if c == 0:
                                    v.tensor_copy(new_n, small[:, 0:MK]).then_inc(n_made, 1)
                                else:
                                    v.scalar_tensor_tensor(out=new_n, in0=old_n, scalar=dk, in1=small[:, 0:MK],
                                                           op0=ALU.mult, op1=ALU.add).then_inc(n_made, 1)
                            if c == 0:
                                v.tensor_copy(new_c[:, hs, :], pair[half][:, :, :]).then_inc(c_made, 1)
                            else:
                                v.scalar_tensor_tensor(out=new_c[:, hs, :], in0=old_c[:, hs, :], scalar=dk,
                                                       in1=pair[half][:, :, :], op0=ALU.mult, op1=ALU.add)\
                                    .then_inc(c_made, 1)
                    dve.wait_ge(num_ready, g + 1)
                    if c == 0:
                        link(v.tensor_copy(d[:, 0:1], small[:, 4:5]))
                    else:
                        link(v.tensor_copy(d[:, 1:2], small[:, 4:5]))
                        link(v.scalar_tensor_tensor(out=d[:, 0:1], in0=small[:, 5:6],
                                                    scalar=tokp[:, 1, c, h:h + 1], in1=d[:, 1:2],
                                                    op0=ALU.mult, op1=ALU.add))
                    link(v.tensor_scalar(d[:, 3:4], d[:, 0:1], -1.0, tokp[:, 2, c, h:h + 1], ALU.mult, ALU.max))
                    link(v.tensor_tensor(d[:, 2:3], d[:, 0:1], d[:, 3:4], ALU.max))
                    v.reciprocal(d[:, 4:5], d[:, 2:3]).then_inc(r_made, 1)
                    if c > 0:
                        dve.wait_ge(r_made, g + 1)
                        link(v.tensor_tensor(d[:, 5:6], d[:, 4:5], tokp[:, 1, c, h:h + 1], ALU.mult))
                        dve.wait_ge(h_part, g + 1)
                        v.scalar_tensor_tensor(out=h_m[:, c, :], in0=inter(c), scalar=d[:, 5:6],
                                               in1=h_m[:, c, :], op0=ALU.mult, op1=ALU.add).then_inc(h_made, 1)
                if h < M_HEADS - 1:
                    xm_lo_dve(h + 1, 0)
                for e in range(MK):
                    dve.wait_ge(h_turned, MK * h + e + 1)
                    if e >= 2:
                        dve.wait_ge(yml_made, MK * h + e - 1)
                    v.scalar_tensor_tensor(out=y_f[e % 2][:, :], in0=pair[2 + e // 2][:, e % 2, :],
                                           scalar=pcol("m_head_norm", MK * h + e), in1=o_sig[:, e, :],
                                           op0=ALU.mult, op1=ALU.mult).then_inc(yf_made, 1)
                    if e > 0:
                        y_lo(h, e - 1)
                y_lo(h, MK - 1)
                next_lo()
                if h < M_HEADS - 1:
                    xm_lo_dve(h + 1, 1)
                next_lo()
                if h < M_HEADS - 1:
                    conv_tap(h + 1, 3)
                    conv_tap(h + 1, 0)
                for m in range(2):
                    done()
                    for j in range(2):
                        ms = merged[:, 4 * m + 2 * j:4 * m + 2 * j + 2, :]
                        if h == 0:
                            ins = v.tensor_copy(ms, pair[2 * m + j][:, :, :])
                        else:
                            ins = v.tensor_tensor(ms, ms, pair[2 * m + j][:, :, :], ALU.add)
                        ins.then_inc(bm_added, 1)
                    next_lo()
                    if h < M_HEADS - 1:
                        conv_tap(h + 1, 1 + m)

            def y_lo(h, e):
                dve.wait_ge(ymh_made, MK * h + e + 1)
                nc.vector.tensor_tensor(ym_lo[:, e, :], y_f[e % 2][:, :], ym_hi[:, e, :].bitcast(F32), ALU.subtract)\
                    .then_inc(yml_made, 1)

            def merge_m_dve():
                dve.wait_ge(bm_added, 4 * M_HEADS)
                for m in range(4):
                    ms = merged[:, 2 * m:2 * m + 2, :]
                    dve.wait_ge(g_sig_made, m + 1)
                    nc.vector.tensor_tensor(ms, ms, g_sig_m[:, 2 * m:2 * m + 2, :], ALU.mult).then_inc(mg_made, 1)
                    if m >= 2:
                        next_lo()

            def merge_dve(base, split=False):
                v = nc.vector
                for m in range(4):
                    ms = merged[:, 2 * m:2 * m + 2, :]
                    if m < 3:
                        next_lo()
                    done()
                    dve.wait_ge(g_sig_made, base + m + 1)
                    link(v.tensor_tensor(g_tmp[:, :, :], g_sig[:, :, :], pair[2 * (m % 2) + 1][:, :, :], ALU.mult))
                    v.tensor_tensor(ms, ms, g_tmp[:, :, :], ALU.add).then_inc(mg_made, 1)
                    next_lo()
                    if split:
                        dve.wait_ge(mgh_made, m + 1)
                        v.tensor_tensor(mg_lo[:, 2 * m:2 * m + 2, :], ms,
                                        mg_hi[:, 2 * m:2 * m + 2, :].bitcast(F32), ALU.subtract).then_inc(mgl_made, 1)

            def attention_dve():
                v = nc.vector
                for _ in range(4):
                    next_lo()
                dve.wait_ge(g_exp, 3)
                link(v.tensor_tensor(smalls[:, 6:7], smalls[:, 3:4], smalls[:, 2:3], ALU.subtract))
                link(v.tensor_scalar(smalls[:, 6:7], smalls[:, 6:7], -LAM_INIT, None, ALU.add))
                g0 = PC["a_head_norm"][0]
                link(v.tensor_scalar(par[:, 168:176], par[:, g0:g0 + 8], 1.0 - LAM_INIT, None, ALU.mult))
                next_lo()
                done()
                v.tensor_copy(k_a[0][:, :, :], pair[1][:, :, :]).then_inc(ka_made, 1)
                next_lo()

                def shifts(u):
                    b = u % 2
                    dve.wait_ge(a_scored, u + 1)
                    dve.wait_ge(bias_loaded[u % 4], 16 * (u // 4 + 1))
                    if u >= 2:
                        dve.wait_ge(a_turned, u - 1)
                    for j in range(2):
                        top = smalls[:, 28 + 2 * b + j:29 + 2 * b + j]
                        link(v.tensor_tensor_reduce(probs[b][:, j, :], pair[2 + b][:, j, :], bias_sb[u % 4][:, :],
                                                    1.0, HIDE * 10, ALU.add, ALU.max, top))
                        v.tensor_scalar(smalls[:, 8 + 2 * b + j:9 + 2 * b + j], top, -A_SCALE, None, ALU.mult)\
                            .then_inc(a_shifted, 1)

                def head_y(e):
                    dve.wait_ge(a_r, e + 1)
                    v.scalar_tensor_tensor(out=y_af[:, :], in0=y_af[:, :], scalar=par[:, 168 + e:169 + e],
                                           in1=o_sq[:, :], op0=ALU.mult, op1=ALU.mult).then_inc(a_y, 1)

                def head_lo(e):
                    dve.wait_ge(a_yh, e + 1)
                    v.tensor_tensor(ya_lo[:, e, :], y_af[:, :], ya_hi[:, e, :].bitcast(F32), ALU.subtract)\
                        .then_inc(a_yl, 1)

                shifts(0)
                for u in range(4 * A_HEADS):
                    b, e, hp = u % 2, u // 4 - 1, u // 8
                    if u + 1 < 4 * A_HEADS:
                        shifts(u + 1)
                    dve.wait_ge(a_exp, 2 * u + 2)
                    r = smalls[:, 16 + 2 * b:18 + 2 * b]
                    link(v.reciprocal(r, smalls[:, 12 + 2 * b:14 + 2 * b]))
                    link(v.tensor_tensor(r[:, 1:2], r[:, 1:2], smalls[:, 6:7], ALU.mult))
                    link(v.tensor_scalar(probs[b][:, 0, :], probs[b][:, 0, :], r[:, 0:1], None, ALU.mult))
                    v.scalar_tensor_tensor(out=probs[b][:, 0, :], in0=probs[b][:, 1, :], scalar=r[:, 1:2],
                                           in1=probs[b][:, 0, :], op0=ALU.mult, op1=ALU.add).then_inc(a_mixed, 1)
                    if u % 4 == 2 and e >= 0:
                        head_y(e)
                    if u % 4 == 3 and e >= 0:
                        head_lo(e)
                    if u % 8 == QA_UNIT + 1:
                        next_lo()
                    if u % 8 == KA_UNIT and hp < 3:
                        done()
                        v.tensor_copy(k_a[(hp + 1) % 2][:, :, :], pair[0][:, :, :]).then_inc(ka_made, 1)
                    if u % 8 == 0 and u:
                        next_lo()
                for k in range(KD):
                    if k % 4 == 0:
                        dve.wait_ge(mem_turned, k // 4 + 1)
                    v.tensor_scalar(memn_f[:, k, :], pair[2 + k // 4][:, k // 2 % 2, k % 2 * MEM:(k % 2 + 1) * MEM],
                                    pcol("mem_norm", k), None, ALU.mult).then_inc(memn_made, 1)
                head_y(A_HEADS - 1)
                head_lo(A_HEADS - 1)
                for k in range(KD):
                    dve.wait_ge(memh_made, k + 1)
                    v.tensor_tensor(memn_lo[:, k, :], memn_f[:, k, :], memn_hi[:, k, :].bitcast(F32), ALU.subtract)\
                        .then_inc(meml_made, 1)

            def cross_dve():
                v = nc.vector
                for _ in range(9):
                    next_lo()

                def maxima(u):
                    b = u % 2
                    dve.wait_ge(x_scored, u + 1)
                    link(v.tensor_reduce(smalls[:, 28 + b:29 + b], pair[2][:, b, 0:MEM], AX.X, ALU.max))
                    v.tensor_scalar(smalls[:, 24 + b:25 + b], smalls[:, 28 + b:29 + b], -X_SCALE, None, ALU.mult)\
                        .then_inc(x_max, 1)

                def head_lo(h):
                    dve.wait_ge(x_yh, h + 1)
                    v.tensor_tensor(yx_lo[:, 2 * h:2 * h + 2, :], pair[X_OUT_PAIR[h]][:, :, :],
                                    yx_hi[:, 2 * h:2 * h + 2, :].bitcast(F32), ALU.subtract).then_inc(x_yl, 1)

                maxima(0)
                for u in range(4 * X_HEADS):
                    b = u % 2
                    if u + 1 < 4 * X_HEADS:
                        maxima(u + 1)
                    dve.wait_ge(x_exp, u + 1)
                    link(v.reciprocal(smalls[:, 30 + b:31 + b], smalls[:, 26 + b:27 + b]))
                    v.tensor_scalar(p_x[b][:, :], p_x[b][:, :], smalls[:, 30 + b:31 + b], None, ALU.mult).then_inc(x_norm, 1)
                    if u % 4 == 0 and u:
                        next_lo()
                        head_lo(u // 4 - 1)
                head_lo(X_HEADS - 1)
                next_lo()

            def out_dve():
                v = nc.vector
                for m in range(4):
                    done()
                    xs = xT[:, 2 * m:2 * m + 2, :]
                    v.tensor_tensor(xs, xs, pair[2 + m % 2][:, :, :], ALU.add).then_inc(x_mixed, 1)
                    if m < 3:
                        next_lo()
                    fold(n_ffn[1], m, sq_pair[m % 2])
                next_lo()

            dve.wait_ge(par_turned, 1)
            nc.vector.tensor_copy(par[:, 0:104], pair[3][:, 0, 0:104])
            nc.vector.tensor_copy(par[:, 104:168], pair[3][:, 0, 128:192]).then_inc(par_made, 1)
            positions_dve()
            lo_at(0, 0)
            dve.wait_ge(par_made, 1)
            norm_split(n_ffn[0], "ffn1_norm")
            lo_at(0, 1)
            bias_dve()
            ffn_dve(ffn[0], n_mix, bias=True)
            norm_split(n_mix, "mix_norm")
            gates_dve()
            for h in range(M_HEADS):
                head_dve(h)
            merge_m_dve()
            attention_dve()
            merge_dve(4)
            cross_dve()
            merge_dve(8, split=True)
            out_dve()
            norm_split(n_ffn[1], "ffn2_norm")
            ffn_dve(ffn[1], n_fin)
            dve.wait_ge(n_fin.r_made, 1)
            for k in range(KD):
                norm_raw(n_fin, "final_norm", k)
            for a in range(NT):
                dve.wait_ge(out_turned, NT + a + 1)
                nc.vector.tensor_copy(o_tok[:, a, D // 2:D], pair[a][:, 1, :]).then_inc(out_hi_made, 1)

        @block.tensor
        def _(pe):
            q = Progress()
            pe.wait_ge(consts_made, 4)
            for k in range(KD):
                if k % 4 == 0:
                    pe.wait_ge(x_loaded[k // 4], 16)
                if k >= 4:
                    pe.wait_ge(xt_made, k - 3)
                for a in range(NT):
                    last = nc.tensor.transpose(pair[2 * (k // 2 % 2)][:, k % 2, a * P:(a + 1) * P],
                                               x_tok[:, a, k * P:(k + 1) * P], ident[:, :])
                last.then_inc(xt_turned, 1)
            def sum_pair(s, g, src):
                pe.wait_ge(s.folded, g + 1)
                nc.tensor.matmul(pair[1][:, 0, :], ones[:, :], src[:, 0, :], start=g == 0, stop=g == 3).then_inc(s.sum_ready if g == 3 else s.summed, 1)

            def product(out, w_h, w_l, x_h, x_l, first, last):
                nc.tensor.matmul(out, w_h, x_h, start=first, stop=False)
                nc.tensor.matmul(out, w_h, x_l, start=False, stop=False)
                return nc.tensor.matmul(out, w_l, x_h, start=False, stop=last)

            def narrow_block(slot, out, xs_hi, xs_lo, x0, kts, first, last, ready=None):
                wh = w_hi[slot][:, 0:kts * COLS].rearrange("p (k c) -> p k c", c=COLS)
                wl = w_lo[slot][:, 0:kts * COLS].rearrange("p (k c) -> p k c", c=COLS)
                for k in range(kts):
                    if ready and k % ready[1] == 0:
                        pe.wait_ge(ready[0], k // ready[1] + 1)
                    for j in range(2):
                        mm = product(out[:, j, :], wh[:, k, j * P:(j + 1) * P], wl[:, k, j * P:(j + 1) * P],
                                     xs_hi[:, x0 + k, :], xs_lo[:, x0 + k, :],
                                     first and k == 0, last and k == kts - 1)
                mm.then_inc(block_done, 1)

            def bias_step(i, slot):
                pe.wait_ge(past_made, i + 1)
                if not isinstance(i, int) or i:
                    pe.wait_ge(bias_made, i)
                for j in range(4):
                    for part in range(3):
                        mm = nc.tensor.matmul(pair[3][j * 32:(j + 1) * 32, 0, :], step_b[part][:, :],
                                              past[slot][:, 4 * j:4 * j + 4, :].rearrange("p q c -> p (q c)"),
                                              start=part == 0, stop=part == 2, tile_position=(0, 32 * j))
                mm.then_inc(bias_summed, 1)

            def ffn_pe(s, n_in, n_next, bias=False):
                b = q.block
                for o in range(2):
                    pe.wait_ge(lo_made, b + o + 1)
                    if o == 1:
                        pe.wait_ge(n_in.ln_made, 1)
                    narrow_block((b + o) % 2, pair[o], h_hi, h_lo, 0, KD, True, True,
                                 (n_in.ready, 1) if o == 0 else None)
                    if bias and o == 0:
                        pe.wait_ge(pos_made, 1)
                        nc.tensor.matmul(pair[2][:, 0, :], sign_row[:, :], pos_r[:, :], start=True, stop=True)\
                            .then_inc(pos_spread, 1)
                if bias:
                    for o in range(2):
                        bias_step(o, o)
                with pe.Fori(1, F // COLS) as i:
                    pe.wait_ge(lo_made, b + 1 + 2 * i)
                    pe.wait_ge(s.gate_made, i)
                    narrow_block(b % 2, pair[0], h_hi, h_lo, 0, KD, True, True)
                    if bias:
                        bias_step(2 * i, 0)
                    pe.wait_ge(lo_made, b + 2 + 2 * i)
                    pe.wait_ge(s.act_made, i)
                    narrow_block((b + 1) % 2, pair[1], h_hi, h_lo, 0, KD, True, True)
                    if bias:
                        bias_step(2 * i + 1, 1)
                b = q.block = b + 2 * (F // COLS)
                for g in range(4):
                    for c, k0 in enumerate((0, 8, 16)):
                        o = 3 * g + c
                        kts = min(8, KF - k0)
                        pe.wait_ge(lo_made, b + o + 1)
                        pe.wait_ge(s.act_ready, (k0 + kts) // 2)
                        if c == 0 and g >= 2:
                            pe.wait_ge(s.x_added, g - 1)
                        narrow_block((b + o) % 2, pair[DOWN_PAIR[g]], act_hi, act_lo, k0, kts, c == 0, c == 2)
                        if c == 1 and g:
                            if g == 1:
                                pe.wait_ge(s.act_made, F // COLS)
                            sum_pair(n_next, g - 1, sq_pair[(g - 1) % 2])
                        if bias and 22 + o < BSTEPS:
                            bias_step(22 + o, o % 2)
                sum_pair(n_next, 3, sq_pair[1])
                q.block = b + 12

            def claim(bank):
                if q.reader[bank]:
                    pe.wait_ge(*q.reader[bank])

            def claim_pair(k, sem_, value):
                claim(2 * k)
                claim(2 * k + 1)
                q.reader[2 * k] = q.reader[2 * k + 1] = (sem_, value)

            def next_narrow(k, xs_hi, xs_lo, reader, cols=None, ready=None):
                claim_pair(k, *reader)
                pe.wait_ge(lo_made, q.block + 1)
                out = pair[k] if cols is None else pair[k][:, :, 0:cols]
                narrow_block(q.block % 2, out, xs_hi, xs_lo, 0, KD, True, True, ready)
                q.block += 1

            def wide_slot():
                pe.wait_ge(lo_made, q.block + 1)
                b = q.block % 2
                q.block += 1
                return (w_hi[b][:, :].rearrange("p (k c) -> p k c", c=WIDE),
                        w_lo[b][:, :].rearrange("p (k c) -> p k c", c=WIDE))

            def wide_features(k, xs_hi, xs_lo, readers, ready=None):
                wh, wl = wide_slot()
                for m in range(4):
                    if m % 2 == 0:
                        claim_pair(k + m // 2, *readers[m // 2])
                    for kt in range(4):
                        if ready and m == 0:
                            pe.wait_ge(ready[0], ready[1] + kt + 1)
                        mm = product(pair[k + m // 2][:, m % 2, :], wh[:, kt, m * P:(m + 1) * P],
                                     wl[:, kt, m * P:(m + 1) * P], xs_hi[:, kt, :], xs_lo[:, kt, :],
                                     kt == 0, kt == 3)
                mm.then_inc(block_done, 1)

            def wide_tokens(k, xs_hi, xs_lo, x0, tiles, first, last, readers=None):
                wh, wl = wide_slot()
                for a in range(tiles):
                    if readers and a % 2 == 0:
                        claim_pair(k + a // 2, *readers[a // 2])
                    out = pair[k + a // 2][:, a % 2, :]
                    for kt in range(4):
                        xh = xs_hi[:, x0 + kt, a * P:(a + 1) * P]
                        nc.tensor.matmul(out, xh, wh[:, kt, :], start=first and kt == 0, stop=False)
                        nc.tensor.matmul(out, xh, wl[:, kt, :], start=False, stop=False)
                        mm = nc.tensor.matmul(out, xs_lo[:, x0 + kt, a * P:(a + 1) * P], wh[:, kt, :],
                                              start=False, stop=last and kt == 3)
                mm.then_inc(block_done, 1)

            def both(sem_, before):
                return (sem_, before + 1), (sem_, before + 2)

            def gates_pe():
                claim_pair(2, g_pre, 1)
                pe.wait_ge(lo_made, q.block + 1)
                b = q.block % 2
                wh = w_hi[b][:, :].rearrange("p (k c) -> p k c", c=COLS)
                wl = w_lo[b][:, :].rearrange("p (k c) -> p k c", c=COLS)
                for j in range(2):
                    c0 = j * M_HEADS
                    for k in range(KD):
                        if j == 0:
                            pe.wait_ge(n_mix.ready, k + 1)
                        mm = product(pair[2][:, j, :], wh[:, k, c0:c0 + P], wl[:, k, c0:c0 + P],
                                     h_hi[:, k, :], h_lo[:, k, :], k == 0, k == KD - 1)
                mm.then_inc(block_done, 1)
                q.block += 1

            def gates_turn_pe():
                claim_pair(3, g_ready, 1)
                pe.wait_ge(g_diag, 1)
                nc.tensor.matmul(pair[3][:, 1, 0:8], ones[0:M_HEADS, :],
                                 dec_diag[:, :, :].rearrange("p c h -> p (c h)"), start=True, stop=True)
                pe.wait_ge(g_exp, 2)
                for a in range(4):
                    for c in range(CHUNKS):
                        col = (a * CHUNKS + c) * M_HEADS
                        mm = nc.tensor.transpose(pair[3][:, 0, col:col + M_HEADS],
                                                 g_rows[:, a, c * P:(c + 1) * P], ident[0:M_HEADS, 0:M_HEADS])
                mm.then_inc(g_turned, 1)

            def head_pe(h):
                if h == 0:
                    for m in range(2):
                        next_narrow(m, h_hi, h_lo, (xmh_made, m + 1))
                def chunk(c):
                    return slice(c * P, (c + 1) * P)

                pe.wait_ge(xml_made, 2 * h + 2)
                wide_tokens(0, xm_hi, xm_lo, 0, NT, True, True, both(v_made, 2 * h))
                if h == 0:
                    gates_turn_pe()
                next_narrow(O_PAIR[0], h_hi, h_lo, (o_made, 2 * h + 1))
                pe.wait_ge(xcl_made, h + 1)
                wide_features(0, xc_hi, xc_lo, both(k_made, 2 * h))
                wide_features(2, xc_hi, xc_lo, both(q_made, 2 * h))
                claim(2)
                if h == 0:
                    pe.wait_ge(consts_made, 8)
                nc.tensor.matmul(pair[1][:, 0, :], sel[:, h, :], g_neg[:, :], start=True, stop=True)\
                    .then_inc(negm_spread, 1)
                q.reader[2] = (w_arg, h + 1)
                next_narrow(O_PAIR[1], h_hi, h_lo, (o_made, 2 * h + 2))
                claim(3)
                for bank in (4, 5, 6, 7):
                    claim(bank)
                for c in range(CHUNKS):
                    for k in range(MK):
                        mm = nc.tensor.matmul(pair[2][:, 0, chunk(c)], k_f[:, k, chunk(c)], q_f[:, k, chunk(c)],
                                              start=k == 0, stop=k == MK - 1)
                mm.then_inc(sc_ready, 1)
                for c in range(CHUNKS - 1):
                    for k in range(MK):
                        mm = nc.tensor.transpose(pair[KT_BANK[c] // 2][:, KT_BANK[c] % 2, k * P:(k + 1) * P],
                                                 k_f[:, k, chunk(c)], ident[:, :])
                    mm.then_inc(kt_ready, 1)
                for bank in range(4):
                    claim(bank)
                small = pair[3][:, 0, :]
                for c in range(CHUNKS):
                    g = CHUNKS * h + c
                    if c < CHUNKS - 1:
                        pe.wait_ge(kws_made, 3 * h + c + 1)
                        for half in range(2):
                            if c > 0:
                                pe.wait_ge(c_made, 2 * (3 * h + c - 1) + half + 1)
                            for j in range(2):
                                ks = slice((2 * half + j) * P, (2 * half + j + 1) * P)
                                mm = nc.tensor.matmul(pair[half][:, j, :], k_ws[:, c, ks], v_f[:, c, :], start=True,
                                                      stop=True)
                            if half == 0:
                                mm.then_inc(upd_ready, 1)
                        if c == 0:
                            pe.wait_ge(kws_made, 3 * h + 3)
                        else:
                            pe.wait_ge(r_made, g)
                        for k in range(MK):
                            mm = nc.tensor.matmul(small[:, k:k + 1], k_ws[:, c, k * P:(k + 1) * P], ones[:, 0:1],
                                                  start=True, stop=True)
                        mm.then_inc(upd_ready, 1)
                    if c == 0:
                        pe.wait_ge(sw_made, h + 1)
                    elif c > 1:
                        pe.wait_ge(h_part, g - 1)
                    nc.tensor.matmul(pair[2 + c % 2][:, 1, :], s_w[:, c, :], v_f[:, c, :], start=True, stop=True)
                    if c > 0:
                        pe.wait_ge(c_made, 2 * (3 * h + c))
                        if c == 2:
                            pe.wait_ge(h_made, 3 * h + 1)
                        for k in range(MK):
                            nc.tensor.matmul(inter(c), q_f[:, k, chunk(c)], c_st[(c - 1) % 2][:, k, :], start=k == 0,
                                             stop=k == MK - 1)
                    if c < CHUNKS - 1:
                        pe.wait_ge(n_made, 3 * h + c + 1)
                    else:
                        pe.wait_ge(r_made, g)
                    if c > 0:
                        for k in range(MK):
                            nc.tensor.matmul(small[:, 5:6], q_f[:, k, chunk(c)], n_st[(c - 1) % 2][:, k:k + 1],
                                             start=k == 0, stop=k == MK - 1)
                    nc.tensor.matmul(small[:, 4:5], s_w[:, c, :], ones[:, 0:1], start=True, stop=True)\
                        .then_inc(num_ready, 1)
                q.reader[0] = q.reader[1] = q.reader[3] = (c_made, 6 * (h + 1))
                q.reader[2] = (h_made, 3 * (h + 1))
                if h < M_HEADS - 1:
                    next_narrow(0, h_hi, h_lo, (xmh_made, 2 * h + 3))
                else:
                    next_narrow(0, h_hi, h_lo, (g_sig_made, 1))
                pe.wait_ge(hn_made, CHUNKS * (h + 1))
                for e in range(MK):
                    for c in range(CHUNKS):
                        mm = nc.tensor.transpose(pair[2 + e // 2][:, e % 2, c * P:(c + 1) * P],
                                                 h_m[:, c, e * P:(e + 1) * P], ident[:, :])
                    mm.then_inc(h_turned, 1)
                if h < M_HEADS - 1:
                    next_narrow(1, h_hi, h_lo, (xmh_made, 2 * h + 4))
                else:
                    next_narrow(1, h_hi, h_lo, (g_sig_made, 2))
                q.reader[4] = q.reader[5] = q.reader[6] = q.reader[7] = (yml_made, MK * (h + 1))
                for m in range(2):
                    wide_features(2 * m, ym_hi, ym_lo, both(bm_added, 4 * h + 2 * m), (yml_made, MK * h) if m == 0 else None)

            def filler(reader):
                b = q.block % 2
                out = pair[reader[0]]
                wh = w_hi[b][:, :].rearrange("p (k c) -> p k c", c=COLS)
                wl = w_lo[b][:, :].rearrange("p (k c) -> p k c", c=COLS)
                for piece in range(4):
                    if piece == 0:
                        claim_pair(*reader)
                        pe.wait_ge(lo_made, q.block + 1)
                    for k in range(2 * piece, 2 * piece + 2):
                        for j in range(2):
                            mm = product(out[:, j, :], wh[:, k, j * P:(j + 1) * P], wl[:, k, j * P:(j + 1) * P],
                                         h_hi[:, k, :], h_lo[:, k, :], k == 0, k == KD - 1)
                    if piece == 3:
                        mm.then_inc(block_done, 1)
                        q.block += 1
                    yield

            def merge_pe(base, xs_hi, xs_lo, ready):
                def gate_block(m):
                    next_narrow(2 * (m % 2), h_hi, h_lo, (g_sig_made, base + m + 1))

                for m in range(4):
                    if m < 3:
                        gate_block(m + 1)
                    if m == 0:
                        pe.wait_ge(*ready)
                    next_narrow(2 * (m % 2) + 1, xs_hi, xs_lo, (mg_made, base + m + 1))

            def attention_pe():
                pe.wait_ge(lam_loaded, 64)
                claim(7)
                for j in range(2):
                    lq = smalls[0:A_QK, 32 + 2 * j:33 + 2 * j]
                    mm = nc.tensor.matmul(pair[3][:, 1, j:j + 1], lq.to_broadcast([A_QK, P]),
                                          smalls[0:A_QK, 33 + 2 * j:34 + 2 * j], start=True, stop=True)
                mm.then_inc(lam_summed, 1)
                q.reader[7] = (g_exp, 3)
                for nh in range(2):
                    wide_tokens(2 * nh, h_hi, h_lo, 0, NT, True, False, both(va_made, 2 * nh))
                    wide_tokens(2 * nh, h_hi, h_lo, 4, NT, False, True)
                def scores(u):
                    hh, qt, hb = (u // 4) % 2, u % 4, (u // 8) % 2
                    b = u % 2
                    if u < 2:
                        claim(4 + 2 * b)
                        claim(5 + 2 * b)
                    else:
                        pe.wait_ge(a_shifted, 2 * (u - 2) + 2)
                    if u % 8 == 0:
                        pe.wait_ge(qa_made, u // 8 + 1)
                        pe.wait_ge(ka_made, u // 8 + 1)
                    for j in range(2):
                        r = slice(j * A_QK, (j + 1) * A_QK)
                        mm = nc.tensor.matmul(pair[2 + b][:, j, :], q_a[hb][r, hh, qt * P:(qt + 1) * P],
                                              k_a[hb][r, hh, :], start=True, stop=True)
                    mm.then_inc(a_scored, 1)

                next_narrow(0, h_hi, h_lo, (qa_made, 1))
                next_narrow(1, h_hi, h_lo, (ka_made, 1))
                def head_out(e):
                    pe.wait_ge(a_tr_made, 4 * e + 4)
                    if e:
                        pe.wait_ge(a_r, e)
                    for k in range(NT):
                        mm = nc.tensor.matmul(pair[1][:, 1, :], va[:, k, e * P:(e + 1) * P], a_tr[:, k, :],
                                              start=k == 0, stop=k == NT - 1)
                    mm.then_inc(a_out, 1)

                def head_sum(e):
                    pe.wait_ge(a_sq, e + 1)
                    nc.tensor.matmul(pair[1][:, 1, :], ones[:, :], o_sq[:, :], start=True, stop=True)\
                        .then_inc(a_sum, 1)

                claim(2)
                claim(3)
                scores(0)
                scores(1)
                for u in range(4 * A_HEADS):
                    hp, e = u // 8, u // 4 - 1
                    if u % 8 == 0:
                        readers = [(0, qa_made, hp + 2), (0, ka_made, hp + 2)] if hp < 3 else [(0, g_sig_made, 5)]
                        pieces = (None for r in readers for _ in filler(r))
                    if u + 2 < 4 * A_HEADS:
                        scores(u + 2)
                    for _ in range(A_FILL[u % 8]):
                        next(pieces, None)
                    if u % 4 == 0 and e >= 0:
                        head_out(e)
                    if u % 4 == 1 and e >= 0:
                        head_sum(e)
                    pe.wait_ge(a_mixed, u + 1)
                    if u:
                        pe.wait_ge(a_tr_made, u)
                    for k in range(NT):
                        mm = nc.tensor.transpose(pair[1][:, 0, k * P:(k + 1) * P],
                                                 probs[u % 2][:, 0, k * P:(k + 1) * P], ident[:, :])
                    mm.then_inc(a_turned, 1)
                head_out(A_HEADS - 1)
                pe.wait_ge(mem_r, MT)
                pe.wait_ge(a_shifted, 64)
                for k in range(KD):
                    for a in range(MT):
                        col = (k % 2) * MEM + a * P
                        mm = nc.tensor.transpose(pair[2 + k // 4][:, k // 2 % 2, col:col + P],
                                                 mem_tok[:, a, k * P:(k + 1) * P], ident[:, :])
                    if k % 4 == 3:
                        mm.then_inc(mem_turned, 1)
                head_sum(A_HEADS - 1)
                q.reader[2] = (a_tr_made, 4 * A_HEADS)
                q.reader[3] = (a_r, A_HEADS)
                q.reader[4] = q.reader[5] = (memn_made, 4)
                q.reader[6] = q.reader[7] = (memn_made, KD)

            def cross_pe():
                pe.wait_ge(meml_made, KD)
                for m in range(4):
                    next_narrow(m % 2, memn_hi, memn_lo, (kx_made, m + 1), cols=MEM)
                for nh in range(2):
                    claim_pair(2 + nh, vx_made, nh + 1)
                    wide_tokens(2 + nh, memn_hi, memn_lo, 0, MT, True, False)
                    wide_tokens(2 + nh, memn_hi, memn_lo, 4, MT, False, True)
                next_narrow(0, h_hi, h_lo, (qx_made, 1))

                def scores(u):
                    h, qt = u // 4, u % 4
                    if u < 2:
                        claim(4 + u)
                        claim(6 + u)
                    else:
                        pe.wait_ge(x_exp, u - 1)
                    if qt == 0:
                        pe.wait_ge(qx_made, h + 1)
                    for k in range(2):
                        mm = nc.tensor.matmul(pair[2][:, u % 2, 0:MEM], q_x[:, 2 * h + k, qt * P:(qt + 1) * P],
                                              k_x[:, 2 * h + k, :], start=k == 0, stop=k == 1)
                    mm.then_inc(x_scored, 1)

                def head_out(h):
                    pe.wait_ge(x_tr_made, 4 * h + 4)
                    claim_pair(X_OUT_PAIR[h], x_yl, h + 1)
                    for j in range(2):
                        for a in range(MT):
                            mm = nc.tensor.matmul(pair[X_OUT_PAIR[h]][:, j, :],
                                                  v_x[:, a, (2 * h + j) * P:(2 * h + j + 1) * P],
                                                  p_tr[:, a, :], start=a == 0, stop=a == MT - 1)
                    mm.then_inc(x_out, 1)

                scores(0)
                scores(1)
                for u in range(4 * X_HEADS):
                    if u % 4 == 0:
                        h = u // 4
                        pieces = filler(((h + 1) % 2, qx_made, h + 2) if h < X_HEADS - 1 else (0, g_sig_made, 9))
                    for _ in range(X_FILL[u % 4]):
                        next(pieces)
                    if u + 2 < 4 * X_HEADS:
                        scores(u + 2)
                    if u % 4 == 0 and u:
                        head_out(u // 4 - 1)
                    pe.wait_ge(x_norm, u + 1)
                    if u >= 2:
                        pe.wait_ge(x_tr_made, u - 1)
                    for a in range(MT):
                        mm = nc.tensor.transpose(pair[3][:, u % 2, a * P:(a + 1) * P],
                                                 p_x[u % 2][:, a * P:(a + 1) * P], ident[:, :])
                    mm.then_inc(x_turned, 1)
                head_out(X_HEADS - 1)
                q.reader[4] = q.reader[5] = (x_exp, 4 * X_HEADS)
                q.reader[6] = q.reader[7] = (x_tr_made, 4 * X_HEADS)

            def out_pe():
                for m in range(4):
                    next_narrow(2 + m % 2, mg_hi, mg_lo, (x_mixed, m + 1), ready=(mgl_made, 2) if m == 0 else None)
                    if m == 0:
                        claim(2)
                    if m:
                        sum_pair(n_ffn[1], m - 1, sq_pair[(m - 1) % 2])
                sum_pair(n_ffn[1], 3, sq_pair[1])

            for g in range(4):
                sum_pair(n_ffn[0], g, sq[:, 2 * g:2 * g + 2, :])
            pe.wait_ge(prm_loaded, 160)
            nc.tensor.transpose(pair[3][:, 0, 0:104], prm1[:, :], ident[0:104, 0:104])
            nc.tensor.transpose(pair[3][:, 0, 128:192], prm2[:, :], ident[0:64, 0:64]).then_inc(par_turned, 1)
            ffn_pe(ffn[0], n_ffn[0], n_mix, bias=True)
            gates_pe()
            for h in range(M_HEADS):
                head_pe(h)
            for m in range(2, 4):
                next_narrow(m % 2, h_hi, h_lo, (g_sig_made, m + 1))
            attention_pe()
            merge_pe(4, ya_hi, ya_lo, (a_yl, A_HEADS))
            cross_pe()
            merge_pe(8, yx_hi, yx_lo, (x_yl, X_HEADS))
            out_pe()
            ffn_pe(ffn[1], n_ffn[1], n_fin)
            for half in range(2):
                pe.wait_ge(n_fin.raw_made, 4 * half + 4)
                for a in range(NT):
                    for k in range(4):
                        last = nc.tensor.transpose(pair[a][:, half, k * P:(k + 1) * P],
                                                   sq[:, 4 * half + k, a * P:(a + 1) * P], ident[:, :])
                    last.then_inc(out_turned, 1)


_INS = ["x", "mem", "positions", "rel_bias", "ffn1_norm", "ffn1_w_gu", "ffn1_w_down", "mix_norm", "mem_norm",
        "w_in", "b_if", "b_gate", "m_conv_w", "m_conv_b", "m_wq", "m_wk", "m_wv", "m_head_norm",
        "a_lam_q1", "a_lam_k1", "a_lam_q2", "a_lam_k2", "a_head_norm", "w_mem_kv", "w_branch_m",
        "w_branch_a", "w_branch_x", "w_out", "ffn2_norm", "ffn2_w_gu", "ffn2_w_down", "final_norm"]


def _thresholds():
    n = np.arange(1, 256)
    large = 16 + (np.log(np.maximum(n, 1) / np.float32(16)) / np.log(128 / 16) * 16).astype(np.int32)
    bucket = np.where(n < 16, n, np.minimum(large, BUCKETS - 1))
    first = [0.5] + [float(n[np.argmax(bucket >= b)]) for b in range(1, BUCKETS)]
    return np.tile(np.array(first, np.float32), 4).reshape(P, 1)


def kernel(**inputs):
    import concourse.bacc as _bacc
    from concourse import mybir as _mybir
    from concourse.bass_utils import run_bass_kernel_spmd as _run

    nc = _bacc.Bacc("TRN2", target_bir_lowering=False, num_devices=1)
    arrays, t = {}, {}
    inputs["thresholds"] = _thresholds()
    for name in _INS + ["thresholds"]:
        a = np.ascontiguousarray(inputs[name])
        if a.ndim > 1 and a.shape[0] == 1:
            a = a.reshape(a.shape[1:])
        arrays[f"in_{name}"] = a
        t[name] = nc.dram_tensor(f"in_{name}", a.shape, _mybir.dt.from_np(a.dtype), kind="ExternalInput").ap()
    out = nc.dram_tensor("out", (S, D), F32, kind="ExternalOutput")
    t["out"] = out.ap()
    build(nc, t)
    r = _run(nc, [arrays], core_ids=[0])
    return r.results[0]["out"].reshape(1, S, D)
```
